# Optimizing a Trainium2 kernel written in Bass

```python
import math
import jax, jax.numpy as jnp
from jax import lax
import numpy as np

D_MODEL = 1024
BATCH = 1
SEQ = 256
DEPTH = 1
DEC_BATCH = 1
DEC_SEQ = 64
PAST_LEN = 256

CHUNK = 64
EPS = 1e-6
GDN_HEADS = 4
GDN_DK = 128
GDN_DV = 128
CONV_W = 4
GDN_QK = GDN_HEADS * GDN_DK
GDN_VW = GDN_HEADS * GDN_DV
CONV_DIM = 2 * GDN_QK + GDN_VW
MLA_HEADS = 4
Q_RANK = 384
KV_RANK = 256
NOPE_DIM = 128
ROPE_DIM = 64
V_DIM = 128
QK_DIM = NOPE_DIM + ROPE_DIM
ROPE_THETA = 10000.0
Q_BLOCK = 128
MIX_WIDTH = GDN_VW + MLA_HEADS * V_DIM
IN_WIDTH = CONV_DIM + GDN_VW + 2 * GDN_HEADS + Q_RANK + KV_RANK + ROPE_DIM
N_MEM = 256
MEM_HEADS = 4
MEM_HEAD_DIM = 128
N_EXPERTS = 32
TOP_K = 4
D_FF = D_MODEL
SWIGLU_ALPHA = 1.702
SWIGLU_LIMIT = 7.0
MOE_BLOCK = 128

kernel_name = 'hybrid_gdn_mla_memxattn_moe_stream_step'

F32 = jnp.float32

def rms_norm(x, gain):
    xf = x.astype(F32)
    y = xf * lax.rsqrt(jnp.mean(xf * xf, axis=-1, keepdims=True) + EPS)
    return (y * gain.astype(F32)).astype(x.dtype)

def l2_norm(x):
    xf = x.astype(F32)
    return xf * lax.rsqrt(jnp.sum(xf * xf, axis=-1, keepdims=True) + EPS)

def rope(x, pos):
    half = ROPE_DIM // 2
    inv = ROPE_THETA ** (-jnp.arange(half, dtype=F32) / half)
    ang = pos.astype(F32)[:, None] * inv[None, :]
    cos = jnp.cos(ang)[:, None, :]
    sin = jnp.sin(ang)[:, None, :]
    xf = x.astype(F32)
    x1, x2 = xf[..., :half], xf[..., half:]
    return jnp.concatenate([x1 * cos - x2 * sin, x2 * cos + x1 * sin], axis=-1).astype(x.dtype)

def causal_conv(u, past, w):
    S = u.shape[1]
    upad = jnp.concatenate([past.astype(u.dtype), u], axis=1)
    out = upad[:, 0:S] * w[0]
    for j in range(1, CONV_W):
        out = out + upad[:, j:j + S] * w[j]
    return jax.nn.silu(out), upad[:, upad.shape[1] - (CONV_W - 1):]

def gated_delta_rule(q, k, v, g, beta, s0, chunk):
    B, S, H, DK = q.shape
    DV = v.shape[-1]
    N = S // chunk
    q = l2_norm(q) * (DK ** -0.5)
    k = l2_norm(k)
    v = v.astype(F32)

    def blocks(t):
        return t.reshape(B, N, chunk, H, t.shape[-1]).transpose(1, 0, 3, 2, 4)

    qc, kc, vc = blocks(q), blocks(k), blocks(v)
    gc = g.astype(F32).reshape(B, N, chunk, H).transpose(1, 0, 3, 2)
    bc = beta.astype(F32).reshape(B, N, chunk, H).transpose(1, 0, 3, 2)
    gcum = jnp.cumsum(gc, axis=-1)
    tril = jnp.tril(jnp.ones((chunk, chunk), bool))
    strict = jnp.tril(jnp.ones((chunk, chunk), bool), -1)
    diff = gcum[..., :, None] - gcum[..., None, :]
    decay = jnp.where(tril, jnp.exp(jnp.where(tril, diff, 0.0)), 0.0)
    kb = kc * bc[..., None]
    vb = vc * bc[..., None]
    m = jnp.where(strict, jnp.einsum('nbhid,nbhjd->nbhij', kb, kc) * decay, 0.0)
    eye = jnp.eye(chunk, dtype=F32)
    tinv = lax.linalg.triangular_solve(eye + m, jnp.broadcast_to(eye, m.shape), left_side=True, lower=True)
    u = tinv @ vb
    w = tinv @ (kb * jnp.exp(gcum)[..., None])
    qk = jnp.where(tril, jnp.einsum('nbhid,nbhjd->nbhij', qc, kc) * decay, 0.0)

    def step(state, xs):
        q_i, k_i, u_i, w_i, qk_i, g_i = xs
        v_new = u_i - w_i @ state
        out = (q_i * jnp.exp(g_i)[..., None]) @ state + qk_i @ v_new
        g_last = g_i[..., -1]
        k_dec = k_i * jnp.exp(g_last[..., None] - g_i)[..., None]
        state = state * jnp.exp(g_last)[..., None, None] + jnp.einsum('bhld,bhle->bhde', k_dec, v_new)
        return state, out

    s_final, outs = lax.scan(step, s0.astype(F32), (qc, kc, u, w, qk, gcum))
    o = outs.transpose(1, 0, 3, 2, 4).reshape(B, S, H, DV)
    return o, s_final

def block_causal_attention(q, k, v, q_pos, k_pos):
    B, Sq, H, _ = q.shape
    qb = min(Q_BLOCK, Sq)
    nb = Sq // qb
    qs = q.reshape(B, nb, qb, H, q.shape[-1]).transpose(1, 0, 2, 3, 4)
    ps = q_pos.reshape(nb, qb)
    k_chunk = k_pos // CHUNK

    def one(args):
        qi, pi = args
        s = jnp.einsum('bqhd,bkhd->bhqk', qi, k).astype(F32)
        mask = k_chunk[None, :] <= (pi // CHUNK)[:, None]
        s = jnp.where(mask[None, None], s, -jnp.inf)
        pr = jax.nn.softmax(s, axis=-1).astype(v.dtype)
        return jnp.einsum('bhqk,bkhd->bqhd', pr, v)

    out = lax.map(one, (qs, ps))
    return out.transpose(1, 0, 2, 3, 4).reshape(B, Sq, H, v.shape[-1])

def memory_kv(mem, mem_norm, w_mk, w_mv, mk_norm):
    B = mem.shape[0]
    m = rms_norm(mem, mem_norm)
    k = rms_norm((m @ w_mk).reshape(B, N_MEM, MEM_HEADS, MEM_HEAD_DIM), mk_norm)
    v = (m @ w_mv).reshape(B, N_MEM, MEM_HEADS, MEM_HEAD_DIM)
    return k, v

def moe_ffn(h, w_router, b_router, w_gu, b_gu, w_down, b_down):
    T, D = h.shape
    logits = (h @ w_router + b_router).astype(F32)
    top_val, top_idx = lax.top_k(logits, TOP_K)
    gate = jax.nn.softmax(top_val, axis=-1)
    n_assign = T * TOP_K
    flat_e = top_idx.reshape(-1).astype(jnp.int32)
    flat_tok = jnp.arange(n_assign, dtype=jnp.int32) // TOP_K
    order = jnp.argsort(flat_e)
    e_sorted = flat_e[order]
    tok_sorted = flat_tok[order]
    gate_sorted = gate.reshape(-1)[order]
    counts = jnp.zeros((N_EXPERTS,), jnp.int32).at[flat_e].add(1)
    padded = (counts + MOE_BLOCK - 1) // MOE_BLOCK * MOE_BLOCK
    pad_end = jnp.cumsum(padded)
    pad_start = pad_end - padded
    start = jnp.cumsum(counts) - counts
    dest = pad_start[e_sorted] + jnp.arange(n_assign, dtype=jnp.int32) - start[e_sorted]
    n_blocks = -(-n_assign // MOE_BLOCK) + N_EXPERTS
    row_tok = jnp.full((n_blocks * MOE_BLOCK,), T, jnp.int32).at[dest].set(tok_sorted)
    h_pad = jnp.concatenate([h, jnp.zeros((1, D), h.dtype)], axis=0)
    rows = h_pad[row_tok].reshape(n_blocks, MOE_BLOCK, D)
    block_e = jnp.minimum(jnp.searchsorted(pad_end, jnp.arange(n_blocks, dtype=jnp.int32) * MOE_BLOCK, side='right'), N_EXPERTS - 1)

    def expert_block(args):
        xb, e = args
        gu = xb @ w_gu[e] + b_gu[e]
        gt = jnp.minimum(gu[:, :D_FF], SWIGLU_LIMIT)
        up = jnp.clip(gu[:, D_FF:], -SWIGLU_LIMIT, SWIGLU_LIMIT)
        act = gt * jax.nn.sigmoid(SWIGLU_ALPHA * gt) * (up + 1.0)
        return act @ w_down[e] + b_down[e]

    y_rows = lax.map(expert_block, (rows, block_e)).reshape(n_blocks * MOE_BLOCK, D)
    y = y_rows[dest] * gate_sorted[:, None].astype(h.dtype)
    return jax.ops.segment_sum(y, tok_sorted, num_segments=T)

def trunk_layer(x, lat_past, kpe_past, s0, conv_past, mem_k, mem_v, p):
    B, S, D = x.shape
    P = lat_past.shape[1]
    q_pos = P + jnp.arange(S, dtype=jnp.int32)
    k_pos = jnp.arange(P + S, dtype=jnp.int32)

    h = rms_norm(x, p['norm_mix'])
    proj = h @ p['w_in']
    idx = [int(i) for i in np.cumsum([CONV_DIM, GDN_VW, GDN_HEADS, GDN_HEADS, Q_RANK, KV_RANK])]
    u, z, a, b, cq, ckv, kpe = jnp.split(proj, idx, axis=-1)

    uc, conv_new = causal_conv(u, conv_past, p['conv_w'])
    qg = uc[..., :GDN_QK].reshape(B, S, GDN_HEADS, GDN_DK)
    kg = uc[..., GDN_QK:2 * GDN_QK].reshape(B, S, GDN_HEADS, GDN_DK)
    vg = uc[..., 2 * GDN_QK:].reshape(B, S, GDN_HEADS, GDN_DV)
    beta = jax.nn.sigmoid(b.astype(F32))
    g = -jnp.exp(p['a_log'].astype(F32)) * jax.nn.softplus(a.astype(F32) + p['dt_bias'].astype(F32))
    o_gdn, s_new = gated_delta_rule(qg, kg, vg, g, beta, s0, min(CHUNK, S))
    o_gdn = rms_norm(o_gdn.astype(x.dtype), p['gdn_norm']) * jax.nn.silu(z.reshape(B, S, GDN_HEADS, GDN_DV))

    c_q = rms_norm(cq, p['q_a_norm'])
    q = rms_norm((c_q @ p['w_qb']).reshape(B, S, MLA_HEADS, QK_DIM), p['q_norm'])
    q = jnp.concatenate([q[..., :NOPE_DIM], rope(q[..., NOPE_DIM:], q_pos)], axis=-1)
    lat_new = rms_norm(ckv, p['kv_a_norm'])
    kpe_new = rope(rms_norm(kpe, p['k_rope_norm'])[:, :, None, :], q_pos)[:, :, 0, :]
    lat_all = jnp.concatenate([lat_past.astype(x.dtype), lat_new], axis=1)
    kpe_all = jnp.concatenate([kpe_past.astype(x.dtype), kpe_new], axis=1)
    Sk = P + S
    kv = (lat_all @ p['w_kvb']).reshape(Sk and B, Sk, MLA_HEADS, NOPE_DIM + V_DIM)
    k_nope = rms_norm(kv[..., :NOPE_DIM], p['k_nope_norm'])
    v_mla = kv[..., NOPE_DIM:]
    k_mla = jnp.concatenate([k_nope, jnp.broadcast_to(kpe_all[:, :, None, :], (B, Sk, MLA_HEADS, ROPE_DIM))], axis=-1)
    o_mla = block_causal_attention(q * (QK_DIM ** -0.5), k_mla, v_mla, q_pos, k_pos)

    mix = jnp.concatenate([o_gdn.reshape(B, S, GDN_VW), o_mla.reshape(B, S, MLA_HEADS * V_DIM)], axis=-1)
    x = x + mix @ p['w_out']

    h = rms_norm(x, p['norm_mem'])
    qm = rms_norm((h @ p['w_mq']).reshape(B, S, MEM_HEADS, MEM_HEAD_DIM), p['mq_norm']) * (MEM_HEAD_DIM ** -0.5)
    sm = jnp.einsum('bqhd,bkhd->bhqk', qm, mem_k.astype(x.dtype)).astype(F32)
    pm = jax.nn.softmax(sm, axis=-1).astype(x.dtype)
    om = jnp.einsum('bhqk,bkhd->bqhd', pm, mem_v.astype(x.dtype))
    x = x + om.reshape(B, S, MEM_HEADS * MEM_HEAD_DIM) @ p['w_mo']

    h = rms_norm(x, p['norm_ffn'])
    y = moe_ffn(h.reshape(B * S, D), p['w_router'], p['b_router'], p['w_gu'], p['b_gu'], p['w_down'], p['b_down'])
    x = x + y.reshape(B, S, D)
    return x, lat_new, kpe_new, s_new.astype(s0.dtype), conv_new

def setup_inputs(seed: int = 0) -> dict:
    key = jax.random.key(seed)
    ks = iter(jax.random.split(key, 48))

    def nrm(shape, scale):
        return jax.random.normal(next(ks), shape, F32) * scale

    def gain(n):
        return 1.0 + nrm((DEPTH, n), 0.02)

    L = DEPTH
    dt = jnp.exp(jax.random.uniform(next(ks), (L, GDN_HEADS), F32, math.log(1e-3), math.log(1e-1)))
    dt_bias = dt + jnp.log(-jnp.expm1(-dt))
    a_log = jnp.log(jax.random.uniform(next(ks), (L, GDN_HEADS), F32, 1.0, 16.0))
    return {
        'x_prompt': nrm((BATCH, SEQ, D_MODEL), 1.0),
        'x_sample': nrm((DEC_BATCH, DEC_SEQ, D_MODEL), 1.0),
        'cache_kv_latent': nrm((L, DEC_BATCH, PAST_LEN, KV_RANK), 1.0),
        'cache_k_rope': nrm((L, DEC_BATCH, PAST_LEN, ROPE_DIM), 1.0),
        'state_gdn': nrm((L, DEC_BATCH, GDN_HEADS, GDN_DK, GDN_DV), 0.1),
        'state_conv': nrm((L, DEC_BATCH, CONV_W - 1, CONV_DIM), 1.0),
        'cache_mem_k': nrm((L, DEC_BATCH, N_MEM, MEM_HEADS, MEM_HEAD_DIM), 1.0),
        'cache_mem_v': nrm((L, DEC_BATCH, N_MEM, MEM_HEADS, MEM_HEAD_DIM), 1.0),
        'mem_prompt': nrm((BATCH, N_MEM, D_MODEL), 1.0),
        'norm_mix': gain(D_MODEL),
        'w_in': nrm((L, D_MODEL, IN_WIDTH), D_MODEL ** -0.5),
        'conv_w': nrm((L, CONV_W, CONV_DIM), CONV_W ** -0.5),
        'a_log': a_log,
        'dt_bias': dt_bias,
        'gdn_norm': gain(GDN_DV),
        'q_a_norm': gain(Q_RANK),
        'w_qb': nrm((L, Q_RANK, MLA_HEADS * QK_DIM), Q_RANK ** -0.5),
        'kv_a_norm': gain(KV_RANK),
        'w_kvb': nrm((L, KV_RANK, MLA_HEADS * (NOPE_DIM + V_DIM)), KV_RANK ** -0.5),
        'q_norm': gain(QK_DIM),
        'k_nope_norm': gain(NOPE_DIM),
        'k_rope_norm': gain(ROPE_DIM),
        'w_out': nrm((L, MIX_WIDTH, D_MODEL), MIX_WIDTH ** -0.5),
        'norm_mem': gain(D_MODEL),
        'mem_norm': gain(D_MODEL),
        'w_mq': nrm((L, D_MODEL, MEM_HEADS * MEM_HEAD_DIM), D_MODEL ** -0.5),
        'w_mk': nrm((L, D_MODEL, MEM_HEADS * MEM_HEAD_DIM), D_MODEL ** -0.5),
        'w_mv': nrm((L, D_MODEL, MEM_HEADS * MEM_HEAD_DIM), D_MODEL ** -0.5),
        'mq_norm': gain(MEM_HEAD_DIM),
        'mk_norm': gain(MEM_HEAD_DIM),
        'w_mo': nrm((L, MEM_HEADS * MEM_HEAD_DIM, D_MODEL), (MEM_HEADS * MEM_HEAD_DIM) ** -0.5),
        'norm_ffn': gain(D_MODEL),
        'w_router': nrm((L, D_MODEL, N_EXPERTS), D_MODEL ** -0.5),
        'b_router': nrm((L, N_EXPERTS), 0.01),
        'w_gu': nrm((L, N_EXPERTS, D_MODEL, 2 * D_FF), D_MODEL ** -0.5),
        'b_gu': nrm((L, N_EXPERTS, 2 * D_FF), 0.01),
        'w_down': nrm((L, N_EXPERTS, D_FF, D_MODEL), D_FF ** -0.5),
        'b_down': nrm((L, N_EXPERTS, D_MODEL), 0.01),
    }

def reference(x_prompt, x_sample, cache_kv_latent, cache_k_rope, state_gdn, state_conv, cache_mem_k, cache_mem_v,
              mem_prompt, norm_mix, w_in, conv_w, a_log, dt_bias, gdn_norm, q_a_norm, w_qb, kv_a_norm, w_kvb,
              q_norm, k_nope_norm, k_rope_norm, w_out, norm_mem, mem_norm, w_mq, w_mk, w_mv, mq_norm, mk_norm,
              w_mo, norm_ffn, w_router, b_router, w_gu, b_gu, w_down, b_down):
    yp, ys = x_prompt, x_sample
    bp = x_prompt.shape[0]
    dt = x_prompt.dtype
    p_lat, p_kpe, p_s, p_conv, p_mk, p_mv = [], [], [], [], [], []
    s_lat, s_kpe, s_s, s_conv = [], [], [], []
    for l in range(DEPTH):
        p = {
            'norm_mix': norm_mix[l], 'w_in': w_in[l], 'conv_w': conv_w[l], 'a_log': a_log[l],
            'dt_bias': dt_bias[l], 'gdn_norm': gdn_norm[l], 'q_a_norm': q_a_norm[l], 'w_qb': w_qb[l],
            'kv_a_norm': kv_a_norm[l], 'w_kvb': w_kvb[l], 'q_norm': q_norm[l], 'k_nope_norm': k_nope_norm[l],
            'k_rope_norm': k_rope_norm[l], 'w_out': w_out[l], 'norm_mem': norm_mem[l], 'w_mq': w_mq[l],
            'mq_norm': mq_norm[l], 'w_mo': w_mo[l], 'norm_ffn': norm_ffn[l], 'w_router': w_router[l],
            'b_router': b_router[l], 'w_gu': w_gu[l], 'b_gu': b_gu[l], 'w_down': w_down[l], 'b_down': b_down[l],
        }
        mk, mv = memory_kv(mem_prompt, mem_norm[l], w_mk[l], w_mv[l], mk_norm[l])
        yp, lat, kpe, s_fin, cv = trunk_layer(
            yp, jnp.zeros((bp, 0, KV_RANK), dt), jnp.zeros((bp, 0, ROPE_DIM), dt),
            jnp.zeros((bp, GDN_HEADS, GDN_DK, GDN_DV), dt), jnp.zeros((bp, CONV_W - 1, CONV_DIM), dt), mk, mv, p)
        p_lat.append(lat); p_kpe.append(kpe); p_s.append(s_fin); p_conv.append(cv); p_mk.append(mk); p_mv.append(mv)
        ys, lat2, kpe2, s_fin2, cv2 = trunk_layer(
            ys, cache_kv_latent[l], cache_k_rope[l], state_gdn[l], state_conv[l], cache_mem_k[l], cache_mem_v[l], p)
        s_lat.append(lat2); s_kpe.append(kpe2); s_s.append(s_fin2); s_conv.append(cv2)
    return (yp, ys, jnp.stack(p_lat), jnp.stack(p_kpe), jnp.stack(p_s), jnp.stack(p_conv), jnp.stack(p_mk),
            jnp.stack(p_mv), jnp.stack(s_lat), jnp.stack(s_kpe), jnp.stack(s_s), jnp.stack(s_conv))


_drawn_inputs = setup_inputs


def setup_inputs(seed=0):
    import zlib

    import numpy as np

    out = dict(_drawn_inputs(seed))
    spreads = {}
    factors = {'q_a_norm': 8.0,
     'kv_a_norm': 3.003,
     'q_norm': 5.65,
     'k_nope_norm': 5.731,
     'k_rope_norm': 3.582,
     'norm_mem': 4.374,
     'mem_norm': 2.823,
     'mq_norm': 4.954,
     'mk_norm': 2.893,
     'b_gu': 8.0,
     'b_down': 22.473,
     'gdn_norm': 2.82,
     'norm_ffn': 3.298,
     'b_router': 5.263}
    for name, (base, spread) in spreads.items():
        noise = np.random.default_rng([zlib.crc32(name.encode()), seed]).standard_normal(out[name].shape)
        drawn = base * np.exp(spread * noise) if base else spread * noise
        out[name] = __import__('jax').numpy.asarray(drawn.astype(out[name].dtype))
    for name, factor in factors.items():
        out[name] = (out[name] * factor).astype(out[name].dtype)
    return out
```

```python
from contextlib import ExitStack

import numpy as np
import concourse.bass as bass
from concourse import mybir

F32 = mybir.dt.float32
BF16 = mybir.dt.bfloat16
I32 = mybir.dt.int32
ALU = mybir.AluOpType
ACT = mybir.ActivationFunctionType
AX = mybir.AxisListType.X

P = 128
D = 1024
KD = D // P
SEQ, DEC, PAST = 256, 64, 256
T = SEQ + DEC
TB = (T + P - 1) // P
CH = 64
NC = T // CH
CONV_DIM, CW = 1536, 4
NU, NZ = CONV_DIM // P, 4
H, HD = 4, 128
Q_RANK, KV_RANK, ROPE = 384, 256, 64
QK = HD + ROPE
IN_W = 2760
AB0 = (NU + NZ) * P
CL0 = AB0 + 2 * H
CLW = Q_RANK + KV_RANK + ROPE
NKEY = SEQ + PAST + DEC
NMEM = 256
E, TOPK, FF = 32, 4, 1024
SLOTS = 64
EPS = 1e-6
ALPHA, LIMIT = 1.702, 7.0
NEG = -1e30
BIG = 3e38
XTRA = T // SLOTS - 1
LIST = 32
LEVELS = (1, 2, 4, 8, 16, 32)

C_ID, C_ONE, C_US, C_U, C_LV, C_IO, C_COS, C_SIN, C_AM, C_E3, C_TH, C_EV, C_MH = (
    0, 128, 256, 384, 448, 832, 1152, 1248, 1344, 1472, 1504, 1508, 1513)
C_N = 1520


def constants():
    c = np.zeros((P, C_N), np.float32)
    i = np.arange(P)
    c[:, C_ID:C_ID + P] = np.eye(P)
    c[:, C_ONE:C_ONE + P] = 1.0
    c[:, C_US:C_US + P] = i[:, None] < i[None, :]
    j = np.arange(CH)
    c[:CH, C_U:C_U + CH] = j[:, None] <= j[None, :]
    for n, s in enumerate(LEVELS):
        pair = (j[:, None] // (2 * s)) == (j[None, :] // (2 * s))
        c[:CH, C_LV + CH * n:C_LV + CH * (n + 1)] = pair & (j[:, None] % (2 * s) < s) & (j[None, :] % (2 * s) >= s)
    c[:, C_IO:C_IO + T] = np.arange(T)[None, :]
    half = ROPE // 2
    inv = (np.float32(10000.0) ** (-np.arange(half, dtype=np.float32) / half)).astype(np.float32)
    pos = np.arange(TB * P, dtype=np.float32)
    ang = (pos[:, None] * inv[None, :]).astype(np.float32).reshape(TB, P, half).transpose(1, 0, 2)
    c[:, C_COS:C_COS + TB * half] = np.cos(ang).reshape(P, -1)
    c[:, C_SIN:C_SIN + TB * half] = np.sin(ang).reshape(P, -1)
    c[:CH, C_AM + CH:C_AM + P] = NEG
    c[:96, C_E3:C_E3 + E] = (i[:96, None] % E) == np.arange(E)[None, :]
    c[:, C_TH:C_TH + XTRA] = SLOTS * (1 + np.arange(XTRA))[None, :]
    c[:, C_EV] = i
    c[:, C_MH] = -0.5
    c[:, C_EV + 1:C_EV + 1 + XTRA] = (1 + np.arange(XTRA))[None, :]
    return c


def trunk_kernel(nc, x_prompt, x_sample, cache_kv_latent, cache_k_rope, state_gdn, state_conv, cache_mem_k,
                 cache_mem_v, mem_prompt, norm_mix, w_in, conv_w, a_log, dt_bias, gdn_norm, q_a_norm, w_qb,
                 kv_a_norm, w_kvb, q_norm, k_nope_norm, k_rope_norm, w_out, norm_mem, mem_norm, w_mq, w_mk,
                 w_mv, mq_norm, mk_norm, w_mo, norm_ffn, w_router, b_router, w_gu, b_gu, w_down, b_down,
                 consts, yp, ys, p_lat, p_kpe, p_s, p_conv, p_mk, p_mv, s_lat, s_kpe, s_s, s_conv):
    ctx = ExitStack()
    with ctx:
        def sb(name, cols, dt=F32, parts=P):
            return ctx.enter_context(nc.sbuf_tensor(name, [parts, cols], dt))

        sems = {}

        def sem(name):
            if name not in sems:
                sems[name] = ctx.enter_context(nc.semaphore(name))
            return sems[name]

        ONCE = {
            "tensor": ["ab_tr", "gcum_mm", "gbc_mm", "sum_mm", "lg_mm", "rank_mm", "cnt_mm", "gt_tr", "start_mm",
                       "list_mm"],
            "scalar": ["beta_ready", "egc_ready", "ebc_ready", "kpe_ev", "gt_ev"],
            "vector": ["upad_ready", "state0", "gb_ready", "sp_abs", "g_ready", "g2_ready", "gcum_ready",
                       "diff_ready", "dec_ready", "qg_ready", "kneg_ready", "kd_ready", "cq_ready", "lat_ready",
                       "kpe_ready", "b3_ready", "mask_ready", "top_ready", "gate_ready", "tot_ready", "hot_ready",
                       "list_ready", "y_final"],
        }

        def mark(name):
            return sem(next(engine for engine in ONCE if name in ONCE[engine]) + "_events")

        def at(name):
            engine = next(engine for engine in ONCE if name in ONCE[engine])
            return sem(engine + "_events"), ONCE[engine].index(name) + 1

        NORM = {"mem": 0, "x": KD, "x2n": 2 * KD, "x3n": 3 * KD}
        ATT = {"mla": 0, "mem": H * TB}
        RES = {"x2": (0, 0), "x3": (2 * TB, TB)}

        W = sb("weights", 24576)
        V = sb("stream", 8192)
        R = sb("small_weights", 4352)
        X = sb("x", TB * D)
        XS = sb("scaled", TB * D)
        HM = sb("hT", KD * T)
        KV = sb("mem_kv", 4096)
        CO = sb("const", C_N)
        GN = sb("gain_rows", 768)
        GC = sb("gain_cols", 64)
        SM = sb("stats", 480)
        PS = [ctx.enter_context(nc.psum_tensor(f"bank{i}", [P, 512], F32)) for i in range(8)]

        ident = CO[:, C_ID:C_ID + P]
        ones = CO[:, C_ONE:C_ONE + P]
        ustrict = CO[:, C_US:C_US + P]
        u64 = CO[0:CH, C_U:C_U + CH]
        iota = CO[:, C_IO:C_IO + T]
        cos = CO[:, C_COS:C_COS + 96].rearrange("p (b f) -> p b f", b=TB)
        sin = CO[:, C_SIN:C_SIN + 96].rearrange("p (b f) -> p b f", b=TB)
        minus_half = CO[:, C_MH:C_MH + 1]
        amask = CO[:, C_AM:C_AM + P]
        g_kva, g_q, g_kr, g_mk = GN[:, 0:256], GN[:, 256:448], GN[:, 448:512], GN[:, 512:640]
        g_router = GN[:, 640:672]
        g_dt, g_alog = GN[0:CH, 672:676], GN[0:CH, 676:680]
        c_mix, c_mem, c_memn, c_ffn = GC[:, 0:8], GC[:, 8:16], GC[:, 16:24], GC[:, 24:32]
        c_qa, c_kn, c_gdn, c_mq = GC[:, 32:35], GC[:, 35:36], GC[:, 36:37], GC[:, 37:38]

        w_in_sb = W[:, 0:KD * IN_W].rearrange("p (k n) -> p k n", k=KD)
        mk_out = W[:, 22080:23104].rearrange("p (b n) -> p b n", b=2)
        mk_tmp = W[:, 23104:24128].rearrange("p (b n) -> p b n", b=2)
        g_rows = KV[0:38, 3584:3712]
        wmk_sb = V[:, 0:4096].rearrange("p (k n) -> p k n", k=KD)
        wmv_sb = V[:, 4096:8192].rearrange("p (k n) -> p k n", k=KD)
        UW = SEQ + DEC + 2 * (CW - 1)
        upad = V[:, 0:NU * UW].rearrange("p (f t) -> p f t", f=NU)
        ztile = V[:, 3912:3912 + NZ * T].rearrange("p (h t) -> p h t", h=NZ)
        cl = V[:, 5192:5192 + TB * CLW].rearrange("p (b n) -> p b n", b=TB)
        abT = V[0:2 * H, 7304:7304 + T]
        conv_tmp = V[:, 7624:7624 + 323]
        wout_sb = V[:, 0:8192].rearrange("p (k n) -> p k n", k=KD)
        wqb_sb = R[:, 0:2304].rearrange("p (k n) -> p k n", k=3)
        wkvb_sb = R[:, 2304:4352].rearrange("p (k n) -> p k n", k=2)
        x3 = X[:, :].rearrange("p (b d) -> p b d", b=TB)
        xs3 = XS[:, :].rearrange("p (b d) -> p b d", b=TB)
        mem3 = XS[:, 0:2048].rearrange("p (b d) -> p b d", b=2)
        kcache = XS[:, 2048:3072].rearrange("p (b n) -> p b n", b=2)
        hT = HM[:, :].rearrange("p (k t) -> p k t", k=KD)
        mT = HM[:, 0:KD * NMEM].rearrange("p (k t) -> p k t", k=KD)
        conv7 = KV[0:7, 2048:2048 + CONV_DIM]
        km_p = KV[:, 0:1024].rearrange("p (h t) -> p h t", h=H)
        vm_p = KV[:, 1024:2048].rearrange("p (b n) -> p b n", b=2)
        km_s = KV[:, 2048:3072].rearrange("p (h t) -> p h t", h=H)
        vm_s = KV[:, 3072:4096].rearrange("p (b n) -> p b n", b=2)
        convw = SM[:, 0:84].rearrange("p (f j) -> p f j", f=NU)
        ulast = SM[:, 84:156].rearrange("p (f s j) -> p f s j", f=NU, s=2)
        lvl_masks = CO[0:CH, C_LV:C_LV + CH * len(LEVELS)].rearrange("p (l i) -> p l i", l=len(LEVELS))

        NP_ = NC * H
        sq8 = W[:, 0:2560].rearrange("p (f t) -> p f t", f=8)
        kneg = W[0:CH, 0:2560].rearrange("p (c n) -> p c n", c=NC)
        qkn = W[:, 2560:5120].rearrange("p (f t) -> p f t", f=8)
        ktok = W[0:CH, 5120:7680].rearrange("p (c n) -> p c n", c=NC)
        vtok = XS[0:CH, 0:2560].rearrange("p (c n) -> p c n", c=NC)
        MT = W[0:CH, 7680:8960].rearrange("p (n i) -> p n i", n=NP_)
        KQ = W[0:CH, 8960:10240].rearrange("p (n i) -> p n i", n=NP_)
        TT2 = W[0:CH, 10240:12800].rearrange("p (n a i) -> p n a i", n=NP_, a=2)
        ebc = W[:, 12800:14080].rearrange("p (n i) -> p n i", n=NP_)
        pinv = W[0:CH, 12800:14080].rearrange("p (n i) -> p n i", n=NP_)
        decT = W[0:CH, 14080:15360].rearrange("p (n i) -> p n i", n=NP_)
        wT = W[:, 14080:15360].rearrange("p (n i) -> p n i", n=NP_)
        g2 = W[0:CH, 0:1280].rearrange("p (n i) -> p n i", n=NP_)
        cmask = W[0:CH, 0:1280].rearrange("p (n i) -> p n i", n=NP_)
        cqT = W[:, 15360:16320].rearrange("p (k t) -> p k t", k=3)
        latT = HM[:, 1280:2432].rearrange("p (k t) -> p k t", k=2)
        kT = W[:, 16384:18688].rearrange("p (h t) -> p h t", h=H)
        vk = W[:, 18688:21248].rearrange("p (b n) -> p b n", b=5)
        qTn = W[:, 21248:22528].rearrange("p (h t) -> p h t", h=H)
        qTr = W[0:ROPE, 22528:23808].rearrange("p (h t) -> p h t", h=H)
        kpeT = W[0:ROPE, 23808:24384]
        gstate = X[:, 0:1024].rearrange("p (s n) -> p s n", s=2)
        qraw = X[:, 1024:1792]
        lat_past = X[:, 1792:2304].rearrange("p (b n) -> p b n", b=2)
        kpe_past = X[:, 2304:2432].rearrange("p (b n) -> p b n", b=2)
        otok = X[0:CH, 2432:2944]
        vnew = XS[0:CH, 2560:3072]
        gb = SM[0:CH, 160:200].rearrange("p (c n) -> p c n", c=NC)
        gts = SM[0:CH, 200:220]
        beta = SM[0:CH, 220:240]
        gcum = SM[0:CH, 240:260]
        egc = SM[0:CH, 260:280]
        kds = SM[0:CH, 280:300]
        t20a = SM[0:CH, 300:320]
        t20b = SM[0:CH, 320:340]
        eal = SM[0:CH, 340:344]
        st = SM[:, 344:364]
        ssq = SM[:, 364:376]
        eglast = SM[:, 380:400]
        amx = SM[:, 400:402]
        asum = SM[:, 402:404]
        arec = SM[:, 404:406]
        qk_ss = SM[:, 408:432]
        prob = R[:, 0:640].rearrange("p (u n) -> p u n", u=2)
        probT = R[:, 640:1024 + 384].rearrange("p (u n) -> p u n", u=2)
        nrm_tmp = XS[:, 0:1024]
        qtmp = R[:, 2304:3072]
        om = HM[:, 0:1280].rearrange("p (h t) -> p h t", h=H)
        qmraw = XS[:, 1024:1536]
        qmT = R[:, 1408:2688].rearrange("p (h t) -> p h t", h=H)
        cs_out = XS[0:3, :].rearrange("p (s n) -> p s n", s=2)
        wmq_sb = W[:, 16384:20480].rearrange("p (k n) -> p k n", k=KD)
        wmo_sb = W[:, 20480:24576].rearrange("p (k n) -> p k n", k=4)

        gu_sb = W[:, 0:16384].rearrange("p (k n) -> p k n", k=KD)
        dn_sb = W[:, 16384:24576].rearrange("p (k n) -> p k n", k=KD)
        xparts = V[:, 0:4608].bitcast(BF16).rearrange("p (b s d) -> p b s d", b=TB, s=3)
        yacc = V[:, 4608:7168].rearrange("p (j n) -> p j n", j=NC)
        b3 = V[0:96, 7168:8192].bitcast(BF16)
        braw = V[0:96, 0:2048]
        bhi = V[0:96, 2048:3072].bitcast(BF16)
        bmid = V[0:96, 3072:4096].bitcast(BF16)
        bdn = V[0:E, 4608:5632]
        wr_sb = V[:, 5632:5888].rearrange("p (k n) -> p k n", k=KD)
        gateT = V[0:E, 5888:6272]
        bd = R[:, 0:640].rearrange("p (j t) -> p j t", j=NC)
        xgT = R[:, 640:1152].rearrange("p (k t) -> p k t", k=KD)
        gt_sb, sig_sb, up_sb = R[:, 1152:1664], R[:, 1664:2176], R[:, 2176:2688]
        act_sb = R[:, 2688:3200]
        actT = R[:, 3200:3712].rearrange("p (k t) -> p k t", k=4)
        y_sb = R[:, 3712:4224]
        sel = R[0:96, 4224:4256].bitcast(BF16)
        gcur = R[:, 4256:4261]
        gate = KV[:, 0:96].rearrange("p (b e) -> p b e", b=TB)
        gated = KV[:, 96:256].rearrange("p (j e) -> p j e", j=NC)
        rpos = KV[:, 256:355].rearrange("p (b e) -> p b e", b=TB)
        mask = KV[:, 356:452].rearrange("p (b e) -> p b e", b=TB)
        lg = KV[:, 452:560].rearrange("p (b e) -> p b e", b=TB)
        mrep = KV[:, 560:668].rearrange("p (b e) -> p b e", b=TB)
        top8 = KV[:, 668:692].rearrange("p (b e) -> p b e", b=TB)
        rep8 = KV[:, 692:716].rearrange("p (b e) -> p b e", b=TB)
        S = KV[:, 716:908].bitcast(BF16).rearrange("p (b a s) -> p b a s", b=TB, a=2)
        id3 = KV[0:96, 908:925].bitcast(BF16)
        identb = KV[:, 1212:1276].bitcast(BF16)
        cnt, tot, start = KV[0:E, 988:989], KV[0:E, 989:990], KV[0:E, 990:991]
        flags, pos4 = KV[0:E, 992:996], KV[0:E, 996:1000]
        hot = KV[0:E, 1000:1128].rearrange("p (b s) -> p b s", b=XTRA)
        xlist = KV[:, 1128:1200].bitcast(I32)
        ntop = KV[:, 1200:1203]
        gsum = KV[:, 1203:1206]

        def bank(i, parts=P, **kw):
            return PS[i][0:parts, :]

        def view(i, pattern, parts=P, cols=512, dt=None, **kw):
            a = PS[i][0:parts, 0:cols]
            return a.rearrange(pattern, **kw)

        def bcast(ap, shape, *axes):
            for a in axes:
                ap = ap.unsqueeze(a)
            return ap.broadcast_to(shape)

        def pieces(f):
            return [(upad[:, f, 0:SEQ], 0, SEQ), (upad[:, f, SEQ + 3:SEQ + 3 + DEC], SEQ, DEC)]

        kraw = X[:, 1024:1536]
        cmasks = [W[0:CH, 1280 * i:1280 * i + 1280].rearrange("p (n i) -> p n i", n=NP_) for i in range(2)]

        mla_units, mem_units = [], []
        for h in range(H):
            for b in range(TB):
                rows = P if b < 2 else DEC
                qs = slice(b * P, b * P + rows)
                ks = slice(0, (b + 1) * P) if b < 2 else slice(SEQ, NKEY)
                vs = [vk[:, i, h * P:(h + 1) * P] for i in range(b + 1)] if b < 2 else \
                    [vk[:, 2, h * P:(h + 1) * P], vk[:, 3, h * P:(h + 1) * P], vk[0:DEC, 4, h * P:(h + 1) * P]]
                mla_units.append((rows, [(qTn[:, h, qs], kT[:, h, ks]), (qTr[:, h, qs], kpeT[:, ks])],
                                  ks.stop - ks.start, b < 2, vs, hT[:, H + h, qs]))
                km, vm = (km_p, vm_p) if b < 2 else (km_s, vm_s)
                mem_units.append((rows, [(qmT[:, h, qs], km[:, h, :])], NMEM, False,
                                  [vm[:, i, h * P:(h + 1) * P] for i in range(2)], om[:, h, qs]))

        ROOTS_QK = 5

        block = ctx.enter_context(nc.Block())

        @block.sync
        def _(sp):
            def load(dst, src, name):
                sp.dma_start(dst, src).then_inc(sem(name), 16)

            def k_major(w, k0, k1):
                return w[k0 * P:k1 * P, :].rearrange("(k p) n -> p k n", p=P)

            def b_major(a):
                return a.rearrange("(b p) n -> p b n", p=P)

            load(mem3, b_major(mem_prompt[0]), "ld_mem")
            load(CO[:, :], consts, "ld_const")
            load(wmk_sb, k_major(w_mk[0], 0, KD), "ld_wmk")
            load(kcache, b_major(cache_mem_k[0, 0].rearrange("t h d -> t (h d)")), "ld_kcache")
            load(wmv_sb, k_major(w_mv[0], 0, KD), "ld_wmv")
            load(x3[:, 0:2, :], b_major(x_prompt[0]), "ld_x")
            load(x3[0:DEC, 2, :], x_sample[0], "ld_x")
            for n in range(2):
                load(w_in_sb[:, 4 * n:4 * n + 4, :], k_major(w_in[0], 4 * n, 4 * n + 4), f"ld_win{n}")
            load(wqb_sb, k_major(w_qb[0], 0, 3), "ld_wq")
            load(wkvb_sb, k_major(w_kvb[0], 0, 2), "ld_wq")
            sp.wait_ge(sem("cols_ready"), 2)
            load(vm_s, b_major(cache_mem_v[0, 0].rearrange("t h d -> t (h d)")), "ld_vcache")
            sp.wait_ge(sem("x_scaled"), TB)
            load(gstate[:, 1, :].rearrange("p (h v) -> p h v", h=H), state_gdn[0, 0].rearrange("h k v -> k h v"),
                 "ld_state")
            load(lat_past, b_major(cache_kv_latent[0, 0]), "ld_past")
            load(kpe_past, b_major(cache_k_rope[0, 0]), "ld_past")
            sp.wait_ge(sem("mk_ready"), 2)
            sp.dma_start(b_major(p_mk[0, 0].rearrange("t h d -> t (h d)")), mk_out).then_inc(sem("st_mk"), 16)
            sp.wait_ge(sem("mv_ready"), 2)
            sp.dma_start(b_major(p_mv[0, 0].rearrange("t h d -> t (h d)")), vm_p).then_inc(sem("st_out"), 16)
            sp.wait_ge(sem("state_new"), 4)
            sp.dma_start(p_s[0, 0].rearrange("h k v -> k h v"), gstate[:, 0, :].rearrange("p (h v) -> p h v", h=H))\
              .then_inc(sem("st_state"), 16)
            sp.wait_ge(sem("state_new"), 5)
            sp.dma_start(s_s[0, 0].rearrange("h k v -> k h v"), gstate[:, 1, :].rearrange("p (h v) -> p h v", h=H))\
              .then_inc(sem("st_state"), 16)
            sp.wait_ge(*at("lat_ready"))
            sp.dma_start(b_major(p_lat[0, 0]), cl[:, 0:2, 384:640]).then_inc(sem("st_lat"), 16)
            sp.dma_start(s_lat[0, 0], cl[0:DEC, 2, 384:640]).then_inc(sem("st_lat"), 16)
            sp.wait_ge(*at("kpe_ready"))
            sp.dma_start(b_major(p_kpe[0, 0]), cl[:, 0:2, 640:704]).then_inc(sem("st_lat"), 16)
            sp.dma_start(s_kpe[0, 0], cl[0:DEC, 2, 640:704]).then_inc(sem("st_lat"), 16)
            sp.wait_ge(sem("gdn_mix"), NC)
            sp.wait_ge(sem("st_lat"), 64)
            sp.wait_ge(sem("cl_tr"), 7)
            for n in range(2):
                load(wout_sb[:, 4 * n:4 * n + 4, :], k_major(w_out[0], 4 * n, 4 * n + 4), f"ld_wout{n}")
            sp.wait_ge(sem("cs_ev"), 6)
            sp.dma_start(p_conv[0, 0], cs_out[:, 0, :]).then_inc(sem("st_conv"), 16)
            sp.dma_start(s_conv[0, 0], cs_out[:, 1, :]).then_inc(sem("st_conv"), 16)
            sp.wait_ge(sem("st_state"), 32)
            sp.wait_ge(sem("att_o"), ATT["mem"])
            sp.wait_ge(sem("xpad"), 2)
            load(x3[:, 0:2, :], b_major(x_prompt[0]), "ld_x2")
            load(x3[0:DEC, 2, :], x_sample[0], "ld_x2")
            load(wmq_sb, k_major(w_mq[0], 0, KD), "ld_wmq")
            load(wmo_sb, k_major(w_mo[0], 0, 4), "ld_wmo")
            for k in range(KD):
                load(gu_sb[:, k, :], w_gu[0, 0, k * P:(k + 1) * P, :], f"ld_gu{k}")
            sp.wait_ge(sem("res_add"), RES["x2"][0] + 2 * TB)
            load(wr_sb, k_major(w_router[0], 0, KD), "ld_wr")
            for n in range(3):
                load(braw[32 * n:32 * n + 32, :], b_gu[0], "ld_bias")
            load(bdn, b_down[0], "ld_bias")
            sp.wait_ge(sem("res_add"), RES["x3"][0] + 2 * TB)
            for k in range(KD // 2):
                load(dn_sb[:, 2 * k:2 * k + 2, :], k_major(w_down[0, 0], 2 * k, 2 * k + 2), f"ld_dn{k}")
            sp.wait_ge(sem("y0_add"), 2 * TB)
            for j in range(NC):
                rows = slice(64 * (j % 2), 64 * (j % 2) + 64)
                for half in range(2):
                    load(yacc[64 * half:64 * half + 64, j, :], x3[rows, j // 2, 512 * half:512 * half + 512], "ld_yacc")
                    load(gated[64 * half:64 * half + 64, j, :], gate[rows, j // 2, :], "ld_yacc")

            def expert_loads(it, e):
                for k in range(KD):
                    sp.wait_ge(sem("gu_used"), it * KD + (k + 1))
                    sp.dma_start(gu_sb[:, k, :], w_gu[0, bass.ds(e, 1), k * P:(k + 1) * P, :]
                                 .rearrange("a p n -> p (a n)")).then_inc(sem(f"ld_gu{k}"), 16)
                for k in range(KD // 2):
                    sp.wait_ge(sem("dn_used"), it * (KD // 2) + (k + 1))
                    sp.dma_start(dn_sb[:, 2 * k:2 * k + 2, :], w_down[0, bass.ds(e, 1), 2 * k * P:(2 * k + 2) * P, :]
                                 .rearrange("a (k p) n -> p (a k) n", p=P)).then_inc(sem(f"ld_dn{k}"), 16)

            with sp.Fori(0, E - 1) as it:
                expert_loads(it, it + 1)
            sp.wait_ge(*at("list_ready"))
            n_extra = sp.value_load(xlist[0:1, 2 * LIST:2 * LIST + 1], min_val=0, max_val=LIST - 1)
            with sp.If(n_extra > 0):
                with sp.Fori(0, n_extra) as j:
                    e = sp.value_load(xlist[0:1, bass.ds(j, 1)], min_val=0, max_val=E - 1)
                    expert_loads(j + (E - 1), e)
            sp.wait_ge(*at("y_final"))
            for j in range(NC):
                dst = yp[0, j * CH:(j + 1) * CH, :] if j < SEQ // CH else ys[0]
                for half in range(2):
                    sp.dma_start(dst[:, 512 * half:512 * half + 512], yacc[64 * half:64 * half + 64, j, :])\
                      .then_inc(sem("st_out"), 16)
            for name, n in (("st_state", 2), ("st_lat", 4), ("st_conv", 2), ("st_mk", 1), ("st_out", 1 + 2 * NC)):
                sp.wait_ge(sem(name), 16 * n)

        @block.gpsimd
        def _(pool):
            done = [0]
            pool.wait_ge(sem("ld_const"), 16)

            def root(tile):
                pool.wait_ge(sem("var_ready"), done[0] + 1)
                done[0] += 1
                pool.tensor_tensor(tile, tile, minus_half[0:tile.shape[0], :].broadcast_to(list(tile.shape)), ALU.pow).then_inc(sem("root_ready"), 1)

            def head_roots(n, rows, heads):
                for _ in range(n):
                    root(st[0:rows, 0:heads])

            root(st[:, 0:2])
            root(ssq[:, 0:3])
            head_roots(2, P, H)
            root(qk_ss)
            head_roots(NC, CH, H)
            head_roots(3, P, TB)
            for rows in (P, P, DEC):
                head_roots(1, rows, H)
            for rows in (P, P, P, P, DEC):
                head_roots(1, rows, H)
            root(ssq[:, 5:8])
            for rows in (P, P, DEC):
                head_roots(1, rows, H)
            root(ssq[:, 8:11])

        @block.scalar
        def _(act):
            def run(out, in_, func=ACT.Copy, **kw):
                return act.activation(out, in_, func, **kw)

            act.dma_start(conv7[0:3, :], state_conv[0, 0]).then_inc(sem("ld_rows"), 16)
            act.dma_start(conv7[3:7, :], conv_w[0]).then_inc(sem("ld_rows"), 16)
            for src, r0, nr in ((norm_mix, 0, 8), (norm_mem, 8, 8), (mem_norm, 16, 8), (norm_ffn, 24, 8),
                                (q_a_norm, 32, 3), (k_nope_norm, 35, 1), (gdn_norm, 36, 1), (mq_norm, 37, 1)):
                act.dma_start(g_rows[r0:r0 + nr, :], src[0].rearrange("(k p) -> k p", p=P)).then_inc(sem("ld_rows"), 16)
            for src, c0, n in ((kv_a_norm, 0, 256), (q_norm, 256, 192), (k_rope_norm, 448, 64), (mk_norm, 512, 128),
                               (b_router, 640, 32), (dt_bias, 672, 4), (a_log, 676, 4)):
                act.dma_start(GN[:, c0:c0 + n], src.broadcast_to([P, n])).then_inc(sem("ld_gn"), 16)

            def squares(src, b, col, junk, tag):
                run(junk, src[:, b, :], ACT.Square, accum_out=ssq[:, col:col + 1]).then_inc(sem(tag), 1)

            def feature_major(n, banks, tag, dst, cols, gain, width):
                act.wait_ge(sem("rows_tr"), NORM[tag] + n + 1)
                run(dst[:, n, :], PS[banks[n % len(banks)]][:, 0:width], scale=gain[:, n:n + 1])\
                    .then_inc(sem("rows_ev"), 1)

            act.wait_ge(sem("ld_mem"), 16)
            for b in range(2):
                if b:
                    act.wait_ge(sem("mem_sq"), b)
                squares(mem3, b, 3 + b, W[:, 23104:24128], "mem_sq")
            act.wait_ge(sem("cols_tr"), 1)
            run(convw, PS[7][:, 0:96].rearrange("p (f j) -> p f j", j=8)[:, :, 0:7]).then_inc(sem("cols_ready"), 1)
            act.wait_ge(sem("cols_tr"), 2)
            run(GC[:, 0:38], PS[6][:, 0:38]).then_inc(sem("cols_ready"), 1)
            act.wait_ge(sem("cols_ready"), 2)
            for k in range(KD):
                feature_major(k, (0, 1), "mem", mT, None, c_memn, NMEM)
            act.wait_ge(sem("ld_x"), 32)
            act.wait_ge(sem("xpad"), 1)
            act.wait_ge(sem("mem_sq"), 2)
            for b in range(TB):
                if b:
                    act.wait_ge(sem("x_sq"), b)
                squares(x3, b, b, W[:, 23104:24128], "x_sq")
            for b in range(2):
                act.wait_ge(sem("mk_mm"), b + 1)
                run(mk_out[:, b, :], PS[2 + b][:, :]).then_inc(sem("mk_ev"), 1)
            for b in range(2):
                act.wait_ge(sem("mv_mm"), b + 1)
                run(vm_p[:, b, :], PS[4 + b][:, :]).then_inc(sem("mv_ready"), 1)
            for b in range(2):
                act.wait_ge(sem("km_tr"), b + 1)
                if b == 0:
                    act.wait_ge(sem("cols_tr"), 2)
                run(km_s[:, :, b * P:(b + 1) * P], PS[6 + b][:, :].rearrange("p (h t) -> p h t", h=H))\
                    .then_inc(sem("km_ev"), 1)
            act.wait_ge(sem("mv_mm"), 2)
            for k in range(KD):
                feature_major(k, (0, 1), "x", hT, None, c_mix, T)
            for b in range(2):
                act.wait_ge(sem("km_tr"), b + 3)
                run(km_p[:, :, b * P:(b + 1) * P], PS[6 + b][:, :].rearrange("p (h t) -> p h t", h=H))\
                    .then_inc(sem("km_ev"), 1)
            act.wait_ge(*at("upad_ready"))
            for f in range(NU + NZ + 3):
                if f <= NU + NZ:
                    act.wait_ge(sem("u_mm"), f + 1)
                    src = PS[2 + f % 3]
                    if f < NU:
                        run(upad[:, f, 3:3 + SEQ], src[:, 0:SEQ])
                        run(upad[:, f, 6 + SEQ:6 + T], src[:, SEQ:T]).then_inc(sem("u_ev"), 1)
                    elif f < NU + NZ:
                        run(ztile[:, f - NU, :], src[:, 0:T], ACT.Silu).then_inc(sem("u_ev"), 1)
                    else:
                        run(abT, src[0:2 * H, 0:T]).then_inc(sem("u_ev"), 1)
                if 2 <= f < NU + 2:
                    act.wait_ge(sem("conv_done"), f - 1)
                    run(upad[:, f - 2, 0:323], conv_tmp, ACT.Silu).then_inc(sem("silu_done"), 1)
            for n in range(2 * TB):
                b, half = n // 2, n % 2
                rows = P if b < 2 else DEC
                c0, c1 = (0, 384) if half == 0 else (384, CLW)
                act.wait_ge(sem("cl_mm"), n + 1)
                run(cl[0:rows, b, c0:c1], PS[n % 2][0:rows, 0:c1 - c0]).then_inc(sem("cl_ev"), 1)

            act.wait_ge(*at("gb_ready"))
            run(beta.rearrange("p (c h) -> p c h", c=NC), gb[:, :, H:2 * H], ACT.Sigmoid).then_inc(mark("beta_ready"), 1)
            act.wait_ge(sem("ld_gn"), 112)
            run(eal, g_alog, ACT.Exp)
            act.wait_ge(*at("sp_abs"))
            run(t20b, t20b, ACT.Exp, scale=-1.0).then_inc(sem("sp_act"), 1)
            act.wait_ge(sem("sp_act"), 1)
            run(t20b, t20b, ACT.Ln, bias=1.0).then_inc(sem("sp_act"), 1)
            act.wait_ge(*at("gcum_ready"))
            run(egc, gcum, ACT.Exp).then_inc(mark("egc_ready"), 1)
            act.wait_ge(*at("gbc_mm"))
            for n, w in enumerate((512, 512, 256)):
                m = run(W[:, 12800 + 512 * n:12800 + 512 * n + w], PS[n][:, 0:w], ACT.Exp)
            m.then_inc(mark("ebc_ready"), 1)
            act.wait_ge(*at("diff_ready"))
            run(decT, decT, ACT.Exp).then_inc(sem("dec_exp"), 1)
            run(kds, kds, ACT.Exp).then_inc(sem("dec_exp"), 1)
            act.wait_ge(sem("silu_done"), NU)
            run(sq8[:, :, 0:SEQ], upad[:, 0:8, 0:SEQ], ACT.Square).then_inc(sem("sq_ready"), 1)
            run(sq8[:, :, SEQ:T], upad[:, 0:8, SEQ + 3:SEQ + 3 + DEC], ACT.Square).then_inc(sem("sq_ready"), 1)
            act.wait_ge(sem("rows_tr"), NORM["x"] + KD)
            for n in range(2 * NC):
                c = n // 2
                act.wait_ge(sem("kv_tr"), n + 1)
                run((vtok if n % 2 else ktok)[:, c, :], PS[3 + n % 4][0:CH, :]).then_inc(sem("kv_ev"), 1)
            for c in range(NC):
                act.wait_ge(sem("t0_tr"), c + 1)
                run(TT2[:, 4 * c:4 * c + 4, 0, :], PS[3 + c % 4][0:CH, 0:256].rearrange("p (h i) -> p h i", h=H))\
                    .then_inc(sem("t0_ev"), 1)
            act.wait_ge(*at("qg_ready"))
            for l in range(1, len(LEVELS)):
                for c in range(NC):
                    act.wait_ge(sem("p_mm"), NC * (l - 1) + min(c | 1, NC - 1) + 1)
                    if l > 1:
                        act.wait_ge(sem("q_mm"), NC * (l - 2) + c + 1)
                    run(pinv[:, 4 * c:4 * c + 4, :], PS[c // 2][0:CH, 256 * (c % 2):256 * (c % 2) + 256]
                        .rearrange("p (h i) -> p h i", h=H)).then_inc(sem("p_ev"), 1)
            for c in range(NC):
                act.wait_ge(sem("w_mm"), min(c | 1, NC - 1) + 1)
                run(wT[:, 4 * c:4 * c + 4, :], PS[c // 2][:, 256 * (c % 2):256 * (c % 2) + 256]
                    .rearrange("p (h i) -> p h i", h=H)).then_inc(sem("w_ev"), 1)
            for c in range(NC):
                act.wait_ge(sem("o_mm"), c + 1)
                if c:
                    act.wait_ge(sem("o_tr"), c)
                run(otok, PS[4][0:CH, :]).then_inc(sem("o_copy"), 1)

            for k in range(3):
                act.wait_ge(sem("cl_tr"), k + 1)
                run(cqT[:, k, :], PS[k % 2][:, 0:T], scale=c_qa[:, k:k + 1]).then_inc(sem("cq_ev"), 1)
            for k in range(2):
                act.wait_ge(sem("cl_tr"), 4 + k)
                run(latT[:, k, 0:SEQ], PS[0][:, 0:SEQ])
                run(latT[:, k, SEQ:NKEY], PS[1][:, 0:PAST + DEC]).then_inc(sem("lat_ev"), 1)
            act.wait_ge(sem("cl_tr"), 7)
            run(kpeT[:, 0:SEQ], PS[0][0:ROPE, 0:SEQ])
            run(kpeT[:, SEQ:NKEY], PS[1][0:ROPE, 0:PAST + DEC]).then_inc(mark("kpe_ev"), 1)
            act.wait_ge(sem("st_mk"), 16)
            for b in range(TB):
                rows = P if b < 2 else DEC
                act.wait_ge(sem("q_mmla"), b + 1)
                if b:
                    act.wait_ge(sem("qT_tr"), b)
                for half in range(2):
                    m = run(qraw[0:rows, 384 * half:384 * half + 384], PS[2 + half][0:rows, 0:384])
                m.then_inc(sem("q_ev"), 1)
                act.wait_ge(sem("qT_tr"), b + 1)
                run(qTn[:, :, b * P:b * P + rows], PS[4][:, :].rearrange("p (h t) -> p h t", h=H)[:, :, 0:rows])
                run(qTr[:, :, b * P:b * P + rows], PS[5][0:ROPE, :].rearrange("p (h t) -> p h t", h=H)[:, :, 0:rows])\
                    .then_inc(sem("qT_ev"), 1)
            for kb in range(5):
                rows = P if kb < 4 else DEC
                act.wait_ge(sem("kvl_mm"), 2 * kb + 1)
                if kb:
                    act.wait_ge(sem("kT_tr"), kb)
                run(kraw[0:rows, :], PS[0][0:rows, :]).then_inc(sem("k_raw"), 1)
                act.wait_ge(sem("kvl_mm"), 2 * kb + 2)
                run(vk[0:rows, kb, :], PS[1][0:rows, :]).then_inc(sem("v_raw"), 1)
                act.wait_ge(sem("kT_tr"), kb + 1)
                run(kT[:, :, kb * P:kb * P + rows], PS[6][:, :].rearrange("p (h t) -> p h t", h=H)[:, :, 0:rows],
                    scale=c_kn).then_inc(sem("kT_ev"), 1)

            def attention(tag, units, scale):
                for n in range(len(units) + 1):
                    if n < len(units):
                        rows, terms, nkeys, masked, vs, out = units[n]
                        act.wait_ge(sem("att_mx"), ATT[tag] + n + 1)
                        if n >= 2:
                            act.wait_ge(sem("att_tr"), ATT[tag] + n - 1)
                        run(prob[0:rows, n % 2, 0:nkeys], PS[n % 2][0:rows, 0:nkeys], ACT.Exp, scale=scale,
                            bias=amx[0:rows, n % 2:n % 2 + 1], accum_out=asum[0:rows, n % 2:n % 2 + 1])\
                            .then_inc(sem("att_ex"), 1)
                    if n >= 1:
                        rows, terms, nkeys, masked, vs, out = units[n - 1]
                        u = (n - 1) % 2
                        act.wait_ge(sem("att_tr"), ATT[tag] + n)
                        if n >= 3:
                            act.wait_ge(sem("att_pv"), ATT[tag] + n - 2)
                        if vs[-1].shape[0] == P:
                            m = run(probT[:, u, 0:len(vs) * P].rearrange("p (t q) -> p t q", q=P)[:, :, 0:rows],
                                    PS[2 + u][:, 0:len(vs) * P].rearrange("p (t q) -> p t q", q=P)[:, :, 0:rows])
                        else:
                            for t, v in enumerate(vs):
                                m = run(probT[0:v.shape[0], u, t * P:t * P + rows], PS[2 + u][0:v.shape[0], t * P:t * P + rows])
                        m.then_inc(sem("att_pt"), 1)

            attention("mla", mla_units, QK ** -0.5)

            act.wait_ge(sem("o_tr"), NC)
            for n in range(6):
                s, q = n // 3, n % 3
                act.wait_ge(sem("cs_tr"), n + 1)
                run(cs_out[:, s, 512 * q:512 * q + 512], PS[6 + n % 2][0:3, :]).then_inc(sem("cs_ev"), 1)

            act.wait_ge(sem("st_conv"), 32)
            for b in range(TB):
                act.wait_ge(sem("res_add"), RES["x2"][0] + 2 * b + 2)
                squares(x3, b, 5 + b, xs3[:, b, :], "res_sq")
            act.wait_ge(sem("res_mm"), RES["x2"][0] + 2 * TB)
            for k in range(KD):
                feature_major(k, (6, 7), "x2n", hT, None, c_mem, T)
            act.wait_ge(sem("rows_tr"), NORM["x2n"] + KD)
            for b in range(TB):
                rows = P if b < 2 else DEC
                act.wait_ge(sem("qm_mm"), b + 1)
                if b:
                    act.wait_ge(sem("qmT_tr"), b)
                run(qmraw[0:rows, :], PS[b][0:rows, :]).then_inc(sem("qm_ev"), 1)
                act.wait_ge(sem("qmT_tr"), b + 1)
                run(qmT[:, :, b * P:b * P + rows], PS[4 + b % 2][:, :].rearrange("p (h t) -> p h t", h=H)[:, :, 0:rows],
                    scale=c_mq).then_inc(sem("qmT_ev"), 1)
            attention("mem", mem_units, HD ** -0.5)

            for b in range(TB):
                act.wait_ge(sem("res_add"), RES["x3"][0] + 2 * b + 2)
                squares(x3, b, 8 + b, xs3[:, b, :], "res_sq")
            for k in range(KD):
                feature_major(k, (6, 7), "x3n", hT, None, c_ffn, T)
            act.wait_ge(*at("top_ready"))
            for b in range(TB):
                rows = P if b < 2 else DEC
                run(gate[0:rows, b, :], lg[0:rows, b, 0:E], ACT.Exp, bias=ntop[0:rows, b:b + 1]).then_inc(sem("gate_exp"), 1)
            act.wait_ge(*at("gt_tr"))
            run(gateT, PS[3][0:E, 0:384]).then_inc(mark("gt_ev"), 1)
            for b in range(TB):
                run(xparts[:, b, 0, :], xs3[:, b, :]).then_inc(sem("part0"), 1)

            def turn(it):
                act.wait_ge(sem("gt_ready"), it + 1)
                run(sig_sb, gt_sb, ACT.Sigmoid, scale=ALPHA).then_inc(sem("sig_ready"), 1)
                act.wait_ge(sem("actT_tr"), it + 1)
                run(actT, PS[2][:, :].rearrange("p (k t) -> p k t", k=4)).then_inc(sem("actT_ev"), 1)
                act.wait_ge(sem("dn_used"), it * (KD // 2) + KD // 2)
                run(y_sb, PS[3][:, :]).then_inc(sem("y_ev"), 1)

            with act.Fori(0, E) as it:
                turn(it)
            act.wait_ge(*at("list_ready"))
            n_extra = act.value_load(xlist[0:1, 2 * LIST:2 * LIST + 1], min_val=0, max_val=LIST - 1)
            with act.If(n_extra > 0):
                with act.Fori(0, n_extra) as j:
                    turn(j + E)

        @block.tensor
        def _(pe):
            def mm(out, lhsT, rhs, start=True, stop=True):
                return pe.matmul(out, lhsT, rhs, start=start, stop=stop)

            def tr(out, in_):
                return pe.transpose(out, in_, ident[0:in_.shape[0], 0:in_.shape[0]])

            def norm_transposes(src, nb, banks, tag):
                for k in range(KD):
                    if k >= len(banks):
                        pe.wait_ge(sem("rows_ev"), NORM[tag] + k - len(banks) + 1)
                    for b in range(nb):
                        m = tr(PS[banks[k % len(banks)]][:, b * P:(b + 1) * P], src[:, b, k * P:(k + 1) * P])
                    m.then_inc(sem("rows_tr"), 1)

            pe.wait_ge(sem("ld_const"), 16)
            pe.wait_ge(sem("ld_rows"), 160)
            for f in range(NU):
                m = tr(PS[7][:, 8 * f:8 * f + 7], conv7[:, f * P:(f + 1) * P])
            m.then_inc(sem("cols_tr"), 1)
            tr(PS[6][:, 0:38], g_rows).then_inc(sem("cols_tr"), 1)

            pe.wait_ge(sem("mem_scaled"), 2)
            norm_transposes(mem3, 2, (0, 1), "mem")
            pe.wait_ge(sem("rows_ev"), NORM["mem"] + KD)
            pe.wait_ge(sem("ld_wmk"), 16)
            for b in range(2):
                for k in range(KD):
                    m = mm(PS[2 + b][:, :], mT[:, k, b * P:(b + 1) * P], wmk_sb[:, k, :], k == 0, k == KD - 1)
                m.then_inc(sem("mk_mm"), 1)
            pe.wait_ge(sem("ld_wmv"), 16)
            for b in range(2):
                for k in range(KD):
                    m = mm(PS[4 + b][:, :], mT[:, k, b * P:(b + 1) * P], wmv_sb[:, k, :], k == 0, k == KD - 1)
                m.then_inc(sem("mv_mm"), 1)
            pe.wait_ge(sem("ld_kcache"), 16)
            pe.wait_ge(sem("cols_ready"), 2)
            for b in range(2):
                for h in range(H):
                    m = tr(PS[6 + b][:, h * P:(h + 1) * P], kcache[:, b, h * P:(h + 1) * P])
                m.then_inc(sem("km_tr"), 1)

            pe.wait_ge(sem("x_scaled"), TB)
            norm_transposes(xs3, TB, (0, 1), "x")
            for b in range(2):
                pe.wait_ge(sem("mk_ready"), b + 1)
                pe.wait_ge(sem("km_ev"), b + 1)
                for h in range(H):
                    m = tr(PS[6 + b][:, h * P:(h + 1) * P], mk_out[:, b, h * P:(h + 1) * P])
                m.then_inc(sem("km_tr"), 1)
            pe.wait_ge(sem("rows_ev"), NORM["x"] + KD)
            for f in range(NU + NZ + 1):
                cols = slice(f * P, (f + 1) * P) if f < NU + NZ else slice(AB0, AB0 + 2 * H)
                rows = cols.stop - cols.start
                if f < 3:
                    pe.wait_ge(sem("mk_ev" if f < 2 else "mv_ready"), f + 1 if f < 2 else 1)
                else:
                    pe.wait_ge(sem("u_ev"), f - 2)
                for k in range(KD):
                    if f == 0 and k % 4 == 0:
                        pe.wait_ge(sem(f"ld_win{k // 4}"), 16)
                    m = mm(PS[2 + f % 3][0:rows, 0:T], w_in_sb[:, k, cols], hT[:, k, :], k == 0, k == KD - 1)
                m.then_inc(sem("u_mm"), 1)
            for n in range(2 * TB):
                b, half = n // 2, n % 2
                rows = P if b < 2 else DEC
                c0, c1 = (0, 384) if half == 0 else (384, CLW)
                if n >= 2:
                    pe.wait_ge(sem("cl_ev"), n - 1)
                else:
                    pe.wait_ge(sem("rows_ev"), NORM["x"] + KD)
                for k in range(KD):
                    m = mm(PS[n % 2][0:rows, 0:c1 - c0], hT[:, k, b * P:b * P + rows],
                           w_in_sb[:, k, CL0 + c0:CL0 + c1], k == 0, k == KD - 1)
                m.then_inc(sem("cl_mm"), 1)

            pe.wait_ge(sem("u_ev"), NU + NZ + 1)
            pe.wait_ge(sem("km_ev"), 4)
            for c in range(NC):
                m = tr(PS[7][0:CH, 8 * c:8 * c + 8], abT[:, c * CH:(c + 1) * CH])
            m.then_inc(mark("ab_tr"), 1)
            pe.wait_ge(*at("g_ready"))
            mm(PS[7][0:CH, 64:84], u64, gts).then_inc(mark("gcum_mm"), 1)
            pe.wait_ge(*at("g2_ready"))
            pe.wait_ge(sem("cl_ev"), 2 * TB)
            for n, w in enumerate((512, 512, 256)):
                m = mm(PS[n][:, 0:w], ones[0:CH, :], W[0:CH, 512 * n:512 * n + w])
            m.then_inc(mark("gbc_mm"), 1)
            pe.wait_ge(sem("sq_ready"), 2)
            pe.wait_ge(*at("gcum_ready"))
            for b in range(TB):
                rows = P if b < 2 else DEC
                for f in range(2 * H):
                    m = mm(PS[7][0:rows, 96 + 8 * b + f:97 + 8 * b + f], sq8[:, f, b * P:b * P + rows], ones[:, 0:1])
            m.then_inc(mark("sum_mm"), 1)
            pe.wait_ge(sem("root_ready"), ROOTS_QK)
            for f in range(2 * H):
                if f >= 4:
                    pe.wait_ge(sem("qkn_ready"), f - 3)
                for b in range(TB):
                    rows = P if b < 2 else DEC
                    m = mm(PS[3 + f % 4][:, b * P:b * P + rows],
                           qk_ss[0:rows, 8 * b + f:8 * b + f + 1].broadcast_to([rows, P]), ident[0:rows, 0:rows])
                m.then_inc(sem("ss_mm"), 1)
            pe.wait_ge(sem("qkn_ready"), 2 * H)
            for n in range(2 * NC):
                c, isv = n // 2, n % 2
                if n >= 4:
                    pe.wait_ge(sem("kv_ev"), n - 3)
                for h in range(H):
                    src = qkn[:, H + h, c * CH:(c + 1) * CH] if not isv else \
                        (upad[:, 2 * H + h, c * CH:(c + 1) * CH] if c < 4 else upad[:, 2 * H + h, SEQ + 3:SEQ + 3 + CH])
                    m = tr(PS[3 + n % 4][0:CH, h * P:(h + 1) * P], src)
                m.then_inc(sem("kv_tr"), 1)
            pe.wait_ge(*at("dec_ready"))
            qkh = qkn.rearrange("p (a h) t -> p a h t", a=2)
            for c in range(NC):
                if c >= 3:
                    pe.wait_ge(sem("kq_ev"), c - 2)
                for h in range(H):
                    m = mm(PS[c % 3][0:CH, h * P:(h + 1) * P].rearrange("p (a i) -> p a i", a=2),
                           qkn[:, H + h, c * CH:(c + 1) * CH], qkh[:, :, h, c * CH:(c + 1) * CH])
                m.then_inc(sem("kq_mm"), 1)
            pe.wait_ge(sem("kv_ev"), 2 * NC)
            for c in range(NC):
                pe.wait_ge(sem("tt0"), c + 1)
                for h in range(H):
                    m = tr(PS[3 + c % 4][0:CH, h * CH:(h + 1) * CH], TT2[:, 4 * c + h, 1, :])
                m.then_inc(sem("t0_tr"), 1)
                if c == NC - 2:
                    pe.wait_ge(sem("t0_ev"), 1)
            for l in range(1, len(LEVELS)):
                pe.wait_ge(sem("cm_ready"), l)
                for c in range(NC):
                    pe.wait_ge(sem("t0_ev") if l == 1 else sem("tt_ev"), NC if l == 1 else NC * (l - 2) + c + 1)
                    if c == 0:
                        pe.wait_ge(sem("kq_ev"), NC)
                    for h in range(H):
                        i = 4 * c + h
                        m = mm(PS[c // 2][0:CH, 256 * (c % 2) + h * CH:256 * (c % 2) + (h + 1) * CH],
                               cmasks[l % 2][:, i, :], TT2[:, i, 0, :])
                    m.then_inc(sem("p_mm"), 1)
                for c in range(NC):
                    pe.wait_ge(sem("p_ev"), NC * (l - 1) + c + 1)
                    for h in range(H):
                        i = 4 * c + h
                        mm(PS[3 + c][0:CH, h * P:h * P + CH], TT2[:, i, 1, :], pinv[:, i, :])
                        m = mm(PS[3 + c][0:CH, h * P + CH:(h + 1) * P], pinv[:, i, :], TT2[:, i, 1, :])
                    m.then_inc(sem("q_mm"), 1)
            pe.wait_ge(sem("tt_ev"), NC * (len(LEVELS) - 1))
            pe.wait_ge(*at("kneg_ready"))
            for c in range(NC):
                for h in range(H):
                    i = 4 * c + h
                    m = mm(PS[c // 2][:, 256 * (c % 2) + h * CH:256 * (c % 2) + (h + 1) * CH],
                           kneg[:, c, h * P:(h + 1) * P], TT2[:, i, 1, :])
                m.then_inc(sem("w_mm"), 1)
            pe.wait_ge(sem("ld_state"), 16)
            pe.wait_ge(*at("qg_ready"))
            pe.wait_ge(*at("kd_ready"))
            for c in range(NC):
                s = 0 if c < 4 else 1
                pe.wait_ge(sem("w_ev"), c + 1)
                if c:
                    pe.wait_ge(sem("state_new"), c)
                else:
                    pe.wait_ge(*at("state0"))
                for h in range(H):
                    hs, i = slice(h * P, (h + 1) * P), 4 * c + h
                    mm(PS[3][0:CH, hs], TT2[:, i, 1, :], vtok[:, c, hs], True, False)
                    m = mm(PS[3][0:CH, hs], wT[:, i, :], gstate[:, s, hs], False, True)
                m.then_inc(sem("vn_mm"), 1)
                pe.wait_ge(sem("vn_ready"), c + 1)
                if c:
                    pe.wait_ge(sem("o_copy"), c)
                for h in range(H):
                    hs, i = slice(h * P, (h + 1) * P), 4 * c + h
                    m = mm(PS[5][:, hs], ktok[:, c, hs], vnew[:, hs])
                m.then_inc(sem("ds_mm"), 1)
                for h in range(H):
                    hs, i = slice(h * P, (h + 1) * P), 4 * c + h
                    mm(PS[4][0:CH, hs], qkn[:, h, c * CH:(c + 1) * CH], gstate[:, s, hs], True, False)
                    m = mm(PS[4][0:CH, hs], KQ[:, i, :], vnew[:, hs], False, True)
                m.then_inc(sem("o_mm"), 1)
                pe.wait_ge(sem("o_norm"), c + 1)
                for h in range(H):
                    m = tr(PS[6][:, h * CH:(h + 1) * CH], otok[:, h * P:(h + 1) * P])
                m.then_inc(sem("o_tr"), 1)

            pe.wait_ge(*at("cq_ready"))
            pe.wait_ge(sem("w_ev"), NC)
            for k in range(3):
                if k >= 2:
                    pe.wait_ge(sem("cq_ev"), k - 1)
                for b in range(TB):
                    m = tr(PS[k % 2][:, b * P:(b + 1) * P], cl[:, b, k * P:(k + 1) * P])
                m.then_inc(sem("cl_tr"), 1)
            pe.wait_ge(sem("cq_ev"), 3)
            pe.wait_ge(*at("lat_ready"))
            pe.wait_ge(sem("ld_past"), 32)
            for k in range(2):
                cs = slice(384 + k * P, 384 + (k + 1) * P)
                if k:
                    pe.wait_ge(sem("lat_ev"), 1)
                for b in range(2):
                    tr(PS[0][:, b * P:(b + 1) * P], cl[:, b, cs])
                for b in range(2):
                    tr(PS[1][:, b * P:(b + 1) * P], lat_past[:, b, k * P:(k + 1) * P])
                tr(PS[1][:, 256:320], cl[0:DEC, 2, cs]).then_inc(sem("cl_tr"), 1)
            pe.wait_ge(*at("kpe_ready"))
            pe.wait_ge(sem("lat_ev"), 2)
            for b in range(2):
                tr(PS[0][0:ROPE, b * P:(b + 1) * P], cl[:, b, 640:704])
            for b in range(2):
                tr(PS[1][0:ROPE, b * P:(b + 1) * P], kpe_past[:, b, :])
            tr(PS[1][0:ROPE, 256:320], cl[0:DEC, 2, 640:704]).then_inc(sem("cl_tr"), 2)
            pe.wait_ge(sem("ld_wq"), 32)
            pe.wait_ge(sem("gdn_mix"), NC)
            for b in range(TB):
                rows = P if b < 2 else DEC
                if b:
                    pe.wait_ge(sem("q_ev"), b)
                for half in range(2):
                    for k in range(3):
                        m = mm(PS[2 + half][0:rows, 0:384], cqT[:, k, b * P:b * P + rows],
                               wqb_sb[:, k, 384 * half:384 * half + 384], k == 0, k == 2)
                m.then_inc(sem("q_mmla"), 1)
                pe.wait_ge(sem("q_ready"), b + 1)
                if b:
                    pe.wait_ge(sem("qT_ev"), b)
                for h in range(H):
                    tr(PS[4][:, h * P:h * P + rows], qraw[0:rows, h * QK:h * QK + P])
                for h in range(H):
                    m = tr(PS[5][0:ROPE, h * P:h * P + rows], qraw[0:rows, h * QK + P:(h + 1) * QK])
                m.then_inc(sem("qT_tr"), 1)
            pe.wait_ge(*at("kpe_ev"))
            pe.wait_ge(sem("qT_ev"), TB)
            wk4 = wkvb_sb.rearrange("p k (h n) -> p k h n", h=H)
            for kb in range(5):
                rows = P if kb < 4 else DEC
                if kb:
                    pe.wait_ge(sem("k_raw"), kb)
                    pe.wait_ge(sem("v_raw"), kb)
                for part in range(2):
                    for k in range(2):
                        m = mm(PS[part][0:rows, :].rearrange("p (h n) -> p h n", h=H),
                               latT[:, k, kb * P:kb * P + rows], wk4[:, k, :, part * P:(part + 1) * P], k == 0, k == 1)
                    m.then_inc(sem("kvl_mm"), 1)
                pe.wait_ge(sem("k_norm"), kb + 1)
                if kb:
                    pe.wait_ge(sem("kT_ev"), kb)
                for h in range(H):
                    m = tr(PS[6][:, h * P:h * P + rows], kraw[0:rows, h * P:(h + 1) * P])
                m.then_inc(sem("kT_tr"), 1)

            def attention(tag, units):
                for n in range(len(units) + 2):
                    if n < len(units):
                        rows, terms, nkeys, masked, vs, out = units[n]
                        if n >= 2:
                            pe.wait_ge(sem("att_ex"), ATT[tag] + n - 1)
                        for t, (q, k) in enumerate(terms):
                            m = mm(PS[n % 2][0:rows, 0:nkeys], q, k, t == 0, t == len(terms) - 1)
                        m.then_inc(sem("att_s"), 1)
                    if 1 <= n <= len(units):
                        rows, terms, nkeys, masked, vs, out = units[n - 1]
                        u = (n - 1) % 2
                        pe.wait_ge(sem("att_nm"), ATT[tag] + n)
                        if n >= 3:
                            pe.wait_ge(sem("att_pt"), ATT[tag] + n - 2)
                        for t, v in enumerate(vs):
                            kr = v.shape[0]
                            m = tr(PS[2 + u][0:kr, t * P:t * P + rows], prob[0:rows, u, t * P:t * P + kr])
                        m.then_inc(sem("att_tr"), 1)
                    if n >= 2:
                        rows, terms, nkeys, masked, vs, out = units[n - 2]
                        u = n % 2
                        pe.wait_ge(sem("att_pt"), ATT[tag] + n - 1)
                        if n >= 4:
                            pe.wait_ge(sem("att_o"), ATT[tag] + n - 3)
                        for t, v in enumerate(vs):
                            kr = v.shape[0]
                            m = mm(PS[4 + u][:, 0:rows], v, probT[0:kr, u, t * P:t * P + rows], t == 0, t == len(vs) - 1)
                        m.then_inc(sem("att_pv"), 1)

            pe.wait_ge(sem("kT_ev"), 5)
            pe.wait_ge(sem("v_raw"), 5)
            attention("mla", mla_units)

            pe.wait_ge(sem("att_o"), ATT["mem"])
            for n in range(6):
                s, q = n // 3, n % 3
                if n >= 2:
                    pe.wait_ge(sem("cs_ev"), n - 1)
                for i in range(4):
                    m = tr(PS[6 + n % 2][0:3, i * P:(i + 1) * P], ulast[:, 4 * q + i, s, :])
                m.then_inc(sem("cs_tr"), 1)

            def project(tag, lhs, w, nk, loads, banks):
                for n in range(2 * TB):
                    b, half = n // 2, n % 2
                    rows = P if b < 2 else DEC
                    if n >= len(banks):
                        pe.wait_ge(sem("res_add"), RES[tag][0] + n - len(banks) + 1)
                    for k in range(nk):
                        if n == 0 and k % (nk // len(loads)) == 0:
                            pe.wait_ge(sem(loads[k // (nk // len(loads))]), 16)
                        m = mm(PS[banks[n % len(banks)]][0:rows, :], lhs[:, k, b * P:b * P + rows],
                               w[:, k, 512 * half:512 * half + 512], k == 0, k == nk - 1)
                    m.then_inc(sem("res_mm"), 1)

            project("x2", hT, wout_sb, KD, ["ld_wout0", "ld_wout1"], (0, 1, 2, 3))

            pe.wait_ge(sem("res_scaled"), RES["x2"][1] + TB)
            pe.wait_ge(sem("res_add"), RES["x2"][0] + 2 * TB)
            pe.wait_ge(sem("cs_ev"), 6)
            norm_transposes(xs3, TB, (6, 7), "x2n")
            pe.wait_ge(sem("rows_ev"), NORM["x2n"] + KD)
            pe.wait_ge(sem("ld_wmq"), 16)
            for b in range(TB):
                rows = P if b < 2 else DEC
                for k in range(KD):
                    m = mm(PS[b][0:rows, :], hT[:, k, b * P:b * P + rows], wmq_sb[:, k, :], k == 0, k == KD - 1)
                m.then_inc(sem("qm_mm"), 1)
            for b in range(TB):
                rows = P if b < 2 else DEC
                pe.wait_ge(sem("qm_ready"), b + 1)
                if b == 2:
                    pe.wait_ge(sem("qmT_ev"), 1)
                for h in range(H):
                    m = tr(PS[4 + b % 2][:, h * P:h * P + rows], qmraw[0:rows, h * P:(h + 1) * P])
                m.then_inc(sem("qmT_tr"), 1)
            pe.wait_ge(sem("qmT_ev"), TB)
            pe.wait_ge(sem("ld_vcache"), 16)
            attention("mem", mem_units)
            pe.wait_ge(sem("att_o"), 2 * ATT["mem"])
            project("x3", om, wmo_sb, 4, ["ld_wmo"], (0, 1, 2, 3))

            pe.wait_ge(sem("res_scaled"), RES["x3"][1] + TB)
            norm_transposes(xs3, TB, (6, 7), "x3n")
            pe.wait_ge(sem("rows_ev"), NORM["x3n"] + KD)
            pe.wait_ge(sem("res_add"), RES["x3"][0] + 2 * TB)
            pe.wait_ge(sem("ld_wr"), 16)
            for b in range(TB):
                rows = P if b < 2 else DEC
                for k in range(KD):
                    m = mm(PS[0][0:rows, b * E:(b + 1) * E], hT[:, k, b * P:b * P + rows], wr_sb[:, k, :], k == 0, k == KD - 1)
            m.then_inc(mark("lg_mm"), 1)
            pe.wait_ge(*at("mask_ready"))
            for b in range(TB):
                for a in range(b + 1):
                    m = mm(PS[1][:, b * E:(b + 1) * E], ustrict if a == b else ones, mask[:, a, :], a == 0, a == b)
            m.then_inc(mark("rank_mm"), 1)
            for b in range(TB):
                m = mm(PS[2][0:E, 0:1], mask[:, b, :], ones[:, 0:1], b == 0, b == TB - 1)
            m.then_inc(mark("cnt_mm"), 1)
            pe.wait_ge(*at("gate_ready"))
            for b in range(TB):
                m = tr(PS[3][0:E, b * P:(b + 1) * P], gate[:, b, :])
            m.then_inc(mark("gt_tr"), 1)
            pe.wait_ge(*at("gt_ev"))
            pe.wait_ge(sem("ld_bias"), 64)
            for n in range(2 * TB):
                b, half = n // 2, n % 2
                rows = P if b < 2 else DEC
                if n >= 4:
                    pe.wait_ge(sem("y0_add"), n - 3)
                mm(PS[4 + n % 4][0:rows, :], gateT[:, b * P:b * P + rows], bdn[:, 512 * half:512 * half + 512])\
                    .then_inc(sem("y0_mm"), 1)
            pe.wait_ge(*at("tot_ready"))
            mm(PS[2][0:E, 8:9], ustrict[0:E, 0:E], tot).then_inc(mark("start_mm"), 1)
            pe.wait_ge(*at("hot_ready"))
            for a in range(XTRA):
                mm(PS[3][0:1, 0:LIST], CO[0:E, C_EV:C_EV + 1], hot[:, a, :], a == 0, a == XTRA - 1)
            for a in range(XTRA):
                mm(PS[3][0:1, LIST:2 * LIST], CO[0:E, C_EV + 1 + a:C_EV + 2 + a], hot[:, a, :], a == 0, a == XTRA - 1)
            mm(PS[3][0:1, 2 * LIST:2 * LIST + 1], ones[0:E, 0:1], tot).then_inc(mark("list_mm"), 1)

            def gather(n):
                pe.wait_ge(sem("slots_ready"), n + 1)
                for k in range(KD):
                    for b in range(TB):
                        for s in range(3):
                            m = mm(PS[4][:, k * SLOTS:(k + 1) * SLOTS], xparts[:, b, s, k * P:(k + 1) * P],
                                   S[:, b, 0, :], b == 0 and s == 0, b == TB - 1 and s == 2)
                m.then_inc(sem("gather_mm"), 1)
                for b in range(TB):
                    m = pe.transpose(PS[5][:, 64 * b:64 * b + 64].bitcast(BF16), S[:, b, :, :].rearrange("p a s -> p (a s)"), identb)
                m.then_inc(sem("slots_tr"), 1)

            def gate_up(it):
                pe.wait_ge(sem("sel_ready"), it + 1)
                for g in range(2):
                    for half in range(2):
                        c = g * FF + half * 512
                        m = mm(PS[g][64 * half:64 * half + 64, :], sel, b3[:, c:c + 512], True, False)
                m.then_inc(sem("bias_mm"), 1)
                for k in range(KD):
                    pe.wait_ge(sem(f"ld_gu{k}"), it * 16 + 16)
                    for g in range(2):
                        for half in range(2):
                            c = g * FF + half * 512
                            m = mm(PS[g][64 * half:64 * half + 64, :], xgT[:, k, :], gu_sb[:, k, c:c + 512],
                                   False, k == KD - 1)
                    m.then_inc(sem("gu_used"), 1)

            def down(it):
                pe.wait_ge(sem("act_ready"), it + 1)
                for j in range(4):
                    m = tr(PS[2][:, j * P:(j + 1) * P], act_sb[:, j * P:(j + 1) * P])
                m.then_inc(sem("actT_tr"), 1)
                pe.wait_ge(sem("actT_ev"), it + 1)
                for n in range(KD // 2):
                    pe.wait_ge(sem(f"ld_dn{n}"), it * 16 + 16)
                    for k in (2 * n, 2 * n + 1):
                        for half in range(2):
                            m = mm(PS[3][64 * half:64 * half + 64, :], actT[:, k % 4, 64 * (k // 4):64 * (k // 4) + 64],
                                   dn_sb[:, k, 512 * half:512 * half + 512], k == 0, k == KD - 1)
                    m.then_inc(sem("dn_used"), 1)

            def scatter(it):
                pe.wait_ge(sem("y_ev"), it + 1)
                pe.wait_ge(sem("bd_ready"), it + 1)
                for j in range(NC):
                    pe.wait_ge(sem("acc_done"), it * NC + max(j, 1))
                    mm(PS[6 + j % 2][:, :], bd[:, j, :], y_sb).then_inc(sem("scat_mm"), 1)

            pe.wait_ge(sem("y0_add"), 2 * TB)
            pe.wait_ge(sem("parts_ready"), TB)
            pe.wait_ge(*at("b3_ready"))
            gather(0)
            with pe.Fori(0, E) as it:
                pe.wait_ge(sem("xg_ready"), it + 1)
                gate_up(it)
                gather(it + 1)
                down(it)
                scatter(it)
            pe.wait_ge(*at("list_ready"))
            n_extra = pe.value_load(xlist[0:1, 2 * LIST:2 * LIST + 1], min_val=0, max_val=LIST - 1)
            with pe.If(n_extra > 0):
                with pe.Fori(0, n_extra) as j:
                    gather(j + (E + 1))
                    pe.wait_ge(sem("xg_ready"), j + (E + 2))
                    gate_up(j + E)
                    down(j + E)
                    scatter(j + E)

        @block.vector
        def _(dve):
            steps = [0]

            def link(ins):
                steps[0] += 1
                ins.then_inc(sem("dve_step"), 1)
                dve.wait_ge(sem("dve_step"), steps[0])

            def tt(out, a, b, op):
                return dve.tensor_tensor(out, a, b, op)

            def ts(out, a, s1, s2=None, op0=ALU.mult, op1=None):
                if op1 is None:
                    return dve.tensor_scalar(out, a, s1, None, op0)
                return dve.tensor_scalar(out, a, s1, s2, op0, op1)

            roots = [0]

            def rooted(ins):
                roots[0] += 1
                ins.then_inc(sem("var_ready"), 1)
                dve.wait_ge(sem("root_ready"), roots[0])

            def rstd(dst, sums, n):
                rooted(ts(dst, sums, 1.0 / n, EPS, ALU.mult, ALU.add))

            def head_norm(x, sq, rows, heads, width, gain=None):
                s = st[0:rows, 0:heads]
                link(tt(sq, x, x, ALU.mult))
                link(dve.tensor_reduce(s, sq, AX, ALU.add))
                rstd(s, s, width)
                last = tt(x, x, bcast(s, [rows, heads, width], 2), ALU.mult)
                if gain is not None:
                    link(last)
                    last = tt(x, x, bcast(gain, [rows, heads, width], 1), ALU.mult)
                return last

            def rope(x, c, s, t):
                h = ROPE // 2
                x1, x2 = x[:, :, 0:h], x[:, :, h:ROPE]
                tt(t[0], x1, c, ALU.mult)
                tt(t[1], x2, s, ALU.mult)
                tt(t[2], x2, c, ALU.mult)
                link(tt(t[3], x1, s, ALU.mult))
                tt(x1, t[0], t[1], ALU.subtract)
                return tt(x2, t[2], t[3], ALU.add)

            dve.memset(x3[DEC:P, 2, :], 0.0).then_inc(sem("xpad"), 1)
            dve.memset(qk_ss, 1.0)
            dve.wait_ge(sem("mem_sq"), 2)
            rstd(st[:, 0:2], ssq[:, 3:5], D)
            for b in range(2):
                ts(mem3[:, b, :], mem3[:, b, :], st[:, b:b + 1]).then_inc(sem("mem_scaled"), 1)
            dve.wait_ge(sem("ld_gn"), 112)
            dve.wait_ge(sem("x_sq"), TB)
            rstd(ssq[:, 0:3], ssq[:, 0:3], D)
            for b in range(2):
                dve.wait_ge(sem("mk_ev"), b + 1)
                head_norm(mk_out[:, b, :].rearrange("p (h d) -> p h d", h=H),
                          HM[:, 2048:2560].rearrange("p (h d) -> p h d", h=H), P, H, HD, g_mk)\
                    .then_inc(sem("mk_ready"), 1)
                dve.wait_ge(sem("mk_ready"), b + 1)
            dve.wait_ge(sem("rows_tr"), NORM["mem"] + KD)
            dve.wait_ge(sem("km_tr"), 2)
            for b in range(TB):
                ts(xs3[:, b, :], x3[:, b, :], ssq[:, b:b + 1]).then_inc(sem("x_scaled"), 1)
            dve.wait_ge(sem("mv_mm"), 2)
            dve.wait_ge(sem("cols_ready"), 2)
            dve.memset(upad[:, :, 0:3], 0.0)
            dve.memset(cl[DEC:P, 2, :], 0.0)
            dve.tensor_copy(upad[:, :, 3 + SEQ:6 + SEQ], convw[:, :, 0:3]).then_inc(mark("upad_ready"), 1)
            dve.wait_ge(*at("upad_ready"))
            dve.wait_ge(sem("x_scaled"), TB)
            dve.memset(gstate[:, 0, :], 0.0).then_inc(mark("state0"), 1)
            for f in range(NU):
                dve.wait_ge(sem("u_ev"), f + 1)
                dve.tensor_copy(ulast[:, f, 0, :], upad[:, f, SEQ:SEQ + 3])
                dve.tensor_copy(ulast[:, f, 1, :], upad[:, f, T + 3:T + 6])
                if f:
                    dve.wait_ge(sem("silu_done"), f)
                link(ts(conv_tmp, upad[:, f, 0:323], convw[:, f, 3:4]))
                for j in range(1, CW):
                    m = dve.scalar_tensor_tensor(conv_tmp, upad[:, f, j:j + 323], convw[:, f, 3 + j:4 + j], conv_tmp,
                                                 ALU.mult, ALU.add)
                    if j < CW - 1:
                        link(m)
                m.then_inc(sem("conv_done"), 1)

            dve.wait_ge(*at("ab_tr"))
            dve.tensor_copy(gb, PS[7][0:CH, 0:8 * NC].rearrange("p (c n) -> p c n", c=NC)).then_inc(mark("gb_ready"), 1)
            dve.wait_ge(*at("gb_ready"))
            c20 = [CH, NC, H]

            def by_pair(a):
                return a.rearrange("p (c h) -> p c h", c=NC)

            link(tt(by_pair(t20a), gb[:, :, 0:H], bcast(g_dt, c20, 1), ALU.add))
            dve.scalar_tensor_tensor(t20b, t20a, -1.0, t20a, ALU.mult, ALU.max).then_inc(mark("sp_abs"), 1)
            dve.wait_ge(sem("sp_act"), 2)
            link(dve.scalar_tensor_tensor(gts, t20a, 0.0, t20b, ALU.max, ALU.add))
            link(tt(by_pair(gts), by_pair(gts), bcast(eal, c20, 1), ALU.mult))
            ts(gts, gts, -1.0).then_inc(mark("g_ready"), 1)
            dve.wait_ge(*at("g_ready"))
            full = [CH, NP_, CH]
            dve.wait_ge(sem("cl_mm"), 2 * TB)
            tt(g2, bcast(u64, full, 1), bcast(gts, full, 2), ALU.mult).then_inc(mark("g2_ready"), 1)
            dve.wait_ge(*at("gcum_mm"))
            dve.tensor_copy(gcum, PS[7][0:CH, 64:84]).then_inc(mark("gcum_ready"), 1)
            dve.wait_ge(*at("gcum_ready"))
            dve.wait_ge(*at("ebc_ready"))
            for n, w in enumerate((8, 8, 4)):
                src = PS[n][0:CH, 0:CH * w].rearrange("p (n i) -> p n i", i=CH)
                tt(kds[:, 8 * n:8 * n + w], src[:, :, CH - 1], gcum[:, 8 * n:8 * n + w], ALU.subtract)
                m = tt(decT[:, 8 * n:8 * n + w, :], src, bcast(gcum[:, 8 * n:8 * n + w], [CH, w, CH], 2), ALU.subtract)
            link(m)
            ts(decT, decT, 0.0, None, ALU.min).then_inc(mark("diff_ready"), 1)
            dve.tensor_copy(eglast, ebc[:, :, CH - 1])
            dve.wait_ge(sem("dec_exp"), 2)
            tt(decT, decT, bcast(u64, full, 1), ALU.mult).then_inc(mark("dec_ready"), 1)
            dve.wait_ge(*at("sum_mm"))
            ts(qk_ss[:, 0:16], PS[7][:, 96:112], EPS, None, ALU.add)
            rooted(ts(qk_ss[0:DEC, 16:24], PS[7][0:DEC, 112:120], EPS, None, ALU.add))
            for f in range(2 * H):
                dve.wait_ge(sem("ss_mm"), f + 1)
                for src, c0, n in pieces(f):
                    m = dve.scalar_tensor_tensor(qkn[:, f, c0:c0 + n], PS[3 + f % 4][:, c0:c0 + n],
                                                 HD ** -0.5 if f < H else 1.0, src, ALU.mult, ALU.mult)
                m.then_inc(sem("qkn_ready"), 1)
                dve.wait_ge(sem("qkn_ready"), f + 1)
            dve.wait_ge(*at("dec_ready"))
            dve.wait_ge(*at("beta_ready"))
            dve.wait_ge(sem("ss_mm"), 2 * H)
            four = [CH, H, CH]
            for c in range(NC):
                cs = slice(4 * c, 4 * c + 4)
                dve.wait_ge(sem("kq_mm"), c + 1)
                src = PS[c % 3][0:CH, :].rearrange("p (h a i) -> p h a i", h=H, a=2)
                tt(KQ[:, cs, :], src[:, :, 0, :], decT[:, cs, :], ALU.mult)
                tt(MT[:, cs, :], src[:, :, 1, :], decT[:, cs, :], ALU.mult).then_inc(sem("kq_ev"), 1)
                dve.wait_ge(sem("kq_ev"), c + 1)
                link(tt(MT[:, cs, :], MT[:, cs, :], bcast(beta[:, cs], four, 2), ALU.mult))
                link(tt(cmask[:, cs, :], MT[:, cs, :], bcast(lvl_masks[:, 0, :], four, 1), ALU.mult))
                tt(TT2[:, cs, 1, :], bcast(ident[0:CH, 0:CH], four, 1), cmask[:, cs, :], ALU.subtract)\
                    .then_inc(sem("tt0"), 1)
            dve.wait_ge(sem("tt0"), NC)

            def level_mask(l):
                tt(cmasks[l % 2], MT, bcast(lvl_masks[:, l, :], full, 1), ALU.mult).then_inc(sem("cm_ready"), 1)

            level_mask(1)
            dve.wait_ge(sem("kq_mm"), NC)
            q4 = qkn[:, 0:H, :].rearrange("p h (c i) -> p h c i", c=NC)
            e4 = ebc.rearrange("p (c h) i -> p h c i", c=NC)
            for h in range(H):
                m = tt(q4[:, h], q4[:, h], e4[:, h], ALU.mult)
            m.then_inc(mark("qg_ready"), 1)
            for l in range(1, len(LEVELS)):
                if l + 1 < len(LEVELS):
                    if l > 1:
                        dve.wait_ge(sem("p_mm"), NC * (l - 1))
                    level_mask(l + 1)
                for c in range(NC):
                    dve.wait_ge(sem("q_mm"), NC * (l - 1) + c + 1)
                    if c == 0 and l == 1:
                        dve.wait_ge(sem("t0_ev"), NC)
                    elif c == 0:
                        dve.wait_ge(sem("tt_ev"), NC * (l - 1))
                    t = TT2[:, 4 * c:4 * c + 4, :, :].rearrange("p n a i -> p (n a i)")
                    tt(t, t, PS[3 + c][0:CH, :], ALU.subtract).then_inc(sem("tt_ev"), 1)
            dve.wait_ge(sem("p_mm"), NC * (len(LEVELS) - 1))
            dve.wait_ge(sem("kv_ev"), 2 * NC)
            dve.wait_ge(*at("egc_ready"))
            for c in range(NC):
                k4 = ktok[:, c, :].rearrange("p (h d) -> p h d", h=H)
                m = tt(kneg[:, c, :].rearrange("p (h d) -> p h d", h=H), k4,
                       bcast(egc[:, 4 * c:4 * c + 4], [CH, H, HD], 2), ALU.mult)
            link(m)
            ts(kneg, kneg, -1.0).then_inc(mark("kneg_ready"), 1)
            for c in range(NC):
                k4 = ktok[:, c, :].rearrange("p (h d) -> p h d", h=H)
                m = tt(k4, k4, bcast(kds[:, 4 * c:4 * c + 4], [CH, H, HD], 2), ALU.mult)
            m.then_inc(mark("kd_ready"), 1)
            for c in range(NC):
                s = 0 if c < 4 else 1
                ps = slice(4 * c, 4 * c + 4)
                dve.wait_ge(sem("vn_mm"), c + 1)
                if c:
                    dve.wait_ge(sem("o_mm"), c)
                tt(vnew.rearrange("p (h d) -> p h d", h=H), PS[3][0:CH, :].rearrange("p (h d) -> p h d", h=H),
                   bcast(beta[:, ps], [CH, H, HD], 2), ALU.mult).then_inc(sem("vn_ready"), 1)
                dve.wait_ge(sem("ds_mm"), c + 1)
                dve.wait_ge(sem("o_mm"), c + 1)
                if s:
                    dve.wait_ge(sem("ld_state"), 16)
                g4 = gstate[:, s, :].rearrange("p (h d) -> p h d", h=H)
                if c:
                    dve.wait_ge(sem("state_new"), c)
                link(tt(g4, g4, bcast(eglast[:, ps], [P, H, HD], 2), ALU.mult))
                tt(gstate[:, s, :], gstate[:, s, :], PS[5][:, :], ALU.add).then_inc(sem("state_new"), 1)
                dve.wait_ge(sem("o_copy"), c + 1)
                if c == 0:
                    dve.wait_ge(sem("w_mm"), NC)
                head_norm(otok.rearrange("p (h d) -> p h d", h=H), W[0:CH, 0:512].rearrange("p (h d) -> p h d", h=H),
                          CH, H, HD).then_inc(sem("o_norm"), 1)
                dve.wait_ge(sem("o_tr"), c + 1)
                dve.scalar_tensor_tensor(hT[:, 0:H, c * CH:(c + 1) * CH],
                                         PS[6][:, 0:256].rearrange("p (h t) -> p h t", h=H), c_gdn,
                                         ztile[:, :, c * CH:(c + 1) * CH], ALU.mult, ALU.mult)\
                    .then_inc(sem("gdn_mix"), 1)

            dve.wait_ge(sem("cl_ev"), 2 * TB)
            sq = XS[:, 0:1152].rearrange("p (b n) -> p b n", b=TB)
            head_norm(cl[:, :, 0:384], sq, P, TB, Q_RANK).then_inc(mark("cq_ready"), 1)
            dve.wait_ge(*at("cq_ready"))
            head_norm(cl[:, :, 384:640], sq[:, :, 0:256], P, TB, KV_RANK, g_kva).then_inc(mark("lat_ready"), 1)
            dve.wait_ge(*at("lat_ready"))
            link(head_norm(cl[:, :, 640:704], sq[:, :, 0:64], P, TB, ROPE, g_kr))

            def temps(rows, n):
                return [XS[0:rows, 1152 + 128 * i:1152 + 128 * i + 32 * n].rearrange("p (n f) -> p n f", n=n)
                        for i in range(4)]

            rope(cl[:, :, 640:704], cos, sin, temps(P, TB)).then_inc(mark("kpe_ready"), 1)
            dve.wait_ge(*at("kpe_ready"))
            for b in range(TB):
                rows = P if b < 2 else DEC
                dve.wait_ge(sem("q_ev"), b + 1)
                q4 = qraw[0:rows, :].rearrange("p (h n) -> p h n", h=H)
                link(head_norm(q4, XS[0:rows, 0:768].rearrange("p (h n) -> p h n", h=H), rows, H, QK, g_q[0:rows, :]))
                tab = [bcast(t[0:rows, b, :], [rows, H, 32], 1) for t in (cos, sin)]
                rope(q4[:, :, P:QK], tab[0], tab[1], temps(rows, H)).then_inc(sem("q_ready"), 1)
                dve.wait_ge(sem("q_ready"), b + 1)
            for kb in range(5):
                rows = P if kb < 4 else DEC
                dve.wait_ge(sem("k_raw"), kb + 1)
                head_norm(kraw[0:rows, :].rearrange("p (h n) -> p h n", h=H),
                          XS[0:rows, 0:512].rearrange("p (h n) -> p h n", h=H), rows, H, HD).then_inc(sem("k_norm"), 1)
                dve.wait_ge(sem("k_norm"), kb + 1)

            def attention(tag, units, scale):
                for n in range(len(units) + 2):
                    if n < len(units):
                        rows, terms, nkeys, masked, vs, out = units[n]
                        dve.wait_ge(sem("att_s"), ATT[tag] + n + 1)
                        if n >= 2:
                            dve.wait_ge(sem("att_ex"), ATT[tag] + n - 1)
                        sc = PS[n % 2][0:rows, 0:nkeys]
                        if masked:
                            link(tt(sc[:, nkeys - P:nkeys], sc[:, nkeys - P:nkeys], amask, ALU.add))
                        a = amx[0:rows, n % 2:n % 2 + 1]
                        link(dve.tensor_reduce(a, sc, AX, ALU.max))
                        ts(a, a, -scale).then_inc(sem("att_mx"), 1)
                    if 1 <= n <= len(units):
                        rows, terms, nkeys, masked, vs, out = units[n - 1]
                        u = (n - 1) % 2
                        dve.wait_ge(sem("att_ex"), ATT[tag] + n)
                        link(dve.reciprocal(arec[0:rows, u:u + 1], asum[0:rows, u:u + 1]))
                        p = prob[0:rows, u, 0:nkeys]
                        ts(p, p, arec[0:rows, u:u + 1]).then_inc(sem("att_nm"), 1)
                    if n >= 2:
                        rows, terms, nkeys, masked, vs, out = units[n - 2]
                        dve.wait_ge(sem("att_pv"), ATT[tag] + n - 1)
                        dve.tensor_copy(out, PS[4 + n % 2][:, 0:rows]).then_inc(sem("att_o"), 1)

            attention("mla", mla_units, QK ** -0.5)

            dve.memset(x3[DEC:P, 2, :], 0.0).then_inc(sem("xpad"), 1)

            def add_rows(tag, banks):
                for n in range(2 * TB):
                    b, half = n // 2, n % 2
                    rows = P if b < 2 else DEC
                    dve.wait_ge(sem("res_mm"), RES[tag][0] + n + 1)
                    xx = x3[0:rows, b, 512 * half:512 * half + 512]
                    tt(xx, xx, PS[banks[n % len(banks)]][0:rows, :], ALU.add).then_inc(sem("res_add"), 1)

            def scale_rows(tag, col):
                for b in range(TB):
                    dve.wait_ge(sem("res_sq"), RES[tag][1] + b + 1)
                rstd(ssq[:, col:col + 3], ssq[:, col:col + 3], D)
                for b in range(TB):
                    ts(xs3[:, b, :], x3[:, b, :], ssq[:, col + b:col + b + 1]).then_inc(sem("res_scaled"), 1)

            dve.wait_ge(sem("ld_x2"), 32)
            add_rows("x2", (0, 1, 2, 3))

            scale_rows("x2", 5)
            for b in range(TB):
                rows = P if b < 2 else DEC
                dve.wait_ge(sem("qm_ev"), b + 1)
                head_norm(qmraw[0:rows, :].rearrange("p (h n) -> p h n", h=H),
                          XS[0:rows, 0:512].rearrange("p (h n) -> p h n", h=H), rows, H, HD).then_inc(sem("qm_ready"), 1)
                dve.wait_ge(sem("qm_ready"), b + 1)
            attention("mem", mem_units, HD ** -0.5)
            dve.wait_ge(sem("ld_bias"), 64)
            link(dve.tensor_copy(bhi, braw))
            link(tt(braw, braw, bhi, ALU.subtract))
            link(dve.tensor_copy(bmid, braw))
            link(tt(braw, braw, bmid, ALU.subtract))
            dve.tensor_copy(b3[0:32, :], bhi[0:32, :])
            dve.tensor_copy(b3[32:64, :], bmid[32:64, :])
            dve.tensor_copy(b3[64:96, :], braw[64:96, :]).then_inc(mark("b3_ready"), 1)
            add_rows("x3", (0, 1, 2, 3))

            scale_rows("x3", 8)
            dve.memset(gate, 0.0)
            dve.memset(mask, 0.0)
            dve.memset(rpos, -1.0)
            dve.memset(KV[0:96, 908:925], 0.0)
            dve.memset(lg[:, :, E:E + 4], BIG)
            dve.memset(rep8[:, :, 4:8], BIG)
            dve.memset(bd, 0.0)
            dve.tensor_copy(identb, ident)
            link(dve.memset(xlist, 0))
            dve.tensor_copy(id3[:, 0:E], CO[0:96, C_E3:C_E3 + E])
            dve.wait_ge(*at("lg_mm"))
            for b in range(TB):
                rows = P if b < 2 else DEC
                link(tt(lg[0:rows, b, 0:E], PS[0][0:rows, b * E:(b + 1) * E], g_router[0:rows, :], ALU.add))
                link(dve.max(top8[0:rows, b, :], lg[0:rows, b, 0:E]))
                dve.tensor_copy(rep8[0:rows, b, 0:TOPK], top8[0:rows, b, 0:TOPK])
                m = ts(ntop[0:rows, b:b + 1], top8[0:rows, b, 0:1], -1.0)
                link(m)
                link(dve.match_replace(mrep[0:rows, b, :], rep8[0:rows, b, :], lg[0:rows, b, :], NEG))
                link(tt(mask[0:rows, b, :], mrep[0:rows, b, 0:E], lg[0:rows, b, 0:E], ALU.not_equal))
            dve.memset(KV[:, 1206:1207], 0.0).then_inc(mark("mask_ready"), 1)
            dve.memset(KV[:, 1207:1208], 0.0).then_inc(mark("top_ready"), 1)
            dve.wait_ge(sem("gate_exp"), TB)
            link(tt(gate, gate, mask, ALU.mult))
            for b in range(TB):
                rows = P if b < 2 else DEC
                link(dve.tensor_reduce(gsum[0:rows, b:b + 1], gate[0:rows, b, :], AX, ALU.add))
                link(dve.reciprocal(gsum[0:rows, b:b + 1], gsum[0:rows, b:b + 1]))
                link(ts(gate[0:rows, b, :], gate[0:rows, b, :], gsum[0:rows, b:b + 1]))
            dve.memset(KV[:, 1208:1209], 0.0).then_inc(mark("gate_ready"), 1)
            dve.wait_ge(*at("rank_mm"))
            r = rpos[:, :, 0:E]
            link(dve.scalar_tensor_tensor(r, PS[1][:, 0:96].rearrange("p (b e) -> p b e", b=TB), 1.0, mask,
                                          ALU.add, ALU.mult))
            link(ts(r, r, 1.0, None, ALU.subtract))
            dve.wait_ge(*at("cnt_mm"))
            link(dve.tensor_copy(cnt, PS[2][0:E, 0:1]))
            link(ts(flags, CO[0:E, C_TH:C_TH + XTRA], cnt, None, ALU.is_lt))
            dve.tensor_reduce(tot, flags, AX, ALU.add).then_inc(mark("tot_ready"), 1)
            for n in range(2 * TB):
                b, half = n // 2, n % 2
                rows = P if b < 2 else DEC
                dve.wait_ge(sem("y0_mm"), n + 1)
                xx = x3[0:rows, b, 512 * half:512 * half + 512]
                tt(xx, xx, PS[4 + n % 4][0:rows, :], ALU.add).then_inc(sem("y0_add"), 1)
            dve.wait_ge(*at("start_mm"))
            link(dve.tensor_copy(start, PS[2][0:E, 8:9]))
            link(ts(pos4, CO[0:E, C_EV + 1:C_EV + 1 + XTRA], start, -1.0, ALU.add, ALU.add))
            sh = [E, XTRA, LIST]
            link(tt(hot, bcast(iota[0:E, 0:LIST], sh, 1), bcast(pos4, sh, 2), ALU.is_equal))
            tt(hot, hot, bcast(flags, sh, 2), ALU.mult).then_inc(mark("hot_ready"), 1)
            for b in range(TB):
                dve.wait_ge(sem("part0"), b + 1)
                if b == 0:
                    dve.wait_ge(sem("rows_tr"), NORM["x3n"] + KD)
                link(tt(xs3[:, b, :], xs3[:, b, :], xparts[:, b, 0, :], ALU.subtract))
                link(dve.tensor_copy(xparts[:, b, 1, :], xs3[:, b, :]))
                tt(xparts[:, b, 2, :], xs3[:, b, :], xparts[:, b, 1, :], ALU.subtract).then_inc(sem("parts_ready"), 1)
            dve.wait_ge(*at("list_mm"))
            dve.tensor_copy(xlist[0:1, 0:2 * LIST + 1], PS[3][0:1, 0:2 * LIST + 1]).then_inc(mark("list_ready"), 1)
            dve.wait_ge(sem("ld_yacc"), 16 * 4 * NC)
            dve.memset(KV[:, 1209:1210], 0.0).then_inc(sem("acc_done"), 1)

            def slots(e, first):
                sh = [P, TB, 2, SLOTS]
                rank = rpos[:, :, bass.ds(e, 1)]
                io = iota[:, 0:SLOTS] if first is None else iota[:, bass.ds(first, SLOTS)]
                tt(S, bcast(io, sh, 1, 1), bcast(rank, sh, 3), ALU.is_equal).then_inc(sem("slots_ready"), 1)

            def select(e):
                dve.tensor_copy(sel, id3[:, bass.ds(e, 1)].broadcast_to([96, SLOTS])).then_inc(sem("sel_ready"), 1)

            def rows_in(g):
                dve.wait_ge(sem("gather_mm"), g + 1)
                tt(xgT, PS[4][:, :].rearrange("p (k t) -> p k t", k=KD), bcast(c_ffn, [P, KD, SLOTS], 2), ALU.mult)\
                    .then_inc(sem("xg_ready"), 1)

            def rows_back(it, g):
                dve.wait_ge(sem("slots_tr"), g + 1)
                src = PS[5][:, 0:TB * 64].bitcast(BF16)[:, 0:T].rearrange("p (j t) -> p j t", j=NC)
                dve.tensor_copy(bd[0:64, :, 0:64], src[0:64])
                dve.tensor_copy(bd[64:128, :, 64:128], src[64:128]).then_inc(sem("bd_ready"), 1)

            def activations(it):
                dve.wait_ge(sem("gu_used"), it * KD + KD)
                ts(gt_sb, PS[0][:, :], LIMIT, None, ALU.min).then_inc(sem("gt_ready"), 1)
                ts(up_sb, PS[1][:, :], LIMIT, -LIMIT, ALU.min, ALU.max)
                dve.wait_ge(sem("sig_ready"), it + 1)
                tt(sig_sb, gt_sb, sig_sb, ALU.mult).then_inc(sem("glu_step"), 1)
                dve.wait_ge(sem("glu_step"), it + 1)
                dve.scalar_tensor_tensor(act_sb, up_sb, 1.0, sig_sb, ALU.add, ALU.mult).then_inc(sem("act_ready"), 1)

            def accumulate(it, e):
                dve.tensor_copy(gcur, gated[:, :, bass.ds(e, 1)].rearrange("p j a -> p (j a)")).then_inc(sem("gcur_ready"), 1)
                dve.wait_ge(sem("gcur_ready"), it + 1)
                for j in range(NC):
                    dve.wait_ge(sem("scat_mm"), it * NC + (j + 1))
                    dve.scalar_tensor_tensor(yacc[:, j, :], PS[6 + j % 2][:, :], gcur[:, j:j + 1], yacc[:, j, :],
                                             ALU.mult, ALU.add).then_inc(sem("acc_done"), 1)

            dve.wait_ge(*at("b3_ready"))
            slots(0, None)
            select(0)
            rows_in(0)
            with dve.Fori(0, E) as it:
                rows_back(it, it)
                slots(it + 1, None)
                activations(it)
                select(it + 1)
                rows_in(it + 1)
                accumulate(it, it)
                dve.wait_ge(sem("acc_done"), it * NC + (NC + 1))
            n_extra = dve.value_load(xlist[0:1, 2 * LIST:2 * LIST + 1], min_val=0, max_val=LIST - 1)
            with dve.If(n_extra > 0):
                with dve.Fori(0, n_extra) as j:
                    e = dve.value_load(xlist[0:1, bass.ds(j, 1)], min_val=0, max_val=E - 1)
                    part = dve.value_load(xlist[0:1, bass.ds(j + LIST, 1)], min_val=1, max_val=XTRA)
                    dve.wait_ge(sem("slots_tr"), j + (E + 1))
                    slots(e, part * SLOTS)
                    dve.wait_ge(sem("bias_mm"), j + E)
                    select(e)
                    rows_in(j + (E + 1))
                    rows_back(j + E, j + (E + 1))
                    activations(j + E)
                    accumulate(j + E, e)
                    dve.wait_ge(sem("acc_done"), j * NC + (E * NC + NC + 1))
            dve.memset(KV[:, 1210:1211], 0.0).then_inc(mark("y_final"), 1)


_INS = ['x_prompt', 'x_sample', 'cache_kv_latent', 'cache_k_rope', 'state_gdn', 'state_conv', 'cache_mem_k',
        'cache_mem_v', 'mem_prompt', 'norm_mix', 'w_in', 'conv_w', 'a_log', 'dt_bias', 'gdn_norm', 'q_a_norm',
        'w_qb', 'kv_a_norm', 'w_kvb', 'q_norm', 'k_nope_norm', 'k_rope_norm', 'w_out', 'norm_mem', 'mem_norm',
        'w_mq', 'w_mk', 'w_mv', 'mq_norm', 'mk_norm', 'w_mo', 'norm_ffn', 'w_router', 'b_router', 'w_gu', 'b_gu',
        'w_down', 'b_down']
_OUTS = [(1, SEQ, D), (1, DEC, D), (1, 1, SEQ, KV_RANK), (1, 1, SEQ, ROPE), (1, 1, H, HD, HD), (1, 1, 3, CONV_DIM),
         (1, 1, NMEM, H, HD), (1, 1, NMEM, H, HD), (1, 1, DEC, KV_RANK), (1, 1, DEC, ROPE), (1, 1, H, HD, HD),
         (1, 1, 3, CONV_DIM)]


def kernel(**inputs):
    import concourse.bacc as bacc
    from concourse.bass_utils import run_bass_kernel_spmd

    nc = bacc.Bacc("TRN2", target_bir_lowering=False, num_devices=1)
    arrays, args = {}, []
    for name in _INS:
        a = np.ascontiguousarray(inputs[name])
        arrays[f"in_{name}"] = a
        args.append(nc.dram_tensor(f"in_{name}", a.shape, F32, kind="ExternalInput").ap())
    arrays["in_consts"] = constants()
    args.append(nc.dram_tensor("in_consts", (P, C_N), F32, kind="ExternalInput").ap())
    for i, shape in enumerate(_OUTS):
        args.append(nc.dram_tensor(f"out_{i}", shape, F32, kind="ExternalOutput").ap())
    trunk_kernel(nc, *args)
    r = run_bass_kernel_spmd(nc, [arrays], core_ids=[0])
    return tuple(r.results[0][f"out_{i}"] for i in range(len(_OUTS)))
```

```python
from contextlib import ExitStack

import numpy as np
import concourse.bass as bass
from concourse import mybir

F32 = mybir.dt.float32
BF16 = mybir.dt.bfloat16
I32 = mybir.dt.int32
ALU = mybir.AluOpType
ACT = mybir.ActivationFunctionType
AX = mybir.AxisListType.X

P = 128
D = 1024
KD = D // P
SEQ, DEC, PAST = 256, 64, 256
T = SEQ + DEC
TB = (T + P - 1) // P
CH = 64
NC = T // CH
CONV_DIM, CW = 1536, 4
NU, NZ = CONV_DIM // P, 4
H, HD = 4, 128
Q_RANK, KV_RANK, ROPE = 384, 256, 64
QK = HD + ROPE
IN_W = 2760
AB0 = (NU + NZ) * P
CL0 = AB0 + 2 * H
CLW = Q_RANK + KV_RANK + ROPE
NKEY = SEQ + PAST + DEC
NMEM = 256
E, TOPK, FF = 32, 4, 1024
SLOTS = 64
EPS = 1e-6
ALPHA, LIMIT = 1.702, 7.0
NEG = -1e30
BIG = 3e38
XTRA = T // SLOTS - 1
LIST = 32
LEVELS = (1, 2, 4, 8, 16, 32)

C_ID, C_ONE, C_US, C_U, C_LV, C_IO, C_COS, C_SIN, C_AM, C_E3, C_TH, C_EV, C_MH = (
    0, 128, 256, 384, 448, 832, 1152, 1248, 1344, 1472, 1504, 1508, 1513)
C_N = 1520


def constants():
    c = np.zeros((P, C_N), np.float32)
    i = np.arange(P)
    c[:, C_ID:C_ID + P] = np.eye(P)
    c[:, C_ONE:C_ONE + P] = 1.0
    c[:, C_US:C_US + P] = i[:, None] < i[None, :]
    j = np.arange(CH)
    c[:CH, C_U:C_U + CH] = j[:, None] <= j[None, :]
    for n, s in enumerate(LEVELS):
        pair = (j[:, None] // (2 * s)) == (j[None, :] // (2 * s))
        c[:CH, C_LV + CH * n:C_LV + CH * (n + 1)] = pair & (j[:, None] % (2 * s) < s) & (j[None, :] % (2 * s) >= s)
    c[:, C_IO:C_IO + T] = np.arange(T)[None, :]
    half = ROPE // 2
    inv = (np.float32(10000.0) ** (-np.arange(half, dtype=np.float32) / half)).astype(np.float32)
    pos = np.arange(TB * P, dtype=np.float32)
    ang = (pos[:, None] * inv[None, :]).astype(np.float32).reshape(TB, P, half).transpose(1, 0, 2)
    c[:, C_COS:C_COS + TB * half] = np.cos(ang).reshape(P, -1)
    c[:, C_SIN:C_SIN + TB * half] = np.sin(ang).reshape(P, -1)
    c[:CH, C_AM + CH:C_AM + P] = NEG
    c[:96, C_E3:C_E3 + E] = (i[:96, None] % E) == np.arange(E)[None, :]
    c[:, C_TH:C_TH + XTRA] = SLOTS * (1 + np.arange(XTRA))[None, :]
    c[:, C_EV] = i
    c[:, C_MH] = -0.5
    c[:, C_EV + 1:C_EV + 1 + XTRA] = (1 + np.arange(XTRA))[None, :]
    return c


def trunk_kernel(nc, x_prompt, x_sample, cache_kv_latent, cache_k_rope, state_gdn, state_conv, cache_mem_k,
                 cache_mem_v, mem_prompt, norm_mix, w_in, conv_w, a_log, dt_bias, gdn_norm, q_a_norm, w_qb,
                 kv_a_norm, w_kvb, q_norm, k_nope_norm, k_rope_norm, w_out, norm_mem, mem_norm, w_mq, w_mk,
                 w_mv, mq_norm, mk_norm, w_mo, norm_ffn, w_router, b_router, w_gu, b_gu, w_down, b_down,
                 consts, yp, ys, p_lat, p_kpe, p_s, p_conv, p_mk, p_mv, s_lat, s_kpe, s_s, s_conv):
    ctx = ExitStack()
    with ctx:
        def sb(name, cols, dt=F32, parts=P):
            return ctx.enter_context(nc.sbuf_tensor(name, [parts, cols], dt))

        sems = {}

        def sem(name):
            if name not in sems:
                sems[name] = ctx.enter_context(nc.semaphore(name))
            return sems[name]

        ONCE = {
            "tensor": ["ab_tr", "gcum_mm", "gbc_mm", "sum_mm", "lg_mm", "rank_mm", "cnt_mm", "gt_tr", "start_mm",
                       "list_mm"],
            "scalar": ["beta_ready", "egc_ready", "ebc_ready", "kpe_ev", "gt_ev"],
            "vector": ["upad_ready", "state0", "gb_ready", "sp_abs", "g_ready", "g2_ready", "gcum_ready",
                       "diff_ready", "dec_ready", "qg_ready", "cq_ready", "lat_ready", "kpe_ready", "kneg_ready",
                       "kd_ready", "b3_ready", "mask_ready", "top_ready", "tot_ready", "gate_ready", "hot_ready",
                       "list_ready", "y_final"],
        }

        def mark(name):
            return sem(next(engine for engine in ONCE if name in ONCE[engine]) + "_events")

        def at(name):
            engine = next(engine for engine in ONCE if name in ONCE[engine])
            return sem(engine + "_events"), ONCE[engine].index(name) + 1

        NORM = {"mem": 0, "x": KD, "x2n": 2 * KD, "x3n": 3 * KD}
        ATT = {"mla": 0, "mem": H * TB}
        RES = {"x2": (0, 0), "x3": (2 * TB, TB)}

        W = sb("weights", 24576)
        V = sb("stream", 8192)
        R = sb("small_weights", 4352)
        X = sb("x", TB * D)
        XS = sb("scaled", TB * D)
        HM = sb("hT", KD * T)
        KV = sb("mem_kv", 4096)
        CO = sb("const", C_N)
        GN = sb("gain_rows", 768)
        GC = sb("gain_cols", 64)
        SM = sb("stats", 480)
        PS = [ctx.enter_context(nc.psum_tensor(f"bank{i}", [P, 512], F32)) for i in range(8)]

        ident = CO[:, C_ID:C_ID + P]
        ones = CO[:, C_ONE:C_ONE + P]
        ustrict = CO[:, C_US:C_US + P]
        u64 = CO[0:CH, C_U:C_U + CH]
        iota = CO[:, C_IO:C_IO + T]
        cos = CO[:, C_COS:C_COS + 96].rearrange("p (b f) -> p b f", b=TB)
        sin = CO[:, C_SIN:C_SIN + 96].rearrange("p (b f) -> p b f", b=TB)
        minus_half = CO[:, C_MH:C_MH + 1]
        amask = CO[:, C_AM:C_AM + P]
        g_kva, g_q, g_kr, g_mk = GN[:, 0:256], GN[:, 256:448], GN[:, 448:512], GN[:, 512:640]
        g_router = GN[:, 640:672]
        g_dt, g_alog = GN[0:CH, 672:676], GN[0:CH, 676:680]
        c_mix, c_mem, c_memn, c_ffn = GC[:, 0:8], GC[:, 8:16], GC[:, 16:24], GC[:, 24:32]
        c_qa, c_kn, c_gdn, c_mq = GC[:, 32:35], GC[:, 35:36], GC[:, 36:37], GC[:, 37:38]

        w_in_sb = W[:, 0:KD * IN_W].rearrange("p (k n) -> p k n", k=KD)
        mk_out = W[:, 22080:23104].rearrange("p (b n) -> p b n", b=2)
        mk_tmp = W[:, 23104:24128].rearrange("p (b n) -> p b n", b=2)
        g_rows = KV[0:38, 3584:3712]
        wmk_sb = V[:, 0:4096].rearrange("p (k n) -> p k n", k=KD)
        wmv_sb = V[:, 4096:8192].rearrange("p (k n) -> p k n", k=KD)
        UW = SEQ + DEC + 2 * (CW - 1)
        upad = V[:, 0:NU * UW].rearrange("p (f t) -> p f t", f=NU)
        ztile = V[:, 3912:3912 + NZ * T].rearrange("p (h t) -> p h t", h=NZ)
        cl = V[:, 5192:5192 + TB * CLW].rearrange("p (b n) -> p b n", b=TB)
        abT = V[0:2 * H, 7304:7304 + T]
        conv_tmp = V[:, 7624:7624 + 323]
        wout_sb = V[:, 0:8192].rearrange("p (k n) -> p k n", k=KD)
        wqb_sb = R[:, 0:2304].rearrange("p (k n) -> p k n", k=3)
        wkvb_sb = R[:, 2304:4352].rearrange("p (k n) -> p k n", k=2)
        x3 = X[:, :].rearrange("p (b d) -> p b d", b=TB)
        xs3 = XS[:, :].rearrange("p (b d) -> p b d", b=TB)
        mem3 = XS[:, 0:2048].rearrange("p (b d) -> p b d", b=2)
        kcache = XS[:, 2048:3072].rearrange("p (b n) -> p b n", b=2)
        hT = HM[:, :].rearrange("p (k t) -> p k t", k=KD)
        mT = HM[:, 0:KD * NMEM].rearrange("p (k t) -> p k t", k=KD)
        conv7 = KV[0:7, 2048:2048 + CONV_DIM]
        km_p = KV[:, 0:1024].rearrange("p (h t) -> p h t", h=H)
        vm_p = KV[:, 1024:2048].rearrange("p (b n) -> p b n", b=2)
        km_s = KV[:, 2048:3072].rearrange("p (h t) -> p h t", h=H)
        vm_s = KV[:, 3072:4096].rearrange("p (b n) -> p b n", b=2)
        convw = SM[:, 0:84].rearrange("p (f j) -> p f j", f=NU)
        ulast = SM[:, 84:156].rearrange("p (f s j) -> p f s j", f=NU, s=2)
        lvl_masks = CO[0:CH, C_LV:C_LV + CH * len(LEVELS)].rearrange("p (l i) -> p l i", l=len(LEVELS))

        NP_ = NC * H
        sq8 = W[:, 0:2560].rearrange("p (f t) -> p f t", f=8)
        kneg = W[0:CH, 0:2560].rearrange("p (c n) -> p c n", c=NC)
        qkn = W[:, 2560:5120].rearrange("p (f t) -> p f t", f=8)
        ktok = W[0:CH, 5120:7680].rearrange("p (c n) -> p c n", c=NC)
        vtok = XS[0:CH, 0:2560].rearrange("p (c n) -> p c n", c=NC)
        MT = W[0:CH, 7680:8960].rearrange("p (n i) -> p n i", n=NP_)
        KQ = W[0:CH, 8960:10240].rearrange("p (n i) -> p n i", n=NP_)
        TT2 = W[0:CH, 10240:12800].rearrange("p (n a i) -> p n a i", n=NP_, a=2)
        ebc = W[:, 12800:14080].rearrange("p (n i) -> p n i", n=NP_)
        pinv = W[0:CH, 12800:14080].rearrange("p (n i) -> p n i", n=NP_)
        decT = W[0:CH, 14080:15360].rearrange("p (n i) -> p n i", n=NP_)
        wT = W[:, 14080:15360].rearrange("p (n i) -> p n i", n=NP_)
        g2 = W[0:CH, 0:1280].rearrange("p (n i) -> p n i", n=NP_)
        cmask = W[0:CH, 0:1280].rearrange("p (n i) -> p n i", n=NP_)
        cqT = W[:, 15360:16320].rearrange("p (k t) -> p k t", k=3)
        latT = HM[:, 1280:2432].rearrange("p (k t) -> p k t", k=2)
        kT = W[:, 16384:18688].rearrange("p (h t) -> p h t", h=H)
        vk = W[:, 18688:21248].rearrange("p (b n) -> p b n", b=5)
        qTn = W[:, 21248:22528].rearrange("p (h t) -> p h t", h=H)
        qTr = W[0:ROPE, 22528:23808].rearrange("p (h t) -> p h t", h=H)
        kpeT = W[0:ROPE, 23808:24384]
        gstate = X[:, 0:1024].rearrange("p (s n) -> p s n", s=2)
        qraw = X[:, 1024:1792]
        lat_past = X[:, 1792:2304].rearrange("p (b n) -> p b n", b=2)
        kpe_past = X[:, 2304:2432].rearrange("p (b n) -> p b n", b=2)
        otok = X[0:CH, 2432:2944]
        vnew = XS[0:CH, 2560:3072]
        gb = SM[0:CH, 160:200].rearrange("p (c n) -> p c n", c=NC)
        gts = SM[0:CH, 200:220]
        beta = SM[0:CH, 220:240]
        gcum = SM[0:CH, 240:260]
        egc = SM[0:CH, 260:280]
        kds = SM[0:CH, 280:300]
        t20a = SM[0:CH, 300:320]
        t20b = SM[0:CH, 320:340]
        eal = SM[0:CH, 340:344]
        st = SM[:, 344:364]
        ssq = SM[:, 364:376]
        eglast = SM[:, 380:400]
        amx = SM[:, 400:402]
        asum = SM[:, 402:404]
        arec = SM[:, 404:406]
        head_ss = SM[:, 432:480].rearrange("p (n h) -> p n h", h=H)
        qk_ss = SM[:, 408:432]
        prob = R[:, 0:640].rearrange("p (u n) -> p u n", u=2)
        probT = R[:, 640:1024 + 384].rearrange("p (u n) -> p u n", u=2)
        om = HM[:, 0:1280].rearrange("p (h t) -> p h t", h=H)
        qmraw = XS[:, 1024:1536]
        qmT = R[:, 1408:2688].rearrange("p (h t) -> p h t", h=H)
        cs_out = XS[0:3, :].rearrange("p (s n) -> p s n", s=2)
        wmq_sb = W[:, 16384:20480].rearrange("p (k n) -> p k n", k=KD)
        wmo_sb = W[:, 20480:24576].rearrange("p (k n) -> p k n", k=4)

        gu_sb = W[:, 0:16384].rearrange("p (k n) -> p k n", k=KD)
        dn_sb = W[:, 16384:24576].rearrange("p (k n) -> p k n", k=KD)
        xparts = V[:, 0:4608].bitcast(BF16).rearrange("p (b s d) -> p b s d", b=TB, s=3)
        yacc = V[:, 4608:7168].rearrange("p (j n) -> p j n", j=NC)
        b3 = V[0:96, 7168:8192].bitcast(BF16)
        braw = V[0:96, 0:2048]
        bhi = V[0:96, 2048:3072].bitcast(BF16)
        bmid = V[0:96, 3072:4096].bitcast(BF16)
        bdn = V[0:E, 4608:5632]
        wr_sb = V[:, 5632:5888].rearrange("p (k n) -> p k n", k=KD)
        gateT = V[0:E, 5888:6272]
        bd = R[:, 0:640].rearrange("p (j t) -> p j t", j=NC)
        xgT = R[:, 640:1152].rearrange("p (k t) -> p k t", k=KD)
        x_rest = R[:, 640:3712].rearrange("p (b d) -> p b d", b=TB)
        gt_sb, sig_sb, up_sb = R[:, 1152:1664], R[:, 1664:2176], R[:, 2176:2688]
        act_sb = R[:, 2688:3200]
        actT = R[:, 3200:3712].rearrange("p (k t) -> p k t", k=4)
        y_sb = R[:, 3712:4224]
        sel = R[0:96, 4224:4256].bitcast(BF16)
        gcur = R[:, 4256:4261]
        gate = KV[:, 0:96].rearrange("p (b e) -> p b e", b=TB)
        gated = KV[:, 96:256].rearrange("p (j e) -> p j e", j=NC)
        rpos = KV[:, 256:355].rearrange("p (b e) -> p b e", b=TB)
        mask = KV[:, 356:452].rearrange("p (b e) -> p b e", b=TB)
        lg = KV[:, 452:560].rearrange("p (b e) -> p b e", b=TB)
        mrep = KV[:, 560:668].rearrange("p (b e) -> p b e", b=TB)
        top8 = KV[:, 668:692].rearrange("p (b e) -> p b e", b=TB)
        rep8 = KV[:, 692:716].rearrange("p (b e) -> p b e", b=TB)
        S = KV[:, 716:908].bitcast(BF16).rearrange("p (b a s) -> p b a s", b=TB, a=2)
        id3 = KV[0:96, 908:925].bitcast(BF16)
        identb = KV[:, 1212:1276].bitcast(BF16)
        cnt, tot, start = KV[0:E, 988:989], KV[0:E, 989:990], KV[0:E, 990:991]
        flags, pos4 = KV[0:E, 992:996], KV[0:E, 996:1000]
        hot = KV[0:E, 1000:1128].rearrange("p (b s) -> p b s", b=XTRA)
        xlist = KV[:, 1128:1200].bitcast(I32)
        ntop = KV[:, 1200:1203]
        gsum = KV[:, 1203:1206]

        def bcast(ap, shape, *axes):
            for a in axes:
                ap = ap.unsqueeze(a)
            return ap.broadcast_to(shape)

        def pieces(f):
            return [(upad[:, f, 0:SEQ], 0, SEQ), (upad[:, f, SEQ + 3:SEQ + 3 + DEC], SEQ, DEC)]

        kraws = [X[:, 1024:1536], W[:, 1792:2304]]
        cmasks = [W[0:CH, 1280 * i:1280 * i + 1280].rearrange("p (n i) -> p n i", n=NP_) for i in range(2)]

        mla_units, mem_units = [], []
        for h in range(H):
            for b in range(TB):
                rows = P if b < 2 else DEC
                qs = slice(b * P, b * P + rows)
                ks = slice(0, (b + 1) * P) if b < 2 else slice(SEQ, NKEY)
                vs = [vk[:, i, h * P:(h + 1) * P] for i in range(b + 1)] if b < 2 else \
                    [vk[:, 2, h * P:(h + 1) * P], vk[:, 3, h * P:(h + 1) * P], vk[0:DEC, 4, h * P:(h + 1) * P]]
                mla_units.append((rows, [(qTn[:, h, qs], kT[:, h, ks]), (qTr[:, h, qs], kpeT[:, ks])],
                                  ks.stop - ks.start, b < 2, vs, hT[:, H + h, qs]))
                km, vm = (km_p, vm_p) if b < 2 else (km_s, vm_s)
                mem_units.append((rows, [(qmT[:, h, qs], km[:, h, :])], NMEM, False,
                                  [vm[:, i, h * P:(h + 1) * P] for i in range(2)], om[:, h, qs]))

        MIX = [("a", 0), ("lat", 0), ("b", 0), ("q", 0),
               ("out", 0), ("a", 1), ("out_t", 0), ("q_norm", 0), ("b", 1), ("q_t", 0), ("q", 1),
               ("out", 1), ("a", 2), ("out_t", 1), ("q_norm", 1), ("b", 2), ("q_t", 1), ("q", 2),
               ("out", 2), ("a", 3), ("out_t", 2), ("q_norm", 2), ("b", 3), ("q_t", 2), ("k", 0),
               ("out", 3), ("a", 4), ("out_t", 3), ("k_norm", 0), ("b", 4), ("k", 1), ("k_t", 0), ("k", 2),
               ("k_norm", 1), ("out", 4), ("k_t", 1), ("k", 3), ("k_norm", 2), ("out_t", 4), ("k_t", 2), ("k", 4),
               ("k_norm", 3), ("k_t", 3), ("k_norm", 4), ("k_t", 4)]
        taken_at = [({"b": "out", "q": "q_norm", "k": "k_norm"}[s], i) for s, i in MIX if s in ("b", "q", "k")]
        used_at = [m for m in MIX if m[0] in ("out", "q_norm", "k_norm")]
        HEAD_NORMS = [used_at.index(m) for m in taken_at] + [len(used_at) + b for b in range(TB)]
        ROOTS_QK = 5

        block = ctx.enter_context(nc.Block())

        @block.sync
        def _(sp):
            def load(dst, src, name):
                sp.dma_start(dst, src).then_inc(sem(name), 16)

            def k_major(w, k0, k1):
                return w[k0 * P:k1 * P, :].rearrange("(k p) n -> p k n", p=P)

            def b_major(a):
                return a.rearrange("(b p) n -> p b n", p=P)

            load(mem3, b_major(mem_prompt[0]), "ld_mem")
            load(CO[:, :], consts, "ld_const")
            sp.wait_ge(sem("ld_rows"), 160)
            load(wmk_sb, k_major(w_mk[0], 0, KD), "ld_wmk")
            load(kcache, b_major(cache_mem_k[0, 0].rearrange("t h d -> t (h d)")), "ld_kcache")
            load(wmv_sb, k_major(w_mv[0], 0, KD), "ld_wmv")
            load(x3[:, 0:2, :], b_major(x_prompt[0]), "ld_x")
            load(x3[0:DEC, 2, :], x_sample[0], "ld_x")
            for n in range(2):
                load(w_in_sb[:, 4 * n:4 * n + 4, :], k_major(w_in[0], 4 * n, 4 * n + 4), f"ld_win{n}")
            load(wqb_sb, k_major(w_qb[0], 0, 3), "ld_wq")
            load(wkvb_sb, k_major(w_kvb[0], 0, 2), "ld_wq")
            sp.wait_ge(sem("cols_ready"), 2)
            load(vm_s, b_major(cache_mem_v[0, 0].rearrange("t h d -> t (h d)")), "ld_vcache")
            sp.wait_ge(sem("x_scaled"), TB)
            load(gstate[:, 1, :].rearrange("p (h v) -> p h v", h=H), state_gdn[0, 0].rearrange("h k v -> k h v"),
                 "ld_state")
            load(lat_past, b_major(cache_kv_latent[0, 0]), "ld_past")
            load(kpe_past, b_major(cache_k_rope[0, 0]), "ld_past")
            sp.wait_ge(sem("mk_ready"), 2)
            sp.dma_start(b_major(p_mk[0, 0].rearrange("t h d -> t (h d)")), mk_out).then_inc(sem("st_mk"), 16)
            sp.wait_ge(sem("mv_ready"), 2)
            sp.dma_start(b_major(p_mv[0, 0].rearrange("t h d -> t (h d)")), vm_p).then_inc(sem("st_out"), 16)
            sp.wait_ge(sem("state_new"), 4)
            sp.dma_start(p_s[0, 0].rearrange("h k v -> k h v"), gstate[:, 0, :].rearrange("p (h v) -> p h v", h=H))\
              .then_inc(sem("st_state"), 16)
            sp.wait_ge(sem("state_new"), 5)
            sp.dma_start(s_s[0, 0].rearrange("h k v -> k h v"), gstate[:, 1, :].rearrange("p (h v) -> p h v", h=H))\
              .then_inc(sem("st_state"), 16)
            sp.wait_ge(*at("lat_ready"))
            sp.dma_start(b_major(p_lat[0, 0]), cl[:, 0:2, 384:640]).then_inc(sem("st_lat"), 16)
            sp.dma_start(s_lat[0, 0], cl[0:DEC, 2, 384:640]).then_inc(sem("st_lat"), 16)
            sp.wait_ge(*at("kpe_ready"))
            sp.dma_start(b_major(p_kpe[0, 0]), cl[:, 0:2, 640:704]).then_inc(sem("st_lat"), 16)
            sp.dma_start(s_kpe[0, 0], cl[0:DEC, 2, 640:704]).then_inc(sem("st_lat"), 16)
            sp.wait_ge(sem("gdn_mix"), NC)
            sp.wait_ge(sem("st_lat"), 64)
            sp.wait_ge(sem("cl_tr"), 7)
            for n in range(2):
                load(wout_sb[:, 4 * n:4 * n + 4, :], k_major(w_out[0], 4 * n, 4 * n + 4), f"ld_wout{n}")
            sp.wait_ge(sem("cs_ev"), 6)
            sp.dma_start(p_conv[0, 0], cs_out[:, 0, :]).then_inc(sem("st_conv"), 16)
            sp.dma_start(s_conv[0, 0], cs_out[:, 1, :]).then_inc(sem("st_conv"), 16)
            sp.wait_ge(sem("st_state"), 32)
            sp.wait_ge(sem("att_o"), ATT["mem"])
            sp.wait_ge(sem("xpad"), 2)
            load(x3[:, 0:2, :], b_major(x_prompt[0]), "ld_x2")
            load(x3[0:DEC, 2, :], x_sample[0], "ld_x2")
            load(wmq_sb, k_major(w_mq[0], 0, KD), "ld_wmq")
            load(wmo_sb, k_major(w_mo[0], 0, 4), "ld_wmo")
            for k in range(KD):
                load(gu_sb[:, k, :], w_gu[0, 0, k * P:(k + 1) * P, :], f"ld_gu{k}")
            sp.wait_ge(sem("res_add"), RES["x2"][0] + 2 * TB)
            load(wr_sb, k_major(w_router[0], 0, KD), "ld_wr")
            for n in range(3):
                load(braw[32 * n:32 * n + 32, :], b_gu[0], "ld_bias")
            load(bdn, b_down[0], "ld_bias")
            sp.wait_ge(sem("res_add"), RES["x3"][0] + 2 * TB)
            for k in range(KD // 2):
                load(dn_sb[:, 2 * k:2 * k + 2, :], k_major(w_down[0, 0], 2 * k, 2 * k + 2), f"ld_dn{k}")

            def gate_up_loads(it, e):
                for k in range(KD):
                    sp.wait_ge(sem("gu_used"), it * KD + (k + 1))
                    sp.dma_start(gu_sb[:, k, :], w_gu[0, bass.ds(e, 1), k * P:(k + 1) * P, :]
                                 .rearrange("a p n -> p (a n)")).then_inc(sem(f"ld_gu{k}"), 16)

            def down_loads(it, e):
                for k in range(KD // 2):
                    sp.wait_ge(sem("dn_used"), it * (KD // 2) + (k + 1))
                    sp.dma_start(dn_sb[:, 2 * k:2 * k + 2, :], w_down[0, bass.ds(e, 1), 2 * k * P:(2 * k + 2) * P, :]
                                 .rearrange("a (k p) n -> p (a k) n", p=P)).then_inc(sem(f"ld_dn{k}"), 16)

            gate_up_loads(0, 1)
            sp.wait_ge(sem("y0_add"), 2 * TB)
            for odd in range(2):
                rows = slice(64 * odd, 64 * odd + 64)
                nb = (NC + 1 - odd) // 2
                for half in range(2):
                    dst = slice(64 * half, 64 * half + 64)
                    load(yacc[dst, odd::2, :], x3[rows, 0:nb, 512 * half:512 * half + 512], "ld_yacc")
                    load(gated[dst, odd::2, :], gate[rows, 0:nb, :], "ld_yacc")
            down_loads(0, 1)
            with sp.Fori(1, E - 1) as it:
                gate_up_loads(it, it + 1)
                down_loads(it, it + 1)
            sp.wait_ge(*at("list_ready"))
            n_extra = sp.value_load(xlist[0:1, 2 * LIST:2 * LIST + 1], min_val=0, max_val=LIST - 1)
            with sp.If(n_extra > 0):
                with sp.Fori(0, n_extra) as j:
                    e = sp.value_load(xlist[0:1, bass.ds(j, 1)], min_val=0, max_val=E - 1)
                    gate_up_loads(j + (E - 1), e)
                    down_loads(j + (E - 1), e)
            sp.wait_ge(*at("y_final"))
            for j in range(NC):
                dst = yp[0, j * CH:(j + 1) * CH, :] if j < SEQ // CH else ys[0]
                for half in range(2):
                    sp.dma_start(dst[:, 512 * half:512 * half + 512], yacc[64 * half:64 * half + 64, j, :])\
                      .then_inc(sem("st_out"), 16)
            for name, n in (("st_state", 2), ("st_lat", 4), ("st_conv", 2), ("st_mk", 1), ("st_out", 1 + 2 * NC)):
                sp.wait_ge(sem(name), 16 * n)

        @block.gpsimd
        def _(pool):
            done, taken = [0], 0
            pool.wait_ge(sem("ld_const"), 16)

            def root(tile):
                pool.wait_ge(sem("var_ready"), done[0] + 1)
                done[0] += 1
                pool.tensor_tensor(tile, tile, minus_half[0:tile.shape[0], :].broadcast_to(list(tile.shape)), ALU.pow).then_inc(sem("root_ready"), 1)

            def head_roots(n, rows, heads):
                for _ in range(n):
                    root(st[0:rows, 0:heads])

            root(st[:, 0:2])
            root(ssq[:, 0:3])
            head_roots(2, P, H)
            root(qk_ss)
            for n in range(3):
                root(st[:, 0:TB])
            for step, i in [s for s in MIX if s[0] in ("out", "q_norm", "k_norm")]:
                rows = CH if step == "out" else (DEC if (step, i) in (("q_norm", 2), ("k_norm", 4)) else P)
                root(head_ss[0:rows, HEAD_NORMS.index(taken) % 12, :])
                taken += 1
            root(ssq[:, 5:8])
            for rows in (P, P, DEC):
                root(head_ss[0:rows, HEAD_NORMS.index(taken) % 12, :])
                taken += 1
            root(ssq[:, 8:11])

        @block.scalar
        def _(act):
            def run(out, in_, func=ACT.Copy, **kw):
                return act.activation(out, in_, func, **kw)

            act.dma_start(conv7[0:3, :], state_conv[0, 0]).then_inc(sem("ld_rows"), 16)
            act.dma_start(conv7[3:7, :], conv_w[0]).then_inc(sem("ld_rows"), 16)
            for src, r0, nr in ((norm_mix, 0, 8), (norm_mem, 8, 8), (mem_norm, 16, 8), (norm_ffn, 24, 8),
                                (q_a_norm, 32, 3), (k_nope_norm, 35, 1), (gdn_norm, 36, 1), (mq_norm, 37, 1)):
                act.dma_start(g_rows[r0:r0 + nr, :], src[0].rearrange("(k p) -> k p", p=P)).then_inc(sem("ld_rows"), 16)
            for src, c0, n in ((kv_a_norm, 0, 256), (q_norm, 256, 192), (k_rope_norm, 448, 64), (mk_norm, 512, 128),
                               (b_router, 640, 32), (dt_bias, 672, 4), (a_log, 676, 4)):
                act.dma_start(GN[:, c0:c0 + n], src.broadcast_to([P, n])).then_inc(sem("ld_gn"), 16)

            def squares(src, b, col, junk, tag):
                run(junk, src[:, b, :], ACT.Square, accum_out=ssq[:, col:col + 1]).then_inc(sem(tag), 1)

            def feature_major(n, banks, tag, dst, cols, gain, width):
                act.wait_ge(sem("rows_tr"), NORM[tag] + n + 1)
                run(dst[:, n, :], PS[banks[n % len(banks)]][:, 0:width], scale=gain[:, n:n + 1])\
                    .then_inc(sem("rows_ev"), 1)

            act.wait_ge(sem("ld_mem"), 16)
            for b in range(2):
                if b:
                    act.wait_ge(sem("mem_sq"), b)
                squares(mem3, b, 3 + b, W[:, 23104:24128], "mem_sq")
            act.wait_ge(sem("cols_tr"), 1)
            run(convw, PS[7][:, 0:96].rearrange("p (f j) -> p f j", j=8)[:, :, 0:7]).then_inc(sem("cols_ready"), 1)
            act.wait_ge(sem("cols_tr"), 2)
            run(GC[:, 0:38], PS[6][:, 0:38]).then_inc(sem("cols_ready"), 1)
            act.wait_ge(sem("cols_ready"), 2)
            for k in range(KD):
                feature_major(k, (0, 1), "mem", mT, None, c_memn, NMEM)
            act.wait_ge(sem("ld_x"), 32)
            act.wait_ge(sem("xpad"), 1)
            act.wait_ge(sem("mem_sq"), 2)
            for b in range(TB):
                if b:
                    act.wait_ge(sem("x_sq"), b)
                squares(x3, b, b, W[:, 23104:24128], "x_sq")
            for b in range(2):
                act.wait_ge(sem("mk_mm"), b + 1)
                run(mk_out[:, b, :], PS[2 + b][:, :]).then_inc(sem("mk_ev"), 1)
            for b in range(2):
                act.wait_ge(sem("mv_mm"), b + 1)
                run(vm_p[:, b, :], PS[4 + b][:, :]).then_inc(sem("mv_ready"), 1)
            for b in range(2):
                act.wait_ge(sem("km_tr"), b + 1)
                if b == 0:
                    act.wait_ge(sem("cols_tr"), 2)
                run(km_s[:, :, b * P:(b + 1) * P], PS[6 + b][:, :].rearrange("p (h t) -> p h t", h=H))\
                    .then_inc(sem("km_ev"), 1)
            act.wait_ge(sem("mv_mm"), 2)
            for k in range(KD):
                feature_major(k, (0, 1), "x", hT, None, c_mix, T)
            for b in range(2):
                act.wait_ge(sem("km_tr"), b + 3)
                run(km_p[:, :, b * P:(b + 1) * P], PS[6 + b][:, :].rearrange("p (h t) -> p h t", h=H))\
                    .then_inc(sem("km_ev"), 1)
            act.wait_ge(*at("upad_ready"))
            for f in range(NU + NZ + 3):
                if f <= NU + NZ:
                    act.wait_ge(sem("u_mm"), f + 1)
                    src = PS[2 + f % 3]
                    if f < NU:
                        run(upad[:, f, 3:3 + SEQ], src[:, 0:SEQ])
                        run(upad[:, f, 6 + SEQ:6 + T], src[:, SEQ:T]).then_inc(sem("u_ev"), 1)
                    elif f < NU + NZ:
                        run(ztile[:, f - NU, :], src[:, 0:T], ACT.Silu).then_inc(sem("u_ev"), 1)
                    else:
                        run(abT, src[0:2 * H, 0:T]).then_inc(sem("u_ev"), 1)
                if 2 <= f < NU + 2:
                    act.wait_ge(sem("conv_done"), f - 1)
                    run(upad[:, f - 2, 0:323], conv_tmp, ACT.Silu).then_inc(sem("silu_done"), 1)
            for n in range(2 * TB):
                b, half = n // 2, n % 2
                rows = P if b < 2 else DEC
                c0, c1 = (0, 384) if half == 0 else (384, CLW)
                act.wait_ge(sem("cl_mm"), n + 1)
                run(cl[0:rows, b, c0:c1], PS[n % 2][0:rows, 0:c1 - c0]).then_inc(sem("cl_ev"), 1)

            act.wait_ge(*at("gb_ready"))
            run(beta.rearrange("p (c h) -> p c h", c=NC), gb[:, :, H:2 * H], ACT.Sigmoid).then_inc(mark("beta_ready"), 1)
            act.wait_ge(sem("ld_gn"), 112)
            run(eal, g_alog, ACT.Exp)
            act.wait_ge(*at("sp_abs"))
            run(t20b, t20b, ACT.Exp, scale=-1.0).then_inc(sem("sp_act"), 1)
            act.wait_ge(sem("sp_act"), 1)
            run(t20b, t20b, ACT.Ln, bias=1.0).then_inc(sem("sp_act"), 1)
            act.wait_ge(*at("gcum_ready"))
            run(egc, gcum, ACT.Exp).then_inc(mark("egc_ready"), 1)
            act.wait_ge(*at("gbc_mm"))
            for n, w in enumerate((512, 512, 256)):
                m = run(W[:, 12800 + 512 * n:12800 + 512 * n + w], PS[n][:, 0:w], ACT.Exp)
            m.then_inc(mark("ebc_ready"), 1)
            act.wait_ge(*at("diff_ready"))
            run(decT, decT, ACT.Exp).then_inc(sem("dec_exp"), 1)
            run(kds, kds, ACT.Exp).then_inc(sem("dec_exp"), 1)
            act.wait_ge(sem("silu_done"), NU)
            run(sq8[:, :, 0:SEQ], upad[:, 0:8, 0:SEQ], ACT.Square).then_inc(sem("sq_ready"), 1)
            run(sq8[:, :, SEQ:T], upad[:, 0:8, SEQ + 3:SEQ + 3 + DEC], ACT.Square).then_inc(sem("sq_ready"), 1)
            act.wait_ge(sem("rows_tr"), NORM["x"] + KD)
            for n in range(2 * NC):
                c = n // 2
                act.wait_ge(sem("kv_tr"), n + 1)
                run((vtok if n % 2 else ktok)[:, c, :], PS[3 + n % 4][0:CH, :]).then_inc(sem("kv_ev"), 1)
            for c in range(NC):
                act.wait_ge(sem("t0_tr"), c + 1)
                run(TT2[:, 4 * c:4 * c + 4, 0, :], PS[3 + c % 4][0:CH, 0:256].rearrange("p (h i) -> p h i", h=H))\
                    .then_inc(sem("t0_ev"), 1)
            act.wait_ge(*at("qg_ready"))
            for l in range(1, len(LEVELS)):
                for c in range(NC):
                    act.wait_ge(sem("p_mm"), NC * (l - 1) + min(c | 1, NC - 1) + 1)
                    if l > 1:
                        act.wait_ge(sem("q_mm"), NC * (l - 2) + c + 1)
                    run(pinv[:, 4 * c:4 * c + 4, :], PS[c // 2][0:CH, 256 * (c % 2):256 * (c % 2) + 256]
                        .rearrange("p (h i) -> p h i", h=H)).then_inc(sem("p_ev"), 1)
            for c in range(NC):
                act.wait_ge(sem("w_mm"), min(c | 1, NC - 1) + 1)
                run(wT[:, 4 * c:4 * c + 4, :], PS[c // 2][:, 256 * (c % 2):256 * (c % 2) + 256]
                    .rearrange("p (h i) -> p h i", h=H)).then_inc(sem("w_ev"), 1)

            events = [0]

            def head_squares(srcs, rows, width, junk):
                n = events[0]
                if n:
                    act.wait_ge(sem("act_step"), n)
                for h, src in enumerate(srcs):
                    m = run(junk[0:rows, width * h:width * (h + 1)], src, ACT.Square,
                            accum_out=head_ss[0:rows, n % 12, h:h + 1])
                m.then_inc(sem("act_step"), 1)
                events[0] += 1

            def scan_b(c):
                act.wait_ge(sem("o_mm"), c + 1)
                head_squares([PS[4][0:CH, h * P:(h + 1) * P] for h in range(H)], CH, HD, W[:, 512:1280])
                if c:
                    act.wait_ge(sem("o_tr"), c)
                run(otok, PS[4][0:CH, :]).then_inc(sem("o_copy"), 1)

            def latents():
                for k in range(3):
                    act.wait_ge(sem("cl_tr"), k + 1)
                    run(cqT[:, k, :], PS[k % 2][:, 0:T], scale=c_qa[:, k:k + 1]).then_inc(sem("cq_ev"), 1)
                for k in range(2):
                    act.wait_ge(sem("cl_tr"), 4 + k)
                    run(latT[:, k, 0:SEQ], PS[0][:, 0:SEQ])
                    run(latT[:, k, SEQ:NKEY], PS[1][:, 0:PAST + DEC]).then_inc(sem("lat_ev"), 1)
                act.wait_ge(sem("cl_tr"), 7)
                run(kpeT[:, 0:SEQ], PS[2][0:ROPE, 0:SEQ])
                run(kpeT[:, SEQ + PAST:NKEY], PS[2][0:ROPE, SEQ:T])
                run(kpeT[:, SEQ:SEQ + PAST], PS[0][0:ROPE, 0:PAST]).then_inc(mark("kpe_ev"), 1)

            def q_project(b):
                rows = P if b < 2 else DEC
                act.wait_ge(sem("q_proj"), b + 1)
                head_squares([PS[h // 2][0:rows, QK * (h % 2):QK * (h % 2) + QK] for h in range(H)], rows, QK, W[:, 512:1280])
                if b:
                    act.wait_ge(sem("qT_tr"), b)
                else:
                    act.wait_ge(sem("st_mk"), 16)
                for half in range(2):
                    m = run(qraw[0:rows, 384 * half:384 * half + 384], PS[half][0:rows, 0:384])
                m.then_inc(sem("q_ev"), 1)

            def q_feature_major(b):
                rows = P if b < 2 else DEC
                act.wait_ge(sem("qT_tr"), b + 1)
                run(qTn[:, :, b * P:b * P + rows], PS[2][:, :].rearrange("p (h t) -> p h t", h=H)[:, :, 0:rows])
                run(qTr[:, :, b * P:b * P + rows], PS[7][0:ROPE, :].rearrange("p (h t) -> p h t", h=H)[:, :, 0:rows])\
                    .then_inc(sem("qT_ev"), 1)

            def kv_project(kb):
                rows = P if kb < 4 else DEC
                act.wait_ge(sem("kvl_mm"), 2 * kb + 1)
                head_squares([PS[0][0:rows, h * P:(h + 1) * P] for h in range(H)], rows, HD, W[:, 512:1280])
                if kb >= 2:
                    act.wait_ge(sem("kT_tr"), kb - 1)
                elif kb == 0:
                    act.wait_ge(sem("qT_tr"), TB)
                run(kraws[kb % 2][0:rows, :], PS[0][0:rows, :]).then_inc(sem("k_raw"), 1)
                act.wait_ge(sem("kvl_mm"), 2 * kb + 2)
                run(vk[0:rows, kb, :], PS[1][0:rows, :]).then_inc(sem("v_raw"), 1)

            def k_feature_major(kb):
                rows = P if kb < 4 else DEC
                act.wait_ge(sem("kT_tr"), kb + 1)
                run(kT[:, :, kb * P:kb * P + rows], PS[2][:, :].rearrange("p (h t) -> p h t", h=H)[:, :, 0:rows],
                    scale=c_kn).then_inc(sem("kT_ev"), 1)

            for step, i in MIX:
                if step == "b":
                    scan_b(i)
                elif step == "lat":
                    latents()
                elif step == "q":
                    q_project(i)
                elif step == "q_t":
                    q_feature_major(i)
                elif step == "k":
                    kv_project(i)
                elif step == "k_t":
                    k_feature_major(i)

            def attention(tag, units, scale):
                for n in range(len(units) + 2):
                    if n < len(units):
                        rows, terms, nkeys, masked, vs, out = units[n]
                        act.wait_ge(sem("att_mx"), ATT[tag] + n + 1)
                        if n >= 2:
                            act.wait_ge(sem("att_tr"), ATT[tag] + n - 1)
                        run(prob[0:rows, n % 2, 0:nkeys], PS[n % 2][0:rows, 0:nkeys], ACT.Exp, scale=scale,
                            bias=amx[0:rows, n % 2:n % 2 + 1], accum_out=asum[0:rows, n % 2:n % 2 + 1])\
                            .then_inc(sem("att_ex"), 1)
                    if n >= 2:
                        rows, terms, nkeys, masked, vs, out = units[n - 2]
                        u = n % 2
                        act.wait_ge(sem("att_tr"), ATT[tag] + n - 1)
                        if n >= 4:
                            act.wait_ge(sem("att_pv"), ATT[tag] + n - 3)
                        if vs[-1].shape[0] == P:
                            m = run(probT[:, u, 0:len(vs) * P].rearrange("p (t q) -> p t q", q=P)[:, :, 0:rows],
                                    PS[2 + u][:, 0:len(vs) * P].rearrange("p (t q) -> p t q", q=P)[:, :, 0:rows])
                        else:
                            for t, v in enumerate(vs):
                                m = run(probT[0:v.shape[0], u, t * P:t * P + rows], PS[2 + u][0:v.shape[0], t * P:t * P + rows])
                        m.then_inc(sem("att_pt"), 1)

            attention("mla", mla_units, QK ** -0.5)

            act.wait_ge(sem("o_tr"), NC)
            for n in range(6):
                s, q = n // 3, n % 3
                act.wait_ge(sem("cs_tr"), n + 1)
                run(cs_out[:, s, 512 * q:512 * q + 512], PS[6 + n % 2][0:3, :]).then_inc(sem("cs_ev"), 1)

            act.wait_ge(sem("st_conv"), 32)
            for b in range(TB):
                act.wait_ge(sem("res_add"), RES["x2"][0] + 2 * b + 2)
                squares(x3, b, 5 + b, xs3[:, b, :], "res_sq")
            act.wait_ge(sem("res_mm"), RES["x2"][0] + 2 * TB)
            for k in range(KD):
                feature_major(k, (6, 7), "x2n", hT, None, c_mem, T)
            act.wait_ge(sem("rows_tr"), NORM["x2n"] + KD)
            for b in range(TB):
                rows = P if b < 2 else DEC
                act.wait_ge(sem("qm_mm"), b + 1)
                head_squares([PS[b][0:rows, h * P:(h + 1) * P] for h in range(H)], rows, HD, XS[:, 0:512])
                if b:
                    act.wait_ge(sem("qmT_tr"), b)
                run(qmraw[0:rows, :], PS[b][0:rows, :]).then_inc(sem("qm_ev"), 1)
                act.wait_ge(sem("qmT_tr"), b + 1)
                run(qmT[:, :, b * P:b * P + rows], PS[4 + b % 2][:, :].rearrange("p (h t) -> p h t", h=H)[:, :, 0:rows],
                    scale=c_mq).then_inc(sem("qmT_ev"), 1)
            attention("mem", mem_units, HD ** -0.5)

            for b in range(TB):
                act.wait_ge(sem("res_add"), RES["x3"][0] + 2 * b + 2)
                squares(x3, b, 8 + b, xs3[:, b, :], "res_sq")
            for k in range(KD):
                feature_major(k, (6, 7), "x3n", hT, None, c_ffn, T)
            act.wait_ge(*at("top_ready"))
            for b in range(TB):
                rows = P if b < 2 else DEC
                run(gate[0:rows, b, :], lg[0:rows, b, 0:E], ACT.Exp, bias=ntop[0:rows, b:b + 1]).then_inc(sem("gate_exp"), 1)
            act.wait_ge(*at("gt_tr"))
            run(gateT, PS[3][0:E, 0:384]).then_inc(mark("gt_ev"), 1)
            def sigmoid(it):
                act.wait_ge(sem("gt_ready"), it + 1)
                run(sig_sb, gt_sb, ACT.Sigmoid, scale=ALPHA).then_inc(sem("sig_ready"), 1)

            def copies(it):
                act.wait_ge(sem("actT_tr"), it + 1)
                run(actT, PS[2][:, :].rearrange("p (k t) -> p k t", k=4)).then_inc(sem("actT_ev"), 1)
                act.wait_ge(sem("dn_used"), it * (KD // 2) + KD // 2)
                run(y_sb, PS[3][:, :]).then_inc(sem("y_ev"), 1)

            sigmoid(0)
            copies(0)
            with act.Fori(1, E) as it:
                sigmoid(it)
                copies(it)
            act.wait_ge(*at("list_ready"))
            n_extra = act.value_load(xlist[0:1, 2 * LIST:2 * LIST + 1], min_val=0, max_val=LIST - 1)
            with act.If(n_extra > 0):
                with act.Fori(0, n_extra) as j:
                    sigmoid(j + E)
                    copies(j + E)
        @block.tensor
        def _(pe):
            def mm(out, lhsT, rhs, start=True, stop=True):
                return pe.matmul(out, lhsT, rhs, start=start, stop=stop)

            def tr(out, in_):
                return pe.transpose(out, in_, ident[0:in_.shape[0], 0:in_.shape[0]])

            def norm_transposes(src, nb, banks, tag):
                for k in range(KD):
                    if k >= len(banks):
                        pe.wait_ge(sem("rows_ev"), NORM[tag] + k - len(banks) + 1)
                    for b in range(nb):
                        m = tr(PS[banks[k % len(banks)]][:, b * P:(b + 1) * P], src[:, b, k * P:(k + 1) * P])
                    m.then_inc(sem("rows_tr"), 1)

            pe.wait_ge(sem("ld_const"), 16)
            pe.wait_ge(sem("ld_rows"), 160)
            for f in range(NU):
                m = tr(PS[7][:, 8 * f:8 * f + 7], conv7[:, f * P:(f + 1) * P])
            m.then_inc(sem("cols_tr"), 1)
            tr(PS[6][:, 0:38], g_rows).then_inc(sem("cols_tr"), 1)

            pe.wait_ge(sem("mem_scaled"), 2)
            norm_transposes(mem3, 2, (0, 1), "mem")
            pe.wait_ge(sem("rows_ev"), NORM["mem"] + KD)
            pe.wait_ge(sem("ld_wmk"), 16)
            for b in range(2):
                for k in range(KD):
                    m = mm(PS[2 + b][:, :], mT[:, k, b * P:(b + 1) * P], wmk_sb[:, k, :], k == 0, k == KD - 1)
                m.then_inc(sem("mk_mm"), 1)
            pe.wait_ge(sem("ld_wmv"), 16)
            for b in range(2):
                for k in range(KD):
                    m = mm(PS[4 + b][:, :], mT[:, k, b * P:(b + 1) * P], wmv_sb[:, k, :], k == 0, k == KD - 1)
                m.then_inc(sem("mv_mm"), 1)
            pe.wait_ge(sem("ld_kcache"), 16)
            pe.wait_ge(sem("cols_ready"), 2)
            for b in range(2):
                for h in range(H):
                    m = tr(PS[6 + b][:, h * P:(h + 1) * P], kcache[:, b, h * P:(h + 1) * P])
                m.then_inc(sem("km_tr"), 1)

            pe.wait_ge(sem("x_scaled"), TB)
            norm_transposes(xs3, TB, (0, 1), "x")
            for b in range(2):
                pe.wait_ge(sem("mk_ready"), b + 1)
                pe.wait_ge(sem("km_ev"), b + 1)
                for h in range(H):
                    m = tr(PS[6 + b][:, h * P:(h + 1) * P], mk_out[:, b, h * P:(h + 1) * P])
                m.then_inc(sem("km_tr"), 1)
            pe.wait_ge(sem("rows_ev"), NORM["x"] + KD)
            for f in range(NU + NZ + 1):
                cols = slice(f * P, (f + 1) * P) if f < NU + NZ else slice(AB0, AB0 + 2 * H)
                rows = cols.stop - cols.start
                if f < 3:
                    pe.wait_ge(sem("mk_ev" if f < 2 else "mv_ready"), f + 1 if f < 2 else 1)
                else:
                    pe.wait_ge(sem("u_ev"), f - 2)
                for k in range(KD):
                    if f == 0 and k % 4 == 0:
                        pe.wait_ge(sem(f"ld_win{k // 4}"), 16)
                    m = mm(PS[2 + f % 3][0:rows, 0:T], w_in_sb[:, k, cols], hT[:, k, :], k == 0, k == KD - 1)
                m.then_inc(sem("u_mm"), 1)
            for n in range(2 * TB):
                b, half = n // 2, n % 2
                rows = P if b < 2 else DEC
                c0, c1 = (0, 384) if half == 0 else (384, CLW)
                if n >= 2:
                    pe.wait_ge(sem("cl_ev"), n - 1)
                else:
                    pe.wait_ge(sem("rows_ev"), NORM["x"] + KD)
                for k in range(KD):
                    m = mm(PS[n % 2][0:rows, 0:c1 - c0], hT[:, k, b * P:b * P + rows],
                           w_in_sb[:, k, CL0 + c0:CL0 + c1], k == 0, k == KD - 1)
                m.then_inc(sem("cl_mm"), 1)

            pe.wait_ge(sem("u_ev"), NU + NZ + 1)
            pe.wait_ge(sem("km_ev"), 4)
            for c in range(NC):
                m = tr(PS[7][0:CH, 8 * c:8 * c + 8], abT[:, c * CH:(c + 1) * CH])
            m.then_inc(mark("ab_tr"), 1)
            pe.wait_ge(*at("g_ready"))
            mm(PS[7][0:CH, 64:84], u64, gts).then_inc(mark("gcum_mm"), 1)
            pe.wait_ge(*at("g2_ready"))
            pe.wait_ge(sem("cl_ev"), 2 * TB)
            for n, w in enumerate((512, 512, 256)):
                m = mm(PS[n][:, 0:w], ones[0:CH, :], W[0:CH, 512 * n:512 * n + w])
            m.then_inc(mark("gbc_mm"), 1)
            pe.wait_ge(sem("sq_ready"), 2)
            pe.wait_ge(*at("gcum_ready"))
            for b in range(TB):
                rows = P if b < 2 else DEC
                for f in range(2 * H):
                    m = mm(PS[7][0:rows, 96 + 8 * b + f:97 + 8 * b + f], sq8[:, f, b * P:b * P + rows], ones[:, 0:1])
            m.then_inc(mark("sum_mm"), 1)
            pe.wait_ge(sem("root_ready"), ROOTS_QK)
            for f in range(2 * H):
                if f >= 4:
                    pe.wait_ge(sem("qkn_ready"), f - 3)
                for b in range(TB):
                    rows = P if b < 2 else DEC
                    m = mm(PS[3 + f % 4][:, b * P:b * P + rows],
                           qk_ss[0:rows, 8 * b + f:8 * b + f + 1].broadcast_to([rows, P]), ident[0:rows, 0:rows])
                m.then_inc(sem("ss_mm"), 1)
            pe.wait_ge(sem("qkn_ready"), 2 * H)
            for n in range(2 * NC):
                c, isv = n // 2, n % 2
                if n >= 4:
                    pe.wait_ge(sem("kv_ev"), n - 3)
                for h in range(H):
                    src = qkn[:, H + h, c * CH:(c + 1) * CH] if not isv else \
                        (upad[:, 2 * H + h, c * CH:(c + 1) * CH] if c < 4 else upad[:, 2 * H + h, SEQ + 3:SEQ + 3 + CH])
                    m = tr(PS[3 + n % 4][0:CH, h * P:(h + 1) * P], src)
                m.then_inc(sem("kv_tr"), 1)
            pe.wait_ge(*at("dec_ready"))
            qkh = qkn.rearrange("p (a h) t -> p a h t", a=2)
            for c in range(NC):
                if c >= 3:
                    pe.wait_ge(sem("kq_ev"), c - 2)
                for h in range(H):
                    m = mm(PS[c % 3][0:CH, h * P:(h + 1) * P].rearrange("p (a i) -> p a i", a=2),
                           qkn[:, H + h, c * CH:(c + 1) * CH], qkh[:, :, h, c * CH:(c + 1) * CH])
                m.then_inc(sem("kq_mm"), 1)
            pe.wait_ge(sem("kv_ev"), 2 * NC)
            for c in range(NC):
                pe.wait_ge(sem("tt0"), c + 1)
                for h in range(H):
                    m = tr(PS[3 + c % 4][0:CH, h * CH:(h + 1) * CH], TT2[:, 4 * c + h, 1, :])
                m.then_inc(sem("t0_tr"), 1)
                if c == NC - 2:
                    pe.wait_ge(sem("t0_ev"), 1)
            for l in range(1, len(LEVELS)):
                pe.wait_ge(sem("cm_ready"), l)
                for c in range(NC):
                    pe.wait_ge(sem("t0_ev") if l == 1 else sem("tt_ev"), NC if l == 1 else NC * (l - 2) + c + 1)
                    if c == 0:
                        pe.wait_ge(sem("kq_ev"), NC)
                    for h in range(H):
                        i = 4 * c + h
                        m = mm(PS[c // 2][0:CH, 256 * (c % 2) + h * CH:256 * (c % 2) + (h + 1) * CH],
                               cmasks[l % 2][:, i, :], TT2[:, i, 0, :])
                    m.then_inc(sem("p_mm"), 1)
                for c in range(NC):
                    pe.wait_ge(sem("p_ev"), NC * (l - 1) + c + 1)
                    for h in range(H):
                        i = 4 * c + h
                        mm(PS[3 + c][0:CH, h * P:h * P + CH], TT2[:, i, 1, :], pinv[:, i, :])
                        m = mm(PS[3 + c][0:CH, h * P + CH:(h + 1) * P], pinv[:, i, :], TT2[:, i, 1, :])
                    m.then_inc(sem("q_mm"), 1)
            pe.wait_ge(sem("tt_ev"), NC * (len(LEVELS) - 1))
            pe.wait_ge(*at("kneg_ready"))
            for c in range(NC):
                for h in range(H):
                    i = 4 * c + h
                    m = mm(PS[c // 2][:, 256 * (c % 2) + h * CH:256 * (c % 2) + (h + 1) * CH],
                           kneg[:, c, h * P:(h + 1) * P], TT2[:, i, 1, :])
                m.then_inc(sem("w_mm"), 1)
            pe.wait_ge(sem("ld_state"), 16)
            pe.wait_ge(*at("qg_ready"))
            pe.wait_ge(*at("kd_ready"))

            def scan_a(c):
                s = 0 if c < 4 else 1
                pe.wait_ge(sem("w_ev"), c + 1)
                if c:
                    pe.wait_ge(sem("state_new"), c)
                else:
                    pe.wait_ge(*at("state0"))
                for h in range(H):
                    hs, i = slice(h * P, (h + 1) * P), 4 * c + h
                    mm(PS[3][0:CH, hs], TT2[:, i, 1, :], vtok[:, c, hs], True, False)
                    m = mm(PS[3][0:CH, hs], wT[:, i, :], gstate[:, s, hs], False, True)
                m.then_inc(sem("vn_mm"), 1)

            def scan_b(c):
                s = 0 if c < 4 else 1
                pe.wait_ge(sem("vn_ready"), c + 1)
                if c:
                    pe.wait_ge(sem("o_copy"), c)
                for h in range(H):
                    hs, i = slice(h * P, (h + 1) * P), 4 * c + h
                    mm(PS[5][:, hs], ktok[:, c, hs], vnew[:, hs])
                    mm(PS[4][0:CH, hs], qkn[:, h, c * CH:(c + 1) * CH], gstate[:, s, hs], True, False)
                    m = mm(PS[4][0:CH, hs], KQ[:, i, :], vnew[:, hs], False, True)
                m.then_inc(sem("o_mm"), 1)

            def scan_out(c):
                pe.wait_ge(sem("o_norm"), c + 1)
                if c:
                    pe.wait_ge(sem("gdn_mix"), c)
                for h in range(H):
                    m = tr(PS[6][:, h * CH:(h + 1) * CH], otok[:, h * P:(h + 1) * P])
                m.then_inc(sem("o_tr"), 1)

            def latents():
                pe.wait_ge(*at("cq_ready"))
                pe.wait_ge(sem("w_ev"), NC)
                for k in range(3):
                    if k >= 2:
                        pe.wait_ge(sem("cq_ev"), k - 1)
                    for b in range(TB):
                        m = tr(PS[k % 2][:, b * P:(b + 1) * P], cl[:, b, k * P:(k + 1) * P])
                    m.then_inc(sem("cl_tr"), 1)
                pe.wait_ge(sem("cq_ev"), 3)
                pe.wait_ge(*at("lat_ready"))
                pe.wait_ge(sem("ld_past"), 32)
                for k in range(2):
                    cs = slice(384 + k * P, 384 + (k + 1) * P)
                    if k:
                        pe.wait_ge(sem("lat_ev"), 1)
                    for b in range(2):
                        tr(PS[0][:, b * P:(b + 1) * P], cl[:, b, cs])
                    for b in range(2):
                        tr(PS[1][:, b * P:(b + 1) * P], lat_past[:, b, k * P:(k + 1) * P])
                    tr(PS[1][:, 256:320], cl[0:DEC, 2, cs]).then_inc(sem("cl_tr"), 1)
                pe.wait_ge(*at("kpe_ready"))
                for b in range(2):
                    tr(PS[2][0:ROPE, b * P:(b + 1) * P], cl[:, b, 640:704])
                tr(PS[2][0:ROPE, 256:320], cl[0:DEC, 2, 640:704])
                pe.wait_ge(sem("lat_ev"), 2)
                for b in range(2):
                    m = tr(PS[0][0:ROPE, b * P:(b + 1) * P], kpe_past[:, b, :])
                m.then_inc(sem("cl_tr"), 2)

            def q_project(b):
                rows = P if b < 2 else DEC
                if b:
                    pe.wait_ge(sem("q_ev"), b)
                else:
                    pe.wait_ge(sem("ld_wq"), 32)
                    pe.wait_ge(*at("kpe_ev"))
                for half in range(2):
                    for k in range(3):
                        m = mm(PS[half][0:rows, 0:384], cqT[:, k, b * P:b * P + rows],
                               wqb_sb[:, k, 384 * half:384 * half + 384], k == 0, k == 2)
                m.then_inc(sem("q_proj"), 1)

            def q_feature_major(b):
                rows = P if b < 2 else DEC
                pe.wait_ge(sem("q_ready"), b + 1)
                if b:
                    pe.wait_ge(sem("qT_ev"), b)
                for h in range(H):
                    tr(PS[2][:, h * P:h * P + rows], qraw[0:rows, h * QK:h * QK + P])
                for h in range(H):
                    m = tr(PS[7][0:ROPE, h * P:h * P + rows], qraw[0:rows, h * QK + P:(h + 1) * QK])
                m.then_inc(sem("qT_tr"), 1)

            wk4 = wkvb_sb.rearrange("p k (h n) -> p k h n", h=H)

            def kv_project(kb):
                rows = P if kb < 4 else DEC
                if kb:
                    pe.wait_ge(sem("k_raw"), kb)
                    pe.wait_ge(sem("v_raw"), kb)
                else:
                    pe.wait_ge(sem("q_ev"), TB)
                for part in range(2):
                    for k in range(2):
                        m = mm(PS[part][0:rows, :].rearrange("p (h n) -> p h n", h=H),
                               latT[:, k, kb * P:kb * P + rows], wk4[:, k, :, part * P:(part + 1) * P], k == 0, k == 1)
                    m.then_inc(sem("kvl_mm"), 1)

            def k_feature_major(kb):
                rows = P if kb < 4 else DEC
                pe.wait_ge(sem("k_norm"), kb + 1)
                if kb:
                    pe.wait_ge(sem("kT_ev"), kb)
                else:
                    pe.wait_ge(sem("qT_ev"), TB)
                for h in range(H):
                    m = tr(PS[2][:, h * P:h * P + rows], kraws[kb % 2][0:rows, h * P:(h + 1) * P])
                m.then_inc(sem("kT_tr"), 1)

            for step, i in MIX:
                if step == "a":
                    scan_a(i)
                elif step == "b":
                    scan_b(i)
                elif step == "out_t":
                    scan_out(i)
                elif step == "lat":
                    latents()
                elif step == "q":
                    q_project(i)
                elif step == "q_t":
                    q_feature_major(i)
                elif step == "k":
                    kv_project(i)
                elif step == "k_t":
                    k_feature_major(i)

            def attention(tag, units):
                for n in range(len(units) + 3):
                    if n < len(units):
                        rows, terms, nkeys, masked, vs, out = units[n]
                        if n >= 2:
                            pe.wait_ge(sem("att_ex"), ATT[tag] + n - 1)
                        for t, (q, k) in enumerate(terms):
                            m = mm(PS[n % 2][0:rows, 0:nkeys], q, k, t == 0, t == len(terms) - 1)
                        m.then_inc(sem("att_s"), 1)
                    if 2 <= n <= len(units) + 1:
                        rows, terms, nkeys, masked, vs, out = units[n - 2]
                        u = n % 2
                        pe.wait_ge(sem("att_nm"), ATT[tag] + n - 1)
                        if n >= 4:
                            pe.wait_ge(sem("att_pt"), ATT[tag] + n - 3)
                        for t, v in enumerate(vs):
                            kr = v.shape[0]
                            m = tr(PS[2 + u][0:kr, t * P:t * P + rows], prob[0:rows, u, t * P:t * P + kr])
                        m.then_inc(sem("att_tr"), 1)
                    if n >= 3:
                        rows, terms, nkeys, masked, vs, out = units[n - 3]
                        u = (n - 3) % 2
                        pe.wait_ge(sem("att_pt"), ATT[tag] + n - 2)
                        if n >= 5:
                            pe.wait_ge(sem("att_o"), ATT[tag] + n - 4)
                        for t, v in enumerate(vs):
                            kr = v.shape[0]
                            m = mm(PS[4 + u][:, 0:rows], v, probT[0:kr, u, t * P:t * P + rows], t == 0, t == len(vs) - 1)
                        m.then_inc(sem("att_pv"), 1)

            pe.wait_ge(sem("kT_ev"), 5)
            pe.wait_ge(sem("v_raw"), 5)
            pe.wait_ge(sem("state_new"), NC)
            pe.wait_ge(sem("gdn_mix"), NC)
            attention("mla", mla_units)

            pe.wait_ge(sem("att_o"), ATT["mem"])
            for n in range(6):
                s, q = n // 3, n % 3
                if n >= 2:
                    pe.wait_ge(sem("cs_ev"), n - 1)
                for i in range(4):
                    m = tr(PS[6 + n % 2][0:3, i * P:(i + 1) * P], ulast[:, 4 * q + i, s, :])
                m.then_inc(sem("cs_tr"), 1)

            def project(tag, lhs, w, nk, loads, banks):
                for n in range(2 * TB):
                    b, half = n // 2, n % 2
                    rows = P if b < 2 else DEC
                    if n >= len(banks):
                        pe.wait_ge(sem("res_add"), RES[tag][0] + n - len(banks) + 1)
                    for k in range(nk):
                        if n == 0 and k % (nk // len(loads)) == 0:
                            pe.wait_ge(sem(loads[k // (nk // len(loads))]), 16)
                        m = mm(PS[banks[n % len(banks)]][0:rows, :], lhs[:, k, b * P:b * P + rows],
                               w[:, k, 512 * half:512 * half + 512], k == 0, k == nk - 1)
                    m.then_inc(sem("res_mm"), 1)

            project("x2", hT, wout_sb, KD, ["ld_wout0", "ld_wout1"], (0, 1, 2, 3))

            pe.wait_ge(sem("res_scaled"), RES["x2"][1] + TB)
            pe.wait_ge(sem("res_add"), RES["x2"][0] + 2 * TB)
            pe.wait_ge(sem("cs_ev"), 6)
            norm_transposes(xs3, TB, (6, 7), "x2n")
            pe.wait_ge(sem("rows_ev"), NORM["x2n"] + KD)
            pe.wait_ge(sem("ld_wmq"), 16)
            for b in range(TB):
                rows = P if b < 2 else DEC
                for k in range(KD):
                    m = mm(PS[b][0:rows, :], hT[:, k, b * P:b * P + rows], wmq_sb[:, k, :], k == 0, k == KD - 1)
                m.then_inc(sem("qm_mm"), 1)
            for b in range(TB):
                rows = P if b < 2 else DEC
                pe.wait_ge(sem("qm_ready"), b + 1)
                if b == 2:
                    pe.wait_ge(sem("qmT_ev"), 1)
                for h in range(H):
                    m = tr(PS[4 + b % 2][:, h * P:h * P + rows], qmraw[0:rows, h * P:(h + 1) * P])
                m.then_inc(sem("qmT_tr"), 1)
            pe.wait_ge(sem("qmT_ev"), TB)
            pe.wait_ge(sem("ld_vcache"), 16)
            attention("mem", mem_units)
            pe.wait_ge(sem("att_o"), 2 * ATT["mem"])
            project("x3", om, wmo_sb, 4, ["ld_wmo"], (0, 1, 2, 3))

            pe.wait_ge(sem("res_scaled"), RES["x3"][1] + TB)
            norm_transposes(xs3, TB, (6, 7), "x3n")
            pe.wait_ge(sem("rows_ev"), NORM["x3n"] + KD)
            pe.wait_ge(sem("res_add"), RES["x3"][0] + 2 * TB)
            pe.wait_ge(sem("ld_wr"), 16)
            for b in range(TB):
                rows = P if b < 2 else DEC
                for k in range(KD):
                    m = mm(PS[0][0:rows, b * E:(b + 1) * E], hT[:, k, b * P:b * P + rows], wr_sb[:, k, :], k == 0, k == KD - 1)
            m.then_inc(mark("lg_mm"), 1)
            pe.wait_ge(*at("mask_ready"))
            for b in range(TB):
                for a in range(b + 1):
                    m = mm(PS[1][:, b * E:(b + 1) * E], ustrict if a == b else ones, mask[:, a, :], a == 0, a == b)
            m.then_inc(mark("rank_mm"), 1)
            for b in range(TB):
                m = mm(PS[2][0:E, 0:1], mask[:, b, :], ones[:, 0:1], b == 0, b == TB - 1)
            m.then_inc(mark("cnt_mm"), 1)
            def gates_and_list():
                pe.wait_ge(*at("gate_ready"))
                for b in range(TB):
                    m = tr(PS[3][0:E, b * P:(b + 1) * P], gate[:, b, :])
                m.then_inc(mark("gt_tr"), 1)
                pe.wait_ge(*at("gt_ev"))
                pe.wait_ge(sem("bd_ready"), 1)
                for n in range(2 * TB):
                    b, half = n // 2, n % 2
                    rows = P if b < 2 else DEC
                    if n >= 4:
                        pe.wait_ge(sem("y0_add"), n - 3)
                    mm(PS[4 + n % 4][0:rows, :], gateT[:, b * P:b * P + rows], bdn[:, 512 * half:512 * half + 512])\
                        .then_inc(sem("y0_mm"), 1)
                pe.wait_ge(*at("tot_ready"))
                mm(PS[2][0:E, 8:9], ustrict[0:E, 0:E], tot).then_inc(mark("start_mm"), 1)
                pe.wait_ge(*at("hot_ready"))
                for a in range(XTRA):
                    mm(PS[3][0:1, 0:LIST], CO[0:E, C_EV:C_EV + 1], hot[:, a, :], a == 0, a == XTRA - 1)
                for a in range(XTRA):
                    mm(PS[3][0:1, LIST:2 * LIST], CO[0:E, C_EV + 1 + a:C_EV + 2 + a], hot[:, a, :], a == 0, a == XTRA - 1)
                mm(PS[3][0:1, 2 * LIST:2 * LIST + 1], ones[0:E, 0:1], tot).then_inc(mark("list_mm"), 1)

            def gather(n):
                pe.wait_ge(sem("slots_ready"), n + 1)
                for k in range(KD):
                    for b in range(TB):
                        for s in range(3):
                            m = mm(PS[4][:, k * SLOTS:(k + 1) * SLOTS], xparts[:, b, s, k * P:(k + 1) * P],
                                   S[:, b, 0, :], b == 0 and s == 0, b == TB - 1 and s == 2)
                m.then_inc(sem("gather_mm"), 1)
                for b in range(TB):
                    m = pe.transpose(PS[5][:, 64 * b:64 * b + 64].bitcast(BF16), S[:, b, :, :].rearrange("p a s -> p (a s)"), identb)
                m.then_inc(sem("slots_tr"), 1)

            def gate_up(it):
                pe.wait_ge(sem("sel_ready"), it + 1)
                for g in range(2):
                    for half in range(2):
                        c = g * FF + half * 512
                        m = mm(PS[g][64 * half:64 * half + 64, :], sel, b3[:, c:c + 512], True, False)
                m.then_inc(sem("bias_mm"), 1)
                for k in range(KD):
                    pe.wait_ge(sem(f"ld_gu{k}"), it * 16 + 16)
                    for g in range(2):
                        for half in range(2):
                            c = g * FF + half * 512
                            m = mm(PS[g][64 * half:64 * half + 64, :], xgT[:, k, :], gu_sb[:, k, c:c + 512],
                                   False, k == KD - 1)
                    m.then_inc(sem("gu_used"), 1)

            def down(it):
                pe.wait_ge(sem("act_ready"), it + 1)
                for j in range(4):
                    m = tr(PS[2][:, j * P:(j + 1) * P], act_sb[:, j * P:(j + 1) * P])
                m.then_inc(sem("actT_tr"), 1)
                pe.wait_ge(sem("actT_ev"), it + 1)
                for n in range(KD // 2):
                    pe.wait_ge(sem(f"ld_dn{n}"), it * 16 + 16)
                    for k in (2 * n, 2 * n + 1):
                        for half in range(2):
                            m = mm(PS[3][64 * half:64 * half + 64, :], actT[:, k % 4, 64 * (k // 4):64 * (k // 4) + 64],
                                   dn_sb[:, k, 512 * half:512 * half + 512], k == 0, k == KD - 1)
                    m.then_inc(sem("dn_used"), 1)

            def scatter(it):
                pe.wait_ge(sem("y_ev"), it + 1)
                pe.wait_ge(sem("bd_ready"), it + 1)
                for j in range(NC):
                    pe.wait_ge(sem("acc_done"), it * NC + max(j, 1))
                    mm(PS[6 + j % 2][:, :], bd[:, j, :], y_sb).then_inc(sem("scat_mm"), 1)

            pe.wait_ge(sem("parts_ready"), TB)
            gather(0)
            pe.wait_ge(sem("xg_ready"), 1)
            gate_up(0)
            gates_and_list()
            pe.wait_ge(sem("y0_add"), 2 * TB)
            gather(1)
            pe.wait_ge(*at("list_ready"))
            down(0)
            scatter(0)
            with pe.Fori(1, E) as it:
                pe.wait_ge(sem("xg_ready"), it + 1)
                gate_up(it)
                gather(it + 1)
                down(it)
                scatter(it)
            n_extra = pe.value_load(xlist[0:1, 2 * LIST:2 * LIST + 1], min_val=0, max_val=LIST - 1)
            with pe.If(n_extra > 0):
                with pe.Fori(0, n_extra) as j:
                    gather(j + (E + 1))
                    pe.wait_ge(sem("xg_ready"), j + (E + 2))
                    gate_up(j + E)
                    down(j + E)
                    scatter(j + E)

        @block.vector
        def _(dve):
            steps = [0]

            def link(ins):
                steps[0] += 1
                ins.then_inc(sem("dve_step"), 1)
                dve.wait_ge(sem("dve_step"), steps[0])

            def tt(out, a, b, op):
                return dve.tensor_tensor(out, a, b, op)

            def ts(out, a, s1, s2=None, op0=ALU.mult, op1=None):
                if op1 is None:
                    return dve.tensor_scalar(out, a, s1, None, op0)
                return dve.tensor_scalar(out, a, s1, s2, op0, op1)

            roots = [0]

            def rooted(ins):
                roots[0] += 1
                ins.then_inc(sem("var_ready"), 1)
                dve.wait_ge(sem("root_ready"), roots[0])

            def rstd(dst, sums, n):
                rooted(ts(dst, sums, 1.0 / n, EPS, ALU.mult, ALU.add))

            def head_norm(x, sq, rows, heads, width, gain=None):
                s = st[0:rows, 0:heads]
                link(tt(sq, x, x, ALU.mult))
                link(dve.tensor_reduce(s, sq, AX, ALU.add))
                rstd(s, s, width)
                last = tt(x, x, bcast(s, [rows, heads, width], 2), ALU.mult)
                if gain is not None:
                    link(last)
                    last = tt(x, x, bcast(gain, [rows, heads, width], 1), ALU.mult)
                return last

            scaled = [0]

            def scale_heads(x, rows, width, gain=None):
                n = HEAD_NORMS.index(scaled[0])
                scaled[0] += 1
                s = head_ss[0:rows, n % 12, :]
                rstd(s, s, width)
                last = tt(x, x, bcast(s, [rows, H, width], 2), ALU.mult)
                if gain is not None:
                    link(last)
                    last = tt(x, x, bcast(gain, [rows, H, width], 1), ALU.mult)
                return last

            def rope(x, c, s, t):
                h = ROPE // 2
                x1, x2 = x[:, :, 0:h], x[:, :, h:ROPE]
                tt(t[0], x1, c, ALU.mult)
                tt(t[1], x2, s, ALU.mult)
                tt(t[2], x2, c, ALU.mult)
                link(tt(t[3], x1, s, ALU.mult))
                tt(x1, t[0], t[1], ALU.subtract)
                return tt(x2, t[2], t[3], ALU.add)

            dve.memset(x3[DEC:P, 2, :], 0.0).then_inc(sem("xpad"), 1)
            dve.memset(qk_ss, 1.0)
            dve.wait_ge(sem("mem_sq"), 2)
            rstd(st[:, 0:2], ssq[:, 3:5], D)
            for b in range(2):
                ts(mem3[:, b, :], mem3[:, b, :], st[:, b:b + 1]).then_inc(sem("mem_scaled"), 1)
            dve.wait_ge(sem("ld_gn"), 112)
            dve.wait_ge(sem("x_sq"), TB)
            rstd(ssq[:, 0:3], ssq[:, 0:3], D)
            for b in range(2):
                dve.wait_ge(sem("mk_ev"), b + 1)
                head_norm(mk_out[:, b, :].rearrange("p (h d) -> p h d", h=H),
                          HM[:, 2048:2560].rearrange("p (h d) -> p h d", h=H), P, H, HD, g_mk)\
                    .then_inc(sem("mk_ready"), 1)
                dve.wait_ge(sem("mk_ready"), b + 1)
            dve.wait_ge(sem("rows_tr"), NORM["mem"] + KD)
            dve.wait_ge(sem("km_tr"), 2)
            for b in range(TB):
                ts(xs3[:, b, :], x3[:, b, :], ssq[:, b:b + 1]).then_inc(sem("x_scaled"), 1)
            dve.wait_ge(sem("mv_mm"), 2)
            dve.wait_ge(sem("cols_ready"), 2)
            dve.memset(upad[:, :, 0:3], 0.0)
            dve.memset(cl[DEC:P, 2, :], 0.0)
            dve.tensor_copy(upad[:, :, 3 + SEQ:6 + SEQ], convw[:, :, 0:3]).then_inc(mark("upad_ready"), 1)
            dve.wait_ge(*at("upad_ready"))
            dve.wait_ge(sem("x_scaled"), TB)
            dve.memset(gstate[:, 0, :], 0.0).then_inc(mark("state0"), 1)
            for f in range(NU):
                dve.wait_ge(sem("u_ev"), f + 1)
                dve.tensor_copy(ulast[:, f, 0, :], upad[:, f, SEQ:SEQ + 3])
                dve.tensor_copy(ulast[:, f, 1, :], upad[:, f, T + 3:T + 6])
                if f:
                    dve.wait_ge(sem("silu_done"), f)
                link(ts(conv_tmp, upad[:, f, 0:323], convw[:, f, 3:4]))
                for j in range(1, CW):
                    m = dve.scalar_tensor_tensor(conv_tmp, upad[:, f, j:j + 323], convw[:, f, 3 + j:4 + j], conv_tmp,
                                                 ALU.mult, ALU.add)
                    if j < CW - 1:
                        link(m)
                m.then_inc(sem("conv_done"), 1)

            dve.wait_ge(*at("ab_tr"))
            dve.tensor_copy(gb, PS[7][0:CH, 0:8 * NC].rearrange("p (c n) -> p c n", c=NC)).then_inc(mark("gb_ready"), 1)
            dve.wait_ge(*at("gb_ready"))
            c20 = [CH, NC, H]

            def by_pair(a):
                return a.rearrange("p (c h) -> p c h", c=NC)

            link(tt(by_pair(t20a), gb[:, :, 0:H], bcast(g_dt, c20, 1), ALU.add))
            dve.scalar_tensor_tensor(t20b, t20a, -1.0, t20a, ALU.mult, ALU.max).then_inc(mark("sp_abs"), 1)
            dve.wait_ge(sem("sp_act"), 2)
            link(dve.scalar_tensor_tensor(gts, t20a, 0.0, t20b, ALU.max, ALU.add))
            link(tt(by_pair(gts), by_pair(gts), bcast(eal, c20, 1), ALU.mult))
            ts(gts, gts, -1.0).then_inc(mark("g_ready"), 1)
            dve.wait_ge(*at("g_ready"))
            full = [CH, NP_, CH]
            dve.wait_ge(sem("cl_mm"), 2 * TB)
            tt(g2, bcast(u64, full, 1), bcast(gts, full, 2), ALU.mult).then_inc(mark("g2_ready"), 1)
            dve.wait_ge(*at("gcum_mm"))
            dve.tensor_copy(gcum, PS[7][0:CH, 64:84]).then_inc(mark("gcum_ready"), 1)
            dve.wait_ge(*at("gcum_ready"))
            dve.wait_ge(*at("ebc_ready"))
            for n, w in enumerate((8, 8, 4)):
                src = PS[n][0:CH, 0:CH * w].rearrange("p (n i) -> p n i", i=CH)
                tt(kds[:, 8 * n:8 * n + w], src[:, :, CH - 1], gcum[:, 8 * n:8 * n + w], ALU.subtract)
                m = tt(decT[:, 8 * n:8 * n + w, :], src, bcast(gcum[:, 8 * n:8 * n + w], [CH, w, CH], 2), ALU.subtract)
            link(m)
            ts(decT, decT, 0.0, None, ALU.min).then_inc(mark("diff_ready"), 1)
            dve.tensor_copy(eglast, ebc[:, :, CH - 1])
            dve.wait_ge(sem("dec_exp"), 2)
            tt(decT, decT, bcast(u64, full, 1), ALU.mult).then_inc(mark("dec_ready"), 1)
            dve.wait_ge(*at("sum_mm"))
            ts(qk_ss[:, 0:16], PS[7][:, 96:112], EPS, None, ALU.add)
            rooted(ts(qk_ss[0:DEC, 16:24], PS[7][0:DEC, 112:120], EPS, None, ALU.add))
            for f in range(2 * H):
                dve.wait_ge(sem("ss_mm"), f + 1)
                for src, c0, n in pieces(f):
                    m = dve.scalar_tensor_tensor(qkn[:, f, c0:c0 + n], PS[3 + f % 4][:, c0:c0 + n],
                                                 HD ** -0.5 if f < H else 1.0, src, ALU.mult, ALU.mult)
                m.then_inc(sem("qkn_ready"), 1)
                dve.wait_ge(sem("qkn_ready"), f + 1)
            dve.wait_ge(*at("dec_ready"))
            dve.wait_ge(*at("beta_ready"))
            dve.wait_ge(sem("ss_mm"), 2 * H)
            four = [CH, H, CH]
            for c in range(NC):
                cs = slice(4 * c, 4 * c + 4)
                dve.wait_ge(sem("kq_mm"), c + 1)
                src = PS[c % 3][0:CH, :].rearrange("p (h a i) -> p h a i", h=H, a=2)
                tt(KQ[:, cs, :], src[:, :, 0, :], decT[:, cs, :], ALU.mult)
                tt(MT[:, cs, :], src[:, :, 1, :], decT[:, cs, :], ALU.mult).then_inc(sem("kq_ev"), 1)
                dve.wait_ge(sem("kq_ev"), c + 1)
                link(tt(MT[:, cs, :], MT[:, cs, :], bcast(beta[:, cs], four, 2), ALU.mult))
                link(tt(cmask[:, cs, :], MT[:, cs, :], bcast(lvl_masks[:, 0, :], four, 1), ALU.mult))
                tt(TT2[:, cs, 1, :], bcast(ident[0:CH, 0:CH], four, 1), cmask[:, cs, :], ALU.subtract)\
                    .then_inc(sem("tt0"), 1)
            dve.wait_ge(sem("tt0"), NC)

            def level_mask(l):
                tt(cmasks[l % 2], MT, bcast(lvl_masks[:, l, :], full, 1), ALU.mult).then_inc(sem("cm_ready"), 1)

            level_mask(1)
            dve.wait_ge(sem("kq_mm"), NC)
            q4 = qkn[:, 0:H, :].rearrange("p h (c i) -> p h c i", c=NC)
            e4 = ebc.rearrange("p (c h) i -> p h c i", c=NC)
            for h in range(H):
                m = tt(q4[:, h], q4[:, h], e4[:, h], ALU.mult)
            m.then_inc(mark("qg_ready"), 1)

            def latent_norm(l):
                sq = HM[:, 0:1152].rearrange("p (b n) -> p b n", b=TB)
                if l == 1:
                    dve.wait_ge(sem("cl_ev"), 2 * TB)
                    head_norm(cl[:, :, 0:384], sq, P, TB, Q_RANK).then_inc(mark("cq_ready"), 1)
                    dve.wait_ge(*at("cq_ready"))
                elif l == 2:
                    head_norm(cl[:, :, 384:640], sq[:, :, 0:256], P, TB, KV_RANK, g_kva).then_inc(mark("lat_ready"), 1)
                    dve.wait_ge(*at("lat_ready"))
                else:
                    link(head_norm(cl[:, :, 640:704], sq[:, :, 0:64], P, TB, ROPE, g_kr))
                    t = [HM[:, 1152 + 96 * i:1152 + 96 * i + 96].rearrange("p (n f) -> p n f", n=TB) for i in range(4)]
                    rope(cl[:, :, 640:704], cos, sin, t).then_inc(mark("kpe_ready"), 1)

            for l in range(1, len(LEVELS)):
                if l + 1 < len(LEVELS):
                    if l > 1:
                        dve.wait_ge(sem("p_mm"), NC * (l - 1))
                    level_mask(l + 1)
                if l <= 3:
                    latent_norm(l)
                for c in range(NC):
                    dve.wait_ge(sem("q_mm"), NC * (l - 1) + c + 1)
                    if c == 0 and l == 1:
                        dve.wait_ge(sem("t0_ev"), NC)
                    elif c == 0:
                        dve.wait_ge(sem("tt_ev"), NC * (l - 1))
                    t = TT2[:, 4 * c:4 * c + 4, :, :].rearrange("p n a i -> p (n a i)")
                    tt(t, t, PS[3 + c][0:CH, :], ALU.subtract).then_inc(sem("tt_ev"), 1)
            dve.wait_ge(sem("p_mm"), NC * (len(LEVELS) - 1))
            dve.wait_ge(sem("kv_ev"), 2 * NC)
            dve.wait_ge(*at("egc_ready"))
            for c in range(NC):
                k4 = ktok[:, c, :].rearrange("p (h d) -> p h d", h=H)
                m = tt(kneg[:, c, :].rearrange("p (h d) -> p h d", h=H), k4,
                       bcast(egc[:, 4 * c:4 * c + 4], [CH, H, HD], 2), ALU.mult)
            link(m)
            ts(kneg, kneg, -1.0).then_inc(mark("kneg_ready"), 1)
            for c in range(NC):
                k4 = ktok[:, c, :].rearrange("p (h d) -> p h d", h=H)
                m = tt(k4, k4, bcast(kds[:, 4 * c:4 * c + 4], [CH, H, HD], 2), ALU.mult)
            m.then_inc(mark("kd_ready"), 1)

            def temps(tile, rows, n):
                return [tile[0:rows, 128 * i:128 * i + 32 * n].rearrange("p (n f) -> p n f", n=n) for i in range(4)]

            def scan_a(c):
                dve.wait_ge(sem("vn_mm"), c + 1)
                if c:
                    dve.wait_ge(sem("o_mm"), c)
                tt(vnew.rearrange("p (h d) -> p h d", h=H), PS[3][0:CH, :].rearrange("p (h d) -> p h d", h=H),
                   bcast(beta[:, 4 * c:4 * c + 4], [CH, H, HD], 2), ALU.mult).then_inc(sem("vn_ready"), 1)

            def scan_b(c):
                s = 0 if c < 4 else 1
                dve.wait_ge(sem("o_mm"), c + 1)
                if s:
                    dve.wait_ge(sem("ld_state"), 16)
                if c:
                    dve.wait_ge(sem("state_new"), c)
                for h in range(H):
                    g = gstate[:, s, h * P:(h + 1) * P]
                    m = dve.scalar_tensor_tensor(g, g, eglast[:, 4 * c + h:4 * c + h + 1], PS[5][:, h * P:(h + 1) * P],
                                                 ALU.mult, ALU.add)
                m.then_inc(sem("state_new"), 1)

            def scan_out(c):
                dve.wait_ge(sem("o_copy"), c + 1)
                scale_heads(otok.rearrange("p (h d) -> p h d", h=H), CH, HD).then_inc(sem("o_norm"), 1)

            def scan_mix(c):
                dve.wait_ge(sem("o_tr"), c + 1)
                dve.scalar_tensor_tensor(hT[:, 0:H, c * CH:(c + 1) * CH],
                                         PS[6][:, 0:256].rearrange("p (h t) -> p h t", h=H), c_gdn,
                                         ztile[:, :, c * CH:(c + 1) * CH], ALU.mult, ALU.mult)\
                    .then_inc(sem("gdn_mix"), 1)

            def q_norm(b):
                rows = P if b < 2 else DEC
                dve.wait_ge(sem("q_ev"), b + 1)
                q4 = qraw[0:rows, :].rearrange("p (h n) -> p h n", h=H)
                link(scale_heads(q4, rows, QK, g_q[0:rows, :]))
                tab = [bcast(t[0:rows, b, :], [rows, H, 32], 1) for t in (cos, sin)]
                rope(q4[:, :, P:QK], tab[0], tab[1], temps(W[:, 1280:1792], rows, H)).then_inc(sem("q_ready"), 1)
                dve.wait_ge(sem("q_ready"), b + 1)

            def k_norm(kb):
                rows = P if kb < 4 else DEC
                dve.wait_ge(sem("k_raw"), kb + 1)
                scale_heads(kraws[kb % 2][0:rows, :].rearrange("p (h n) -> p h n", h=H), rows, HD)\
                    .then_inc(sem("k_norm"), 1)

            dve.wait_ge(sem("w_mm"), NC)
            for step, i in MIX:
                if step == "a":
                    scan_a(i)
                elif step == "b":
                    scan_b(i)
                elif step == "out":
                    scan_out(i)
                elif step == "out_t":
                    scan_mix(i)
                elif step == "q_norm":
                    q_norm(i)
                elif step == "k_norm":
                    k_norm(i)

            def attention(tag, units, scale):
                for n in range(len(units) + 3):
                    if n < len(units):
                        rows, terms, nkeys, masked, vs, out = units[n]
                        dve.wait_ge(sem("att_s"), ATT[tag] + n + 1)
                        if n >= 2:
                            dve.wait_ge(sem("att_ex"), ATT[tag] + n - 1)
                        sc = PS[n % 2][0:rows, 0:nkeys]
                        if masked:
                            link(tt(sc[:, nkeys - P:nkeys], sc[:, nkeys - P:nkeys], amask, ALU.add))
                        a = amx[0:rows, n % 2:n % 2 + 1]
                        link(dve.tensor_reduce(a, sc, AX, ALU.max))
                        ts(a, a, -scale).then_inc(sem("att_mx"), 1)
                    if 1 <= n <= len(units):
                        rows, terms, nkeys, masked, vs, out = units[n - 1]
                        u = (n - 1) % 2
                        dve.wait_ge(sem("att_ex"), ATT[tag] + n)
                        link(dve.reciprocal(arec[0:rows, u:u + 1], asum[0:rows, u:u + 1]))
                        p = prob[0:rows, u, 0:nkeys]
                        ts(p, p, arec[0:rows, u:u + 1]).then_inc(sem("att_nm"), 1)
                    if n >= 3:
                        rows, terms, nkeys, masked, vs, out = units[n - 3]
                        dve.wait_ge(sem("att_pv"), ATT[tag] + n - 2)
                        dve.tensor_copy(out, PS[4 + (n - 3) % 2][:, 0:rows]).then_inc(sem("att_o"), 1)

            attention("mla", mla_units, QK ** -0.5)

            dve.memset(x3[DEC:P, 2, :], 0.0).then_inc(sem("xpad"), 1)

            def add_rows(tag, banks):
                for n in range(2 * TB):
                    b, half = n // 2, n % 2
                    rows = P if b < 2 else DEC
                    dve.wait_ge(sem("res_mm"), RES[tag][0] + n + 1)
                    xx = x3[0:rows, b, 512 * half:512 * half + 512]
                    tt(xx, xx, PS[banks[n % len(banks)]][0:rows, :], ALU.add).then_inc(sem("res_add"), 1)

            def scale_rows(tag, col):
                for b in range(TB):
                    dve.wait_ge(sem("res_sq"), RES[tag][1] + b + 1)
                rstd(ssq[:, col:col + 3], ssq[:, col:col + 3], D)
                for b in range(TB):
                    ts(xs3[:, b, :], x3[:, b, :], ssq[:, col + b:col + b + 1]).then_inc(sem("res_scaled"), 1)

            dve.wait_ge(sem("ld_x2"), 32)
            add_rows("x2", (0, 1, 2, 3))

            scale_rows("x2", 5)
            for b in range(TB):
                rows = P if b < 2 else DEC
                dve.wait_ge(sem("qm_ev"), b + 1)
                scale_heads(qmraw[0:rows, :].rearrange("p (h n) -> p h n", h=H), rows, HD).then_inc(sem("qm_ready"), 1)
                dve.wait_ge(sem("qm_ready"), b + 1)
            attention("mem", mem_units, HD ** -0.5)
            dve.wait_ge(sem("ld_bias"), 64)
            link(dve.tensor_copy(bhi, braw))
            link(tt(braw, braw, bhi, ALU.subtract))
            link(dve.tensor_copy(bmid, braw))
            link(tt(braw, braw, bmid, ALU.subtract))
            dve.tensor_copy(b3[0:32, :], bhi[0:32, :])
            dve.tensor_copy(b3[32:64, :], bmid[32:64, :])
            dve.tensor_copy(b3[64:96, :], braw[64:96, :]).then_inc(mark("b3_ready"), 1)
            add_rows("x3", (0, 1, 2, 3))

            scale_rows("x3", 8)
            for b in range(TB):
                dve.wait_ge(sem("res_scaled"), RES["x3"][1] + b + 1)
                dve.tensor_copy(xparts[:, b, 0, :], xs3[:, b, :]).then_inc(sem("part_step"), 1)
            for b in range(TB):
                dve.wait_ge(sem("part_step"), b + 1)
                tt(x_rest[:, b, :], xs3[:, b, :], xparts[:, b, 0, :], ALU.subtract).then_inc(sem("part_step"), 1)
            for b in range(TB):
                dve.wait_ge(sem("part_step"), TB + b + 1)
                dve.tensor_copy(xparts[:, b, 1, :], x_rest[:, b, :]).then_inc(sem("part_step"), 1)
            for b in range(TB):
                dve.wait_ge(sem("part_step"), 2 * TB + b + 1)
                tt(xparts[:, b, 2, :], x_rest[:, b, :], xparts[:, b, 1, :], ALU.subtract).then_inc(sem("parts_ready"), 1)
            dve.memset(gate, 0.0)
            dve.memset(mask, 0.0)
            dve.memset(rpos, -1.0)
            dve.memset(KV[0:96, 908:925], 0.0)
            dve.memset(lg[:, :, E:E + 4], BIG)
            dve.memset(rep8[:, :, 4:8], BIG)
            dve.memset(bd, 0.0)
            dve.tensor_copy(identb, ident)
            link(dve.memset(xlist, 0))
            dve.tensor_copy(id3[:, 0:E], CO[0:96, C_E3:C_E3 + E])
            dve.wait_ge(*at("lg_mm"))
            for b in range(TB):
                rows = P if b < 2 else DEC
                link(tt(lg[0:rows, b, 0:E], PS[0][0:rows, b * E:(b + 1) * E], g_router[0:rows, :], ALU.add))
                link(dve.max(top8[0:rows, b, :], lg[0:rows, b, 0:E]))
                dve.tensor_copy(rep8[0:rows, b, 0:TOPK], top8[0:rows, b, 0:TOPK])
                m = ts(ntop[0:rows, b:b + 1], top8[0:rows, b, 0:1], -1.0)
                link(m)
                link(dve.match_replace(mrep[0:rows, b, :], rep8[0:rows, b, :], lg[0:rows, b, :], NEG))
                link(tt(mask[0:rows, b, :], mrep[0:rows, b, 0:E], lg[0:rows, b, 0:E], ALU.not_equal))
            dve.memset(KV[:, 1206:1207], 0.0).then_inc(mark("mask_ready"), 1)
            dve.memset(KV[:, 1207:1208], 0.0).then_inc(mark("top_ready"), 1)
            dve.wait_ge(*at("rank_mm"))
            r = rpos[:, :, 0:E]
            link(dve.scalar_tensor_tensor(r, PS[1][:, 0:96].rearrange("p (b e) -> p b e", b=TB), 1.0, mask,
                                          ALU.add, ALU.mult))
            link(ts(r, r, 1.0, None, ALU.subtract))
            dve.wait_ge(*at("cnt_mm"))
            link(dve.tensor_copy(cnt, PS[2][0:E, 0:1]))
            link(ts(flags, CO[0:E, C_TH:C_TH + XTRA], cnt, None, ALU.is_lt))
            dve.tensor_reduce(tot, flags, AX, ALU.add).then_inc(mark("tot_ready"), 1)
            def gates():
                dve.wait_ge(sem("gate_exp"), TB)
                link(tt(gate, gate, mask, ALU.mult))
                for b in range(TB):
                    rows = P if b < 2 else DEC
                    link(dve.tensor_reduce(gsum[0:rows, b:b + 1], gate[0:rows, b, :], AX, ALU.add))
                    link(dve.reciprocal(gsum[0:rows, b:b + 1], gsum[0:rows, b:b + 1]))
                    link(ts(gate[0:rows, b, :], gate[0:rows, b, :], gsum[0:rows, b:b + 1]))
                dve.memset(KV[:, 1208:1209], 0.0).then_inc(mark("gate_ready"), 1)

            def bias_rows():
                for n in range(2 * TB):
                    b, half = n // 2, n % 2
                    rows = P if b < 2 else DEC
                    dve.wait_ge(sem("y0_mm"), n + 1)
                    xx = x3[0:rows, b, 512 * half:512 * half + 512]
                    tt(xx, xx, PS[4 + n % 4][0:rows, :], ALU.add).then_inc(sem("y0_add"), 1)

            def extra_list():
                dve.wait_ge(*at("start_mm"))
                link(dve.tensor_copy(start, PS[2][0:E, 8:9]))
                link(ts(pos4, CO[0:E, C_EV + 1:C_EV + 1 + XTRA], start, -1.0, ALU.add, ALU.add))
                sh = [E, XTRA, LIST]
                link(tt(hot, bcast(iota[0:E, 0:LIST], sh, 1), bcast(pos4, sh, 2), ALU.is_equal))
                tt(hot, hot, bcast(flags, sh, 2), ALU.mult).then_inc(mark("hot_ready"), 1)
                dve.wait_ge(*at("list_mm"))
                dve.tensor_copy(xlist[0:1, 0:2 * LIST + 1], PS[3][0:1, 0:2 * LIST + 1]).then_inc(mark("list_ready"), 1)

            def slots(e, first):
                sh = [P, TB, 2, SLOTS]
                rank = rpos[:, :, bass.ds(e, 1)]
                io = iota[:, 0:SLOTS] if first is None else iota[:, bass.ds(first, SLOTS)]
                tt(S, bcast(io, sh, 1, 1), bcast(rank, sh, 3), ALU.is_equal).then_inc(sem("slots_ready"), 1)

            def select(e):
                dve.tensor_copy(sel, id3[:, bass.ds(e, 1)].broadcast_to([96, SLOTS])).then_inc(sem("sel_ready"), 1)

            def rows_in(g):
                dve.wait_ge(sem("gather_mm"), g + 1)
                tt(xgT, PS[4][:, :].rearrange("p (k t) -> p k t", k=KD), bcast(c_ffn, [P, KD, SLOTS], 2), ALU.mult)\
                    .then_inc(sem("xg_ready"), 1)

            def rows_back(it, g):
                dve.wait_ge(sem("slots_tr"), g + 1)
                src = PS[5][:, 0:TB * 64].bitcast(BF16)[:, 0:T].rearrange("p (j t) -> p j t", j=NC)
                dve.tensor_copy(bd[0:64, :, 0:64], src[0:64])
                dve.tensor_copy(bd[64:128, :, 64:128], src[64:128]).then_inc(sem("bd_ready"), 1)

            def activations(it):
                dve.wait_ge(sem("gu_used"), it * KD + KD)
                ts(gt_sb, PS[0][:, :], LIMIT, None, ALU.min).then_inc(sem("gt_ready"), 1)
                ts(up_sb, PS[1][:, :], LIMIT, -LIMIT, ALU.min, ALU.max)
                dve.wait_ge(sem("sig_ready"), it + 1)
                tt(sig_sb, gt_sb, sig_sb, ALU.mult).then_inc(sem("glu_step"), 1)
                dve.wait_ge(sem("glu_step"), it + 1)
                dve.scalar_tensor_tensor(act_sb, up_sb, 1.0, sig_sb, ALU.add, ALU.mult).then_inc(sem("act_ready"), 1)

            def accumulate(it, e):
                dve.tensor_copy(gcur, gated[:, :, bass.ds(e, 1)].rearrange("p j a -> p (j a)")).then_inc(sem("gcur_ready"), 1)
                dve.wait_ge(sem("gcur_ready"), it + 1)
                for j in range(NC):
                    dve.wait_ge(sem("scat_mm"), it * NC + (j + 1))
                    dve.scalar_tensor_tensor(yacc[:, j, :], PS[6 + j % 2][:, :], gcur[:, j:j + 1], yacc[:, j, :],
                                             ALU.mult, ALU.add).then_inc(sem("acc_done"), 1)

            slots(0, None)
            select(0)
            gates()
            rows_in(0)
            rows_back(0, 0)
            slots(1, None)
            activations(0)
            bias_rows()
            extra_list()
            select(1)
            rows_in(1)
            dve.wait_ge(sem("ld_yacc"), 16 * 8)
            dve.memset(KV[:, 1209:1210], 0.0).then_inc(sem("acc_done"), 1)
            accumulate(0, 0)
            dve.wait_ge(sem("acc_done"), NC + 1)
            with dve.Fori(1, E) as it:
                rows_back(it, it)
                slots(it + 1, None)
                activations(it)
                select(it + 1)
                rows_in(it + 1)
                accumulate(it, it)
                dve.wait_ge(sem("acc_done"), it * NC + (NC + 1))
            n_extra = dve.value_load(xlist[0:1, 2 * LIST:2 * LIST + 1], min_val=0, max_val=LIST - 1)
            with dve.If(n_extra > 0):
                with dve.Fori(0, n_extra) as j:
                    e = dve.value_load(xlist[0:1, bass.ds(j, 1)], min_val=0, max_val=E - 1)
                    part = dve.value_load(xlist[0:1, bass.ds(j + LIST, 1)], min_val=1, max_val=XTRA)
                    dve.wait_ge(sem("slots_tr"), j + (E + 1))
                    slots(e, part * SLOTS)
                    dve.wait_ge(sem("bias_mm"), j + E)
                    select(e)
                    rows_in(j + (E + 1))
                    rows_back(j + E, j + (E + 1))
                    activations(j + E)
                    accumulate(j + E, e)
                    dve.wait_ge(sem("acc_done"), j * NC + (E * NC + NC + 1))
            dve.memset(KV[:, 1210:1211], 0.0).then_inc(mark("y_final"), 1)


_INS = ['x_prompt', 'x_sample', 'cache_kv_latent', 'cache_k_rope', 'state_gdn', 'state_conv', 'cache_mem_k',
        'cache_mem_v', 'mem_prompt', 'norm_mix', 'w_in', 'conv_w', 'a_log', 'dt_bias', 'gdn_norm', 'q_a_norm',
        'w_qb', 'kv_a_norm', 'w_kvb', 'q_norm', 'k_nope_norm', 'k_rope_norm', 'w_out', 'norm_mem', 'mem_norm',
        'w_mq', 'w_mk', 'w_mv', 'mq_norm', 'mk_norm', 'w_mo', 'norm_ffn', 'w_router', 'b_router', 'w_gu', 'b_gu',
        'w_down', 'b_down']
_OUTS = [(1, SEQ, D), (1, DEC, D), (1, 1, SEQ, KV_RANK), (1, 1, SEQ, ROPE), (1, 1, H, HD, HD), (1, 1, 3, CONV_DIM),
         (1, 1, NMEM, H, HD), (1, 1, NMEM, H, HD), (1, 1, DEC, KV_RANK), (1, 1, DEC, ROPE), (1, 1, H, HD, HD),
         (1, 1, 3, CONV_DIM)]


def kernel(**inputs):
    import concourse.bacc as bacc
    from concourse.bass_utils import run_bass_kernel_spmd

    nc = bacc.Bacc("TRN2", target_bir_lowering=False, num_devices=1)
    arrays, args = {}, []
    for name in _INS:
        a = np.ascontiguousarray(inputs[name])
        arrays[f"in_{name}"] = a
        args.append(nc.dram_tensor(f"in_{name}", a.shape, F32, kind="ExternalInput").ap())
    arrays["in_consts"] = constants()
    args.append(nc.dram_tensor("in_consts", (P, C_N), F32, kind="ExternalInput").ap())
    for i, shape in enumerate(_OUTS):
        args.append(nc.dram_tensor(f"out_{i}", shape, F32, kind="ExternalOutput").ap())
    trunk_kernel(nc, *args)
    r = run_bass_kernel_spmd(nc, [arrays], core_ids=[0])
    return tuple(r.results[0][f"out_{i}"] for i in range(len(_OUTS)))
```
